# Optimizing a Trainium2 kernel written in Bass

```python
import math
import jax, jax.numpy as jnp
from jax import lax
import numpy as np

D_MODEL = 1024
BATCH = 1
SEQ = 512
DEPTH = 1
DEC_BATCH = 8
DEC_SEQ = 16
PAST_LEN = 512

CHUNK = 64
N_PREV_CHUNKS = 8
BAND = (N_PREV_CHUNKS + 1) * CHUNK
SSM_WIDTH = D_MODEL // 2
SSM_GROUP = 16
SSM_GROUPS = SSM_WIDTH // SSM_GROUP
SSM_STATE = 64
ATT_WIDTH = D_MODEL - SSM_WIDTH
ATT_HEAD_DIM = 64
ATT_HEADS = ATT_WIDTH // ATT_HEAD_DIM
REL_CLIP = 128
N_MEM = 256
MEM_HEADS = 4
MEM_HEAD_DIM = D_MODEL // MEM_HEADS
N_GROUPS = 4
EXPERTS_PER_GROUP = 8
N_EXPERTS = N_GROUPS * EXPERTS_PER_GROUP
TOP_K = 2
D_FF_EXPERT = D_MODEL // 4
EPS = 1e-6
F32 = jnp.float32
NEG_INF = -1e30

kernel_name = 'hymba_s5_chunkband_hmoe_stream_step'

def rms_norm(x, gain):
    xf = x.astype(F32)
    y = xf * lax.rsqrt(jnp.mean(xf * xf, axis=-1, keepdims=True) + EPS)
    return (y * gain.astype(F32)).astype(x.dtype)

def rel_bias_lookup(rel_bias, dist):
    idx = jnp.clip(dist, -REL_CLIP, REL_CLIP) + REL_CLIP
    return rel_bias.astype(F32)[:, idx]

def ssm_discretise(lam_re, lam_im, log_step, b_re, b_im):
    lam = lax.complex(lam_re.astype(F32), lam_im.astype(F32))
    step = jnp.exp(log_step.astype(F32))[:, None]
    lam_bar = jnp.exp(lam * step)
    b = lax.complex(b_re.astype(F32), b_im.astype(F32))
    b_bar = ((lam_bar - 1.0) / lam)[..., None] * b
    return lam_bar, b_bar

def ssm_scan(u, lam_bar, b_bar, c, d_skip, s0):
    bsz, t = u.shape[:2]
    ug = u.astype(F32).reshape(bsz, t, SSM_GROUPS, SSM_GROUP)
    bu = jnp.einsum('gpc,btgc->btgp', b_bar, ug.astype(jnp.complex64))
    if s0 is not None:
        bu = bu.at[:, 0].add(lam_bar * s0)
    a = jnp.broadcast_to(lam_bar, bu.shape)

    def combine(e1, e2):
        return e1[0] * e2[0], e2[0] * e1[1] + e2[1]

    _, states = lax.associative_scan(combine, (a, bu), axis=1)
    y = jnp.einsum('gcp,btgp->btgc', c, states).real
    y = y + d_skip.astype(F32).reshape(SSM_GROUPS, SSM_GROUP) * ug
    return y.reshape(bsz, t, SSM_WIDTH).astype(u.dtype), states[:, -1]

def parallel_mixer_inputs(x, norm_mix, w_in, att_q_gain, att_k_gain):
    bsz, t = x.shape[:2]
    h = rms_norm(x, norm_mix)
    z = jnp.einsum('btd,de->bte', h, w_in)
    u = z[..., :SSM_WIDTH]
    q, k, v = jnp.split(z[..., SSM_WIDTH:], 3, axis=-1)
    shape = (bsz, t, ATT_HEADS, ATT_HEAD_DIM)
    q = rms_norm(q.reshape(shape), att_q_gain)
    k = rms_norm(k.reshape(shape), att_k_gain)
    return u, q, k, v.reshape(shape)

def parallel_mixer_output(y_ssm, y_att, w_glu, out_norm_ssm, out_norm_att, w_out):
    bsz, t = y_ssm.shape[:2]
    g = jnp.einsum('btc,ce->bte', jax.nn.gelu(y_ssm), w_glu)
    val, gate = jnp.split(g, 2, axis=-1)
    y_s = val * jax.nn.sigmoid(gate)
    cat = jnp.concatenate([rms_norm(y_s, out_norm_ssm),
                           rms_norm(y_att.reshape(bsz, t, ATT_WIDTH), out_norm_att)], axis=-1)
    return jnp.einsum('btc,cd->btd', cat, w_out)

def band_attention_prompt(q, k, v, rel_bias):
    bsz, t = q.shape[:2]
    n_chunks = t // CHUNK
    pad = N_PREV_CHUNKS * CHUNK
    kp = jnp.pad(k, ((0, 0), (pad, 0), (0, 0), (0, 0)))
    vp = jnp.pad(v, ((0, 0), (pad, 0), (0, 0), (0, 0)))
    dist = pad + jnp.arange(CHUNK)[:, None] - jnp.arange(BAND)[None, :]
    bias = rel_bias_lookup(rel_bias, dist)
    scale = ATT_HEAD_DIM ** -0.5

    def one_chunk(args):
        c, qc = args
        kb = lax.dynamic_slice_in_dim(kp, c * CHUNK, BAND, axis=1)
        vb = lax.dynamic_slice_in_dim(vp, c * CHUNK, BAND, axis=1)
        s = jnp.einsum('bqhd,bkhd->bhqk', qc, kb).astype(F32) * scale + bias
        key_pos = (c - N_PREV_CHUNKS) * CHUNK + jnp.arange(BAND)
        s = jnp.where((key_pos >= 0)[None, None, None, :], s, NEG_INF)
        p = jax.nn.softmax(s, axis=-1).astype(vb.dtype)
        return jnp.einsum('bhqk,bkhd->bqhd', p, vb)

    qc_all = q.reshape(bsz, n_chunks, CHUNK, ATT_HEADS, ATT_HEAD_DIM).transpose(1, 0, 2, 3, 4)
    out = lax.map(one_chunk, (jnp.arange(n_chunks), qc_all))
    return out.transpose(1, 0, 2, 3, 4).reshape(bsz, t, ATT_HEADS, ATT_HEAD_DIM)

def band_attention_sample(q, k, v, cache_k, cache_v, rel_bias):
    w = cache_k.shape[1]
    s_len = q.shape[1]
    kk = jnp.concatenate([cache_k.astype(k.dtype), k], axis=1)
    vv = jnp.concatenate([cache_v.astype(v.dtype), v], axis=1)
    dist = (w + jnp.arange(s_len))[:, None] - jnp.arange(w + s_len)[None, :]
    bias = rel_bias_lookup(rel_bias, dist)
    s = jnp.einsum('bqhd,bkhd->bhqk', q, kk).astype(F32) * ATT_HEAD_DIM ** -0.5 + bias
    p = jax.nn.softmax(s, axis=-1).astype(vv.dtype)
    return jnp.einsum('bhqk,bkhd->bqhd', p, vv)

def memory_kv(mem, mem_in_norm, w_mem_k, w_mem_v, mem_k_gain):
    bsz, n = mem.shape[:2]
    m = rms_norm(mem, mem_in_norm)
    shape = (bsz, n, MEM_HEADS, MEM_HEAD_DIM)
    k = rms_norm(jnp.einsum('bnd,de->bne', m, w_mem_k).reshape(shape), mem_k_gain)
    v = jnp.einsum('bnd,de->bne', m, w_mem_v).reshape(shape)
    return k, v

def memory_attend(x, mem_k, mem_v, norm_mem, w_mem_q, mem_q_gain, w_mem_o):
    bsz, t = x.shape[:2]
    h = rms_norm(x, norm_mem)
    q = rms_norm(jnp.einsum('btd,de->bte', h, w_mem_q).reshape(bsz, t, MEM_HEADS, MEM_HEAD_DIM), mem_q_gain)
    s = jnp.einsum('bqhd,bkhd->bhqk', q, mem_k.astype(q.dtype)).astype(F32) * MEM_HEAD_DIM ** -0.5
    p = jax.nn.softmax(s, axis=-1).astype(q.dtype)
    o = jnp.einsum('bhqk,bkhd->bqhd', p, mem_v.astype(q.dtype)).reshape(bsz, t, D_MODEL)
    return jnp.einsum('btd,de->bte', o, w_mem_o)

def hier_moe(x, router_g_w, router_g_b, router_e_w, router_e_b, exp_w_gate, exp_w_up, exp_w_down):
    shp = x.shape
    xt = x.reshape(-1, D_MODEL)
    n_tok = xt.shape[0]
    lg = jnp.einsum('td,dg->tg', xt, router_g_w).astype(F32) + router_g_b.astype(F32)
    pg = jax.nn.softmax(lg, axis=-1)
    _, g_top = lax.top_k(lg, 1)
    g_idx = g_top[:, 0]
    tok = jnp.arange(n_tok)
    p1 = pg[tok, g_idx]
    le = jnp.einsum('td,gde->tge', xt, router_e_w).astype(F32) + router_e_b.astype(F32)
    le_sel = le[tok, g_idx]
    top_v, top_i = lax.top_k(le_sel, TOP_K)
    w_sel = p1[:, None] * jax.nn.softmax(top_v, axis=-1)
    expert_id = g_idx[:, None] * EXPERTS_PER_GROUP + top_i
    gates = jnp.sum(jax.nn.one_hot(expert_id, N_EXPERTS, dtype=F32) * w_sel[..., None], axis=1)

    def body(acc, e):
        wg, wu, wd, ge = e
        h = jax.nn.silu(xt @ wg) * (xt @ wu)
        return acc + ge[:, None] * (h @ wd).astype(F32), None

    acc, _ = lax.scan(body, jnp.zeros(xt.shape, F32), (exp_w_gate, exp_w_up, exp_w_down, gates.T))
    return acc.astype(x.dtype).reshape(shp)

def setup_inputs(seed: int = 0) -> dict:
    key = jax.random.key(seed)
    ks = iter(jax.random.split(key, 64))
    nrm = lambda shape, scale=1.0: scale * jax.random.normal(next(ks), shape, F32)
    gain = lambda shape: 1.0 + 0.02 * jax.random.normal(next(ks), shape, F32)
    att_rows = min(N_PREV_CHUNKS * CHUNK, PAST_LEN)
    n_idx = jnp.arange(SSM_STATE, dtype=F32)
    d_in = D_MODEL ** -0.5
    return {
        'x_prompt': nrm((BATCH, SEQ, D_MODEL)),
        'x_sample': nrm((DEC_BATCH, DEC_SEQ, D_MODEL)),
        'mem_prompt': nrm((BATCH, N_MEM, D_MODEL)),
        'cache_attn_k': nrm((DEPTH, DEC_BATCH, att_rows, ATT_HEADS, ATT_HEAD_DIM)),
        'cache_attn_v': nrm((DEPTH, DEC_BATCH, att_rows, ATT_HEADS, ATT_HEAD_DIM)),
        'state_ssm_re': nrm((DEPTH, DEC_BATCH, SSM_GROUPS, SSM_STATE), 0.5),
        'state_ssm_im': nrm((DEPTH, DEC_BATCH, SSM_GROUPS, SSM_STATE), 0.5),
        'cache_mem_k': nrm((DEPTH, DEC_BATCH, N_MEM, MEM_HEADS, MEM_HEAD_DIM)),
        'cache_mem_v': nrm((DEPTH, DEC_BATCH, N_MEM, MEM_HEADS, MEM_HEAD_DIM)),
        'norm_mix': gain((DEPTH, D_MODEL)),
        'w_in': nrm((DEPTH, D_MODEL, SSM_WIDTH + 3 * ATT_WIDTH), d_in),
        'ssm_lambda_re': -0.5 + nrm((DEPTH, SSM_GROUPS, SSM_STATE), 0.01),
        'ssm_lambda_im': math.pi * n_idx + nrm((DEPTH, SSM_GROUPS, SSM_STATE), 0.01),
        'ssm_log_step': jax.random.uniform(next(ks), (DEPTH, SSM_GROUPS), F32, math.log(1e-3), math.log(1e-1)),
        'ssm_b_re': nrm((DEPTH, SSM_GROUPS, SSM_STATE, SSM_GROUP), (2 * SSM_GROUP) ** -0.5),
        'ssm_b_im': nrm((DEPTH, SSM_GROUPS, SSM_STATE, SSM_GROUP), (2 * SSM_GROUP) ** -0.5),
        'ssm_c_re': nrm((DEPTH, SSM_GROUPS, SSM_GROUP, SSM_STATE), SSM_STATE ** -0.5),
        'ssm_c_im': nrm((DEPTH, SSM_GROUPS, SSM_GROUP, SSM_STATE), SSM_STATE ** -0.5),
        'ssm_d': nrm((DEPTH, SSM_WIDTH)),
        'w_glu': nrm((DEPTH, SSM_WIDTH, 2 * SSM_WIDTH), SSM_WIDTH ** -0.5),
        'att_q_gain': gain((DEPTH, ATT_HEAD_DIM)),
        'att_k_gain': gain((DEPTH, ATT_HEAD_DIM)),
        'att_rel_bias': nrm((DEPTH, ATT_HEADS, 2 * REL_CLIP + 1), 0.1),
        'out_norm_ssm': gain((DEPTH, SSM_WIDTH)),
        'out_norm_att': gain((DEPTH, ATT_WIDTH)),
        'w_out': nrm((DEPTH, SSM_WIDTH + ATT_WIDTH, D_MODEL), (SSM_WIDTH + ATT_WIDTH) ** -0.5),
        'norm_mem': gain((DEPTH, D_MODEL)),
        'mem_in_norm': gain((DEPTH, D_MODEL)),
        'w_mem_q': nrm((DEPTH, D_MODEL, D_MODEL), d_in),
        'w_mem_k': nrm((DEPTH, D_MODEL, D_MODEL), d_in),
        'w_mem_v': nrm((DEPTH, D_MODEL, D_MODEL), d_in),
        'w_mem_o': nrm((DEPTH, D_MODEL, D_MODEL), d_in),
        'mem_q_gain': gain((DEPTH, MEM_HEAD_DIM)),
        'mem_k_gain': gain((DEPTH, MEM_HEAD_DIM)),
        'norm_ffn': gain((DEPTH, D_MODEL)),
        'router_g_w': nrm((DEPTH, D_MODEL, N_GROUPS), d_in),
        'router_g_b': nrm((DEPTH, N_GROUPS), 0.01),
        'router_e_w': nrm((DEPTH, N_GROUPS, D_MODEL, EXPERTS_PER_GROUP), d_in),
        'router_e_b': nrm((DEPTH, N_GROUPS, EXPERTS_PER_GROUP), 0.01),
        'exp_w_gate': nrm((DEPTH, N_EXPERTS, D_MODEL, D_FF_EXPERT), d_in),
        'exp_w_up': nrm((DEPTH, N_EXPERTS, D_MODEL, D_FF_EXPERT), d_in),
        'exp_w_down': nrm((DEPTH, N_EXPERTS, D_FF_EXPERT, D_MODEL), D_FF_EXPERT ** -0.5),
    }

def reference(x_prompt, x_sample, mem_prompt, cache_attn_k, cache_attn_v, state_ssm_re, state_ssm_im,
              cache_mem_k, cache_mem_v, norm_mix, w_in, ssm_lambda_re, ssm_lambda_im, ssm_log_step,
              ssm_b_re, ssm_b_im, ssm_c_re, ssm_c_im, ssm_d, w_glu, att_q_gain, att_k_gain, att_rel_bias,
              out_norm_ssm, out_norm_att, w_out, norm_mem, mem_in_norm, w_mem_q, w_mem_k, w_mem_v, w_mem_o,
              mem_q_gain, mem_k_gain, norm_ffn, router_g_w, router_g_b, router_e_w, router_e_b,
              exp_w_gate, exp_w_up, exp_w_down):
    yp, ys = x_prompt, x_sample
    sdt = state_ssm_re.dtype
    p_k, p_v, p_re, p_im, p_mk, p_mv = [], [], [], [], [], []
    s_k, s_v, s_re, s_im = [], [], [], []
    for l in range(DEPTH):
        lam_bar, b_bar = ssm_discretise(ssm_lambda_re[l], ssm_lambda_im[l], ssm_log_step[l], ssm_b_re[l], ssm_b_im[l])
        c_mat = lax.complex(ssm_c_re[l].astype(F32), ssm_c_im[l].astype(F32))
        moe_args = (router_g_w[l], router_g_b[l], router_e_w[l], router_e_b[l], exp_w_gate[l], exp_w_up[l], exp_w_down[l])

        u, q, k, v = parallel_mixer_inputs(yp, norm_mix[l], w_in[l], att_q_gain[l], att_k_gain[l])
        y_ssm, s_fin = ssm_scan(u, lam_bar, b_bar, c_mat, ssm_d[l], None)
        y_att = band_attention_prompt(q, k, v, att_rel_bias[l])
        yp = yp + parallel_mixer_output(y_ssm, y_att, w_glu[l], out_norm_ssm[l], out_norm_att[l], w_out[l])
        mk, mv = memory_kv(mem_prompt, mem_in_norm[l], w_mem_k[l], w_mem_v[l], mem_k_gain[l])
        yp = yp + memory_attend(yp, mk, mv, norm_mem[l], w_mem_q[l], mem_q_gain[l], w_mem_o[l])
        yp = yp + hier_moe(rms_norm(yp, norm_ffn[l]), *moe_args)
        keep = min(N_PREV_CHUNKS * CHUNK, k.shape[1])
        p_k.append(k[:, -keep:])
        p_v.append(v[:, -keep:])
        p_re.append(s_fin.real.astype(sdt))
        p_im.append(s_fin.imag.astype(sdt))
        p_mk.append(mk)
        p_mv.append(mv)

        u, q, k, v = parallel_mixer_inputs(ys, norm_mix[l], w_in[l], att_q_gain[l], att_k_gain[l])
        s0 = lax.complex(state_ssm_re[l].astype(F32), state_ssm_im[l].astype(F32))
        y_ssm, s_new = ssm_scan(u, lam_bar, b_bar, c_mat, ssm_d[l], s0)
        y_att = band_attention_sample(q, k, v, cache_attn_k[l], cache_attn_v[l], att_rel_bias[l])
        ys = ys + parallel_mixer_output(y_ssm, y_att, w_glu[l], out_norm_ssm[l], out_norm_att[l], w_out[l])
        ys = ys + memory_attend(ys, cache_mem_k[l], cache_mem_v[l], norm_mem[l], w_mem_q[l], mem_q_gain[l], w_mem_o[l])
        ys = ys + hier_moe(rms_norm(ys, norm_ffn[l]), *moe_args)
        s_k.append(k)
        s_v.append(v)
        s_re.append(s_new.real.astype(sdt))
        s_im.append(s_new.imag.astype(sdt))

    return (yp, ys,
            jnp.stack(p_k), jnp.stack(p_v), jnp.stack(p_re), jnp.stack(p_im), jnp.stack(p_mk), jnp.stack(p_mv),
            jnp.stack(s_k), jnp.stack(s_v), jnp.stack(s_re), jnp.stack(s_im))


_drawn_inputs = setup_inputs


def setup_inputs(seed=0):
    import zlib

    import numpy as np

    out = dict(_drawn_inputs(seed))
    spreads = {}
    factors = {'ssm_lambda_re': 17.083,
     'att_q_gain': 2.706,
     'att_k_gain': 3.502,
     'out_norm_ssm': 3.328,
     'out_norm_att': 3.491,
     'norm_mem': 7.531,
     'mem_in_norm': 3.112,
     'mem_q_gain': 6.964,
     'mem_k_gain': 2.909,
     'router_g_b': 21.723,
     'router_e_b': 20.469,
     'norm_ffn': 7.936}
    for name, (base, spread) in spreads.items():
        noise = np.random.default_rng([zlib.crc32(name.encode()), seed]).standard_normal(out[name].shape)
        drawn = base * np.exp(spread * noise) if base else spread * noise
        out[name] = __import__('jax').numpy.asarray(drawn.astype(out[name].dtype))
    for name, factor in factors.items():
        out[name] = (out[name] * factor).astype(out[name].dtype)
    return out
```

```python
from contextlib import ExitStack

import numpy as np

import concourse.bass as bass
from concourse import mybir

F32 = mybir.dt.float32
U32 = mybir.dt.uint32
I32 = mybir.dt.int32
ALU = mybir.AluOpType
ACT = mybir.ActivationFunctionType
AXX = mybir.AxisListType.X

P = 128
D = 1024
KT = D // P
TP, TS = 512, 128
NT = (TP + TS) // P
T = NT * P
NB, SQ = 8, 16
HD, NH = 64, 8
AW = NH * HD
NPAIR = NH // 2
CH = 64
REL = 128
G, GC, GS = 32, 16, 64
GP = G // 2
L = 8
NCH = T // L
PCH = TP // L
HALVES = 2
HP = GP // HALVES
NM, MH, MD = 256, 4, 256
NG, EPG = 4, 8
NE = NG * EPG
FF = 256
EPS = 1e-6
NEG = -1e30
CAP = 104
NBLK = -(-T // CAP)
NOV = (2 * T) // CAP - 1
NU = NE + NOV
TWO_PI_HI = 6.28125
TWO_PI_LO = 0.0019353071795864769
GELU_C = 0.7978845608028654
ROUND = 12582912.0

PROMPT_UNITS = [(t, h) for t in range(NT - 1) for h in range(NH)]
MEM_UNITS = [(t, h) for t in range(NT - 1) for h in range(MH)]


FILL = [[[], [("v", 3), ("v", 4), ("mk", 0), ("mk", 1)], []],
        [[("mk", 2), ("mk", 3)], [("mv", 0), ("mv", 1), ("mv", 2)], [("mv", 3)]]]


def pe_order():
    o = [("u", t) for t in range(NT)]
    for i in range(10):
        o.append(("qk", i))
        if i >= 2:
            o.append(("qkT", i - 2))
    o += [("v", 0), ("qkT", 8), ("v", 1), ("qkT", 9), ("v", 2)]
    o += [("UT", i) for i in range(8)]
    for hf in range(HALVES):
        o += [("G", 4 * hf + i) for i in range(4)]
        o += FILL[hf][0]
        o += [("K", 4 * hf + i) for i in range(4)]
        o += [("V", 4 * hf + i) for i in range(4)]
        o += FILL[hf][1]
        o += [("Y", 4 * hf + i) for i in range(4)]
        o += [("YT", 4 * hf + i) for i in range(4)]
        o += FILL[hf][2]
    for c in range(4):
        o += [("gg", c), ("gv", c)]
    o += [("gs", c) for c in range(4)]
    n = len(PROMPT_UNITS)
    for i in range(n + 4):
        if i < n:
            o.append(("S", i))
        if 0 <= i - 2 < n:
            o.append(("PT", i - 2))
        if i >= 4 and (i - 4) % 2 == 1 and i - 4 < n:
            o.append(("PV", (i - 4) // 2))
    for b in range(NB + 3):
        if b < NB:
            o += [("sA", b), ("sB", b)]
        if 0 <= b - 1 < NB:
            o += [("sPa", b - 1), ("sPb", b - 1)]
        if 0 <= b - 2 < NB:
            o.append(("sPV", b - 2))
        if 0 <= b - 3 < NB:
            o.append(("sO", b - 3))
    o += [("mkT", i) for i in range(4)]
    o.append(("ss", 0))
    for t in range(NT + 1):
        if t < NT:
            for c in range(2):
                o += [("oS", 2 * t + c), ("oA", 2 * t + c)]
        if t >= 1:
            o += [("x1T", 2 * t - 2), ("x1T", 2 * t - 1)]
    for i in range(12):
        if i < 10:
            o.append(("mq", i))
        if i >= 2:
            o.append(("mqT", i - 2))
    n = len(MEM_UNITS)
    for i in range(n + 3):
        if i < n:
            o.append(("mS", i))
        if 0 <= i - 2 < n:
            o.append(("mPT", i - 2))
        if 0 <= i - 3 < n:
            o.append(("mPV", i - 3))
    for i in range(7):
        if i < 4:
            o.append(("mS", n + i))
        if 0 <= i - 1 < 4:
            o.append(("mPT", n + i - 1))
        if 0 <= i - 2 < 4:
            o += [("smPV", 2 * (i - 2)), ("smPV", 2 * (i - 2) + 1)]
        if 0 <= i - 3 < 4:
            o += [("smT", 2 * (i - 3)), ("smT", 2 * (i - 3) + 1)]
    for t in range(NT + 1):
        if t < NT:
            o += [("mo", 2 * t), ("mo", 2 * t + 1)]
        if t >= 1:
            o += [("x2T", 2 * t - 2), ("x2T", 2 * t - 1)]
    o += [("rt", t) for t in range(NT)]
    o += [("rank", 0), ("tab", 0)]
    return o


ORDER = pe_order()
NUMBER = {key: n for n, key in enumerate(ORDER)}
KINDS = sorted({k for k, _ in ORDER})

W_SLOT = {0: 0, 1: 1, 2: 2, 3: 0, 5: 2, 6: 0, 7: 2, 8: 0, 4: 2, 9: 1, 10: 0, 11: 2, 12: 1, 13: 0, 14: 2}
W_LOADS = list(W_SLOT)
W_AFTER = {3: ("u", 4), 5: None, 6: ("v", 4), 7: ("mk", 1), 8: ("mk", 3), 4: ("mv", 1), 9: ("mv", 3), 10: ("mv", 3),
           11: ("gs", 3), 12: ("oA", 8), 13: ("oA", 9), 14: ("mq", 8)}


def w_count(u):
    before = W_LOADS[:W_LOADS.index(u) + 1]
    return sum(W_SLOT[i] == W_SLOT[u] for i in before)


HT = 12288
QT = HT + KT * T
KTO = QT + NPAIR * T
VR = KTO + NPAIR * T
CONST = VR + NT * AW
R = CONST + 2560
WORDS = R + 25472


def program(nc, x_t, x_rows, mem_t, mem_rows, dense_w, exp_gu, exp_dn, ck_t, cv, cmk_t, cmv, cols, k_gain, mk_gain,
            router_w, router_b, ssm_small, ssm_bc, ssm_d, ssm_s0, rel_rev,
            y_out, k_out, v_out, mk_out, mv_out, s_out):
    ctx = ExitStack()
    with ctx:
        arena = ctx.enter_context(nc.sbuf_tensor("arena", [P, WORDS], F32))
        banks = ctx.enter_context(nc.psum_tensor("banks", [P, 8, 512], F32))
        slot_idx = ctx.enter_context(nc.sbuf_tensor("slot_idx", [P, 2 * NT], U32))
        tok_idx = ctx.enter_context(nc.sbuf_tensor("tok_idx", [P, NU], U32))
        ov_regs = ctx.enter_context(nc.sbuf_tensor("ov_regs", [P, NOV + 1], I32))
        u_dram = nc.dram_tensor("u_scratch", [T, 512], F32)
        e_dram = nc.dram_tensor("bias_scratch", [NH, P, 385], F32)
        mk_dram = nc.dram_tensor("memory_key_scratch", [NM, D], F32)
        xn_dram = nc.dram_tensor("xn_scratch", [T, D], F32)
        moe_dram = nc.dram_tensor("moe_scratch", [NU * CAP, D], F32)

        def at(off, *dims, p0=0, p1=P):
            n = int(np.prod(dims))
            v = arena[p0:p1, off:off + n]
            if len(dims) == 1:
                return v
            names = "abcd"[:len(dims)]
            s = " ".join(names)
            return v.rearrange(f"p ({s}) -> p {s}", **{k: d for k, d in zip(names, dims)})

        def sem(name):
            return ctx.enter_context(nc.semaphore(name))

        def spread(ap, shape):
            return ap.to_broadcast(shape)

        W = [at(4096 * s, 4096) for s in range(3)]

        def wdense(u):
            return W[W_SLOT[u]]

        hT = at(HT, KT, T)
        qT = at(QT, NPAIR, T)
        kT = at(KTO, NPAIR, T)
        v_rows = at(VR, NT, AW)
        pos = [CONST]

        def const(*dims):
            off = pos[0]
            pos[0] += int(np.prod(dims))
            assert pos[0] <= R
            return at(off, *dims)

        ident = const(P)
        tri = const(P)
        ones = const(P)
        colc = const(56)
        norm_mix, norm_mem, mem_in_norm, norm_ffn = (colc[:, 8 * i:8 * i + 8] for i in range(4))
        out_ssm, out_att = colc[:, 32:36], colc[:, 36:40]
        q_gain, mq_gain = colc[:, 40:41], colc[:, 41:43]
        bias_far = colc[:, 43:44]
        mq_gain4 = colc[:, 44:48]
        minus_half = const(48)
        kg = const(HD)
        mkg = const(MD)
        rw = const(KT, NG + NE)
        rb = const(NG + NE)
        bias_s = const(144)
        bias_new = const(240)
        ssx, rstd_x = const(NT), const(NT)
        ssm_, rstd_m = const(2), const(2)
        ss1, rstd_1 = const(NT), const(NT)
        ss2, rstd_2 = const(NT), const(NT)
        ssg, rstd_g = const(2 * NT), const(2 * NT)
        iota_slot = const(max(CAP, NU))
        iota32, iota4 = iota_slot[:, 0:NE], iota_slot[:, 0:NG]
        qss, qf = const(4, NH), const(4, NH)
        smax, ssum = const(4, 4), const(4, 4)
        rel_ext = const(385)
        tokid = const(NT)
        tmp48 = const(48)
        qss8, qf8 = const(8), const(8)
        d_tmp = const(64)

        yT = at(R, 4, T)
        Uc = at(8192, L, 512, p1=NCH)
        U = at(R + 2560, G, L * GC, p1=NCH)
        Yh = at(R + 2560, L, 256, p1=NCH)
        Gm = at(R + 4608, HP, 2, P)
        UT = at(R + 6656, G, NCH)
        BL = [at(R + 9216 + 1024 * i, HP, L, GC) for i in range(2)]
        Kt = at(R + 9216, HP, 2, P)
        Wm = [at(R + 11264 + 1152 * i, HP, L + 1, GC) for i in range(2)]
        Kpad = [at(R + 13568 + 1024 * i, 4, 256, p1=GC) for i in range(2)]
        tA = R + 15616
        t1, t2 = (lambda *d: at(tA, *d)), (lambda *d: at(tA + 1152, *d))
        Vr, Vi = at(tA, HP, NCH), at(tA + 640, HP, NCH)
        Sr, Si = at(tA + 1280, HP, NCH), at(tA + 1920, HP, NCH)
        Tr, Ti = at(R + 18176, HP, PCH), at(R + 18688, HP, PCH)
        rho_t = at(R + 19200, HP, PCH)
        wr, wi = at(R + 19712, HP, PCH), at(R + 20224, HP, PCH)
        spos = [R + 20736]

        def small(*dims, **k):
            off = spos[0]
            spos[0] += int(np.prod(dims))
            assert spos[0] <= R + 23424
            return at(off, *dims, **k)

        par = small(3, GP)
        bc = small(4, GP, GC)
        Bb = [small(GP, GC) for _ in range(2)]
        Pw = [small(GP, L + 1) for _ in range(2)]
        Pv = [bc[:, r].rearrange("p a c -> p (a c)")[:, 0:GP * L].rearrange("p (a c) -> p a c", c=L) for r in range(2)]
        s0 = small(2, GP, NB)
        dskip = small(G, p1=GC)
        sm = [small(GP) for _ in range(14)]
        fin = small(2, GP, NB + 1)
        stage_off = R + 23424
        raw = [at(stage_off + 512 * i, 512) for i in range(2)]
        nrm = [at(stage_off + 1024 + 512 * i, 512) for i in range(2)]
        x_early = at(R + 9216, NT, D)
        mem_r = at(R + 2560, 2, D)
        squares = at(R + 14336, D)
        memT = at(4096, KT, NM)
        m_stage = [at(4096 + KT * NM + 512 * i, 512) for i in range(2)]

        ysT = at(R + 2560, 4, T)
        xr = at(R + 5120, NT, D)
        yaT = at(R, 4, T)
        qblk = at(R + 10240, NB, NPAIR, P)
        bias_p = at(R + 14336, NH, 256)
        kc = [at(R + 16384 + 2048 * i, NPAIR, 512) for i in range(2)]
        vc = [at(R + 20480 + 2048 * i, 4, 512) for i in range(2)]
        Pb = [at(HT + 640 * i, 640) for i in range(3)]
        PT = [at(HT + 1920 + 640 * i, 5, P) for i in range(4)]
        s_rows = [at(HT + 4480 + P * i, P) for i in range(2)]
        glu_t = [at(R + 16384 + 512 * i, 512) for i in range(2)]
        sq_t = at(HT, 2, T)

        qm = at(QT, 8, T)
        mk_rows = at(R + 14336, 2, D)
        mv_rows = at(R + 16384, 2, D)
        mkT = at(R + 18432, 8, NM)
        mraw = [at(R + 20480 + 512 * i, 512) for i in range(2)]
        mnrm = [at(R + 21504 + 512 * i, 512) for i in range(2)]
        mP = [at(R + 22528 + 256 * i, 256) for i in range(4)]
        mPT = [at(R + 23552 + 256 * i, 2, P) for i in range(4)]
        qblk2 = at(R, NB, 8, 64)
        mkc = [at(R + 10240, 8, NM), at(R + 14336, 8, NM)]
        mvc = [at(R + 12288, 2, D), at(R + 20480, 2, D)]
        sm_rows = [at(VR + D * i, D) for i in range(2)]
        oT = hT

        xn = [at(R + 10240 + 1024 * i, D) for i in range(2)]
        rpos = [R + 12288]

        def rt(*dims):
            off = rpos[0]
            rpos[0] += int(np.prod(dims))
            assert rpos[0] <= R + 15616
            return at(off, *dims)

        gu_buf = [at(o, KT, 512) for o in (0, 4096, 8192, QT)]
        dn_buf = [at(R + 15616 + 2048 * i, 2, D) for i in range(4)]
        xg = [at(HT + 1024 * i, D) for i in range(2)]
        xgT = [at(HT + 2048 + 1024 * i, KT, P) for i in range(2)]
        th_b = [at(HT + 4096 + 256 * i, 2, P) for i in range(2)]
        h_b = [at(HT + 4608 + 256 * i, 2, P) for i in range(2)]
        ye = [at(QT + 4096 + 1024 * i, D) for i in range(2)]
        a_b = at(QT + 6144, 2, P)
        yg = [at(1024 * i, D) for i in range(4)]

        product_ready = sem("product_ready")
        drained = {k: sem(f"drained_{k}") for k in KINDS}
        dve_chain, act_chain, pool_chain = sem("dve_chain"), sem("act_chain"), sem("pool_chain")
        w_landed = [sem(f"w_landed{i}") for i in range(3)]
        names = ("xT_landed xT_rest_landed w0_half_landed x_landed consts_landed ssm_landed rel_landed consts_built x_squared rstd_x_ready hT_ready "
                 "qk_stats qk_factor qk_normed k_stored0 k_stored1 v_stored u_stored0 u_stored1 U_landed U_turned b_ready w_ready "
                 "kpad_ready kt_landed0 kt_landed1 state_ready gelu_sq gelu_arg gelu_th gelu_ready "
                 "rel_built e_stored bias_landed bias_p_landed bias_built xr_landed glu_th "
                 "row_max p_normed p_scaled qblk_ready kc0 kc1 vc0 vc1 "
                 "mem_landed mem_squared rstd_m_ready memT_ready mk_stats mk_factor mk_normed mk_stored memT_landed m_stored0 m_stored1 "
                 "sq_ready sq_used rstd_g_ready branch_scaled x1_squared rstd_1_ready mq_stats mq_factor mq_normed "
                 "mrow_max mp_exp mp_scaled qblk2_ready "
                 "x2_squared rstd_2_ready xn_ready xn_stored0 xn_stored1 logits_ready "
                 "choice_exp choice_ready slots_ready rows_zeroed table_parts_ready s_stored").split()
        S = {n: sem(n) for n in names}

        def bank(key):
            return banks[:, NUMBER[key] % 8, :]

        def claim(pe, key):
            n = NUMBER[key]
            if n >= 8:
                kind, i = ORDER[n - 8]
                pe.wait_ge(drained[kind], i + 1)
            return banks[:, n % 8, :]

        def done(eng, key):
            eng.wait_ge(product_ready, NUMBER[key] + 1)

        logit = rt(NT, NG + NE)
        chosen = rt(NT, NE)
        oh = rt(2, NT, NE)
        oh1, oh2 = oh[:, 0], oh[:, 1]
        lsel, rtmp = rt(NT, NE), rt(2, NT, NE)
        gsm = [rt(NT, NG) for _ in range(3)]
        rs_ = [rt(NT) for _ in range(5)]
        rs2_ = [rt(2, NT) for _ in range(5)]
        slot_f, w12 = rt(2, NT), rt(2, NT)
        rank_sb = rt(NT + 1, NE)
        extra, incl, ovb = rt(NE), rt(NE), rt(NE)
        ovt, ovf = rt(NOV, NE), rt(NOV + 1)
        zeros = at(R + 24576, 512)
        slot_hot = at(R, 2, NT, CAP)
        unit_tok = at(R + 2 * NT * CAP, 2, NT, NU)

        moe_names = ("tx_done xgT_ready gu_done th_ready h_ready dn_done ye_ready xg0 xg1 y_st0 y_st1 "
                     "gu_l0 gu_l1 gu_l2 gu_l3 dn_l0 dn_l1 dn_l2 dn_l3 yg_landed0 yg_landed1 y_ready y_out "
                     "o_w").split()
        moe = {n: sem("moe_" + n) for n in moe_names}

        moe_a = sem("moe_silu_ready")
        n_mem_units = len(MEM_UNITS) + 4

        def late(i, c, n):
            return not isinstance(i, int) or 4 * i + c >= n

        def wo_rows(wo, k, c):
            return wo[c][:, k, :]

        def ssm_scalar(act, link):
            A = nc.scalar.activation
            act.wait_ge(S["ssm_landed"], 64)
            A(sm[0], par[:, 2, :], ACT.Exp).then_inc(act_ssm, 1)
            act.wait_ge(dve_ssm, 1)
            A(sm[3], sm[1], ACT.Exp).then_inc(act_ssm, 1)
            A(sm[6], sm[1], ACT.Exp, scale=float(L)).then_inc(act_ssm, 1)
            A(sm[4], sm[2], ACT.Sin).then_inc(act_ssm, 1)
            A(sm[5], sm[2], ACT.Sin, scale=0.5).then_inc(act_ssm, 1)

        act_ssm, dve_ssm = sem("ssm_functions"), sem("ssm_arguments")

        def moe_load_first(sp, e):
            if e == 0:
                done(sp, ("mq", 9))
                done(sp, ("mo", 9))
            sp.dma_start(gu_buf[e], exp_gu[e]).then_inc(moe[f"gu_l{e}"], 16)
            if e == 0:
                sp.wait_ge(S["mk_stored"], 16)
            sp.dma_start(dn_buf[e], exp_dn[e]).then_inc(moe[f"dn_l{e}"], 16)

        def moe_sync(sp):
            def step(i, c):
                s = 4 * i + c
                if c >= 1:
                    e = (c + 3) % 4
                    sp.wait_ge(moe["gu_done"], s)
                    sp.dma_start(gu_buf[e], exp_gu[bass.ds(s + 3, 1)].rearrange("e p k n -> (e p) k n")).then_inc(moe[f"gu_l{e}"], 16)
                    sp.wait_ge(moe["dn_done"], 2 * s)
                    sp.dma_start(dn_buf[e], exp_dn[bass.ds(s + 3, 1)].rearrange("e p k n -> (e p) k n")).then_inc(moe[f"dn_l{e}"], 16)
                    store(i, c)

            def store(i, c):
                s = 4 * i + c
                sp.wait_ge(moe["ye_ready"], 2 * s)
                sp.dma_start(moe_dram.ap()[bass.ds((s - 1) * CAP, CAP), :], ye[(c - 1) % 2][0:CAP, :]).then_inc(moe[f"y_st{(c - 1) % 2}"], 16)

            with sp.Fori(0, 7) as i:
                for c in range(1, 5):
                    step(i, c)
            for c in range(29, 33):
                store(0, c)
            sp.wait_ge(S["rows_zeroed"], 16 * NOV)
            nov = sp.value_load(ov_regs[0:1, NOV:NOV + 1], min_val=0, max_val=NOV)
            with sp.Fori(0, NOV) as v:
                with sp.If(v < nov):
                    ex = sp.value_load(ov_regs[0:1, bass.ds(v, 1)], min_val=0, max_val=NE - 1)
                    sp.wait_ge(moe["dn_done"], 2 * NE + v)
                    sp.dma_start(gu_buf[0], exp_gu[bass.ds(ex, 1)].rearrange("e p k n -> (e p) k n")).then_inc(moe["o_w"], 16)
                    sp.dma_start(dn_buf[0], exp_dn[bass.ds(ex, 1)].rearrange("e p k n -> (e p) k n")).then_inc(moe["o_w"], 16)
                    sp.wait_ge(moe["ye_ready"], 2 * NE + v + 1)
                    sp.dma_start(moe_dram.ap()[bass.ds((v + NE) * CAP, CAP), :], ye[0][0:CAP, :]).then_inc(moe["y_st0"], 16)

        def unit_turn(ps, src, xi):
            for a in range(4):
                last = nc.tensor.transpose(ps[:, a * P:a * P + CAP], src[0:CAP, (4 * xi + a) * P:(4 * xi + a + 1) * P], ident[0:CAP, 0:CAP])
            return last

        def unit_gate_up(ps, x, w):
            for f in range(4):
                for k in range(KT):
                    last = nc.tensor.matmul(ps[:, f * P:f * P + CAP], w[:, k, f * P:(f + 1) * P], x[:, k, 0:CAP],
                                            start=(k == 0), stop=(k == KT - 1))
            return last

        def unit_down(ps, hb, w, c):
            for k in range(2):
                last = nc.tensor.matmul(ps[0:CAP, :], hb[:, k, 0:CAP], w[:, k, c * 512:(c + 1) * 512], start=(k == 0), stop=(k == 1))
            return last

        def moe_tensor(pe):
            def TX(i, c):
                e = 4 * i + c
                pe.wait_ge(moe[f"xg{c % 2}"], 32 * i + 16 * (c // 2 + 1))
                for xi in range(2):
                    if late(i, c, 2):
                        pe.wait_ge(moe["xgT_ready"], 2 * e - 3 + xi)
                    unit_turn(banks[:, 2 * (c % 2) + xi, :], xg[c % 2], xi).then_inc(moe["tx_done"], 1)

            def GU(i, c):
                e = 4 * i + c
                pe.wait_ge(moe["xgT_ready"], 2 * e + 2)
                pe.wait_ge(moe[f"gu_l{c % 4}"], 16 * i + 16 * (c // 4 + 1))
                if late(i, c, 2):
                    pe.wait_ge(moe["h_ready"], e - 1)
                unit_gate_up(banks[:, 4 + c % 2, :], xgT[c % 2], gu_buf[c % 4]).then_inc(moe["gu_done"], 1)

            def DN(i, c):
                e = 4 * i + c
                pe.wait_ge(moe["h_ready"], e + 1)
                pe.wait_ge(moe[f"dn_l{c % 4}"], 16 * i + 16 * (c // 4 + 1))
                for ch in range(2):
                    if late(i, c, 1):
                        pe.wait_ge(moe["ye_ready"], 2 * e - 1 + ch)
                    unit_down(banks[:, 6 + ch, :], h_b[c % 2], dn_buf[c % 4], ch).then_inc(moe["dn_done"], 1)

            for kind, j in ORDER[-8:]:
                pe.wait_ge(drained[kind], j + 1)
            TX(0, 0)
            TX(0, 1)
            GU(0, 0)
            peeled = [1, 2, 3, 4]
            for c in peeled:
                TX(0, c + 1)
                GU(0, c)
                DN(0, c - 1)
            with pe.Fori(1, 7) as i:
                for c in range(1, 5):
                    TX(i, c + 1)
                    GU(i, c)
                    DN(i, c - 1)
            for c in range(29, 32):
                if c < 31:
                    TX(0, c + 1)
                GU(0, c)
                DN(0, c - 1)
            DN(0, 31)
            nov = pe.value_load(ov_regs[0:1, NOV:NOV + 1], min_val=0, max_val=NOV)
            with pe.Fori(0, NOV) as v:
                with pe.If(v < nov):
                    pe.wait_ge(moe["xg0"], 16 * (NE // 2) + 16 * v + 16)
                    for xi in range(2):
                        unit_turn(banks[:, xi, :], xg[0], xi).then_inc(moe["tx_done"], 1)
                    pe.wait_ge(moe["xgT_ready"], 2 * NE + 2 * v + 2)
                    pe.wait_ge(moe["o_w"], 32 * v + 32)
                    unit_gate_up(banks[:, 4, :], xgT[0], gu_buf[0]).then_inc(moe["gu_done"], 1)
                    pe.wait_ge(moe["h_ready"], NE + v + 1)
                    pe.wait_ge(moe["ye_ready"], 2 * NE + v)
                    unit_down(banks[:, 6, :], h_b[0], dn_buf[0], 0)
                    unit_down(banks[:, 7, :], h_b[0], dn_buf[0], 1).then_inc(moe["dn_done"], 1)

        block = ctx.enter_context(nc.Block())

        @block.sync
        def _(sp):
            def load_w(u):
                if W_AFTER.get(u):
                    done(sp, W_AFTER[u])
                sp.dma_start(wdense(u), dense_w[u]).then_inc(w_landed[W_SLOT[u]], 16)

            sp.dma_start(colc[:, 0:43], cols).then_inc(S["xT_landed"], 16)
            sp.dma_start(hT[:, :, 0:P], x_t[:, :, 0:P]).then_inc(S["xT_landed"], 16)
            sp.dma_start(wdense(0)[:, 0:2048], dense_w[0][:, 0:2048]).then_inc(S["w0_half_landed"], 16)
            sp.dma_start(wdense(0)[:, 2048:4096], dense_w[0][:, 2048:4096]).then_inc(w_landed[0], 16)
            sp.dma_start(hT[:, :, P:T], x_t[:, :, P:T]).then_inc(S["xT_rest_landed"], 16)
            sp.dma_start(x_early, x_rows.rearrange("(t p) d -> p t d", p=P)).then_inc(S["x_landed"], 16)
            sp.dma_start(par, ssm_small).then_inc(S["ssm_landed"], 16)
            sp.dma_start(bc, ssm_bc).then_inc(S["ssm_landed"], 16)
            sp.dma_start(s0, ssm_s0).then_inc(S["ssm_landed"], 16)
            sp.dma_start(dskip, ssm_d).then_inc(S["ssm_landed"], 16)
            load_w(1)
            sp.dma_start(kg, k_gain.partition_broadcast(P)).then_inc(S["consts_landed"], 16)
            sp.dma_start(mkg, mk_gain.partition_broadcast(P)).then_inc(S["consts_landed"], 16)
            sp.dma_start(rw, router_w).then_inc(S["consts_landed"], 16)
            sp.dma_start(rb, router_b.partition_broadcast(P)).then_inc(S["consts_landed"], 16)
            sp.dma_start(rel_ext[0:NH, P:385], rel_rev).then_inc(S["rel_landed"], 16)
            load_w(2)
            sp.dma_start(mem_r, mem_rows.rearrange("(t p) d -> p t d", p=P)).then_inc(S["mem_landed"], 16)
            load_w(3)
            done(sp, ("qk", 4))
            sp.dma_start(memT, mem_t).then_inc(S["memT_landed"], 16)
            sp.wait_ge(S["u_stored0"], 48)
            sp.wait_ge(S["u_stored1"], 32)
            done(sp, ("qk", 9))
            sp.dma_start(at(8192, 4096, p1=NCH), u_dram.ap().rearrange("(c j) d -> c (j d)", j=L)).then_inc(S["U_landed"], 16)
            sp.wait_ge(S["e_stored"], 16)
            for h in range(NH):
                src = bass.AP(e_dram, h * P * 385 + P, [[384, SQ], [1, 144]])
                sp.dma_start(bias_s[SQ * h:SQ * h + SQ, :], src).then_inc(S["bias_landed"], 16)
            sp.wait_ge(S["U_turned"], 1)
            load_w(5)
            for i in range(8):
                if i == 4:
                    load_w(6)
                    load_w(7)
                    load_w(8)
                sp.wait_ge(S["kpad_ready"], i + 1)
                if i % 4 == 0:
                    done(sp, ("G", i + 3))
                if i == 4:
                    done(sp, ("Y", 3))
                q = (i % 4) // 2
                for j in range(L):
                    sp.dma_start(Kt[GC * j:GC * j + GC, 4 * q:4 * q + 4, i % 2, :],
                                 Kpad[i % 2][:, :, P - GC * j:2 * P - GC * j]).then_inc(S[f"kt_landed{i % 2}"], 16)
            load_w(4)
            done(sp, ("Y", 7))
            sp.dma_start(xr, x_rows.rearrange("(t p) d -> p t d", p=P)).then_inc(S["xr_landed"], 16)
            sp.wait_ge(S["kt_landed0"], 16 * 32)
            sp.wait_ge(S["kt_landed1"], 16 * 32)
            src = bass.AP(e_dram, P, [[384, P], [P * 385, NH], [1, 256]])
            sp.dma_start(bias_p, src).then_inc(S["bias_p_landed"], 16)
            for i in range(2):
                sp.wait_ge(S[f"m_stored{i}"], 16 * 4)
            load_w(9)
            load_w(10)

            def load_keys(b):
                if b >= 2:
                    done(sp, ("sB", b - 2))
                elif b == 0:
                    sp.wait_ge(S["s_stored"], 16)
                    sp.wait_ge(S["k_stored0"], 32)
                    sp.wait_ge(S["k_stored1"], 48)
                    sp.wait_ge(drained["gs"], 4)
                sp.dma_start(kc[b % 2], ck_t[b]).then_inc(S[f"kc{b % 2}"], 16)

            def load_values(b):
                if b >= 2:
                    done(sp, ("sPV", b - 2))
                sp.dma_start(vc[b % 2], cv[b].rearrange("(t p) d -> p t d", p=P)).then_inc(S[f"vc{b % 2}"], 16)

            load_keys(0)
            load_keys(1)
            load_values(0)
            load_values(1)
            load_keys(2)
            for b in range(3, NB):
                load_keys(b)
                load_values(b - 1)
            load_values(NB - 1)
            done(sp, ("sB", NB - 1))
            sp.dma_start(mk_rows, mk_dram.ap().rearrange("(t p) d -> p t d", p=P)).then_inc(S["mem_landed"], 16)
            sp.dma_start(mv_rows, mv_out.rearrange("(t p) d -> p t d", p=P)).then_inc(S["mem_landed"], 16)

            def load_mem_keys(b):
                if b >= 2:
                    done(sp, ("mS", len(MEM_UNITS) + (b - 2) // 2))
                elif b == 1:
                    sp.wait_ge(S["mk_stored"], 16)
                    done(sp, ("mkT", 3))
                sp.dma_start(mkc[b % 2], cmk_t[b]).then_inc(S[f"kc{b % 2}"], 16)

            def load_mem_values(b):
                if b >= 2:
                    done(sp, ("smPV", 2 * (b // 2) - 1))
                elif b == 1:
                    done(sp, ("mqT", 9))
                else:
                    done(sp, ("sPV", NB - 1))
                sp.dma_start(mvc[b % 2], cmv[b].rearrange("(t p) d -> p t d", p=P)).then_inc(S[f"vc{b % 2}"], 16)

            load_w(11)
            load_mem_keys(0)
            load_mem_values(0)
            load_mem_keys(1)
            load_w(12)
            load_w(13)
            load_w(14)
            load_mem_values(1)
            for load, bs in ((load_mem_keys, (2, 3, 4, 5)), (load_mem_values, (2, 3)), (load_mem_keys, (6, 7)),
                             (load_mem_values, (4, 5, 6, 7))):
                for b in bs:
                    load(b)

            for e in range(4):
                moe_load_first(sp, e)
            moe_sync(sp)
            for t in range(NT):
                sp.wait_ge(moe["y_ready"], t + 1)
                sp.dma_start(y_out[t * P:(t + 1) * P, :], xr[:, t, :]).then_inc(moe["y_out"], 16)
            sp.wait_ge(moe["y_out"], 16 * NT)
            sp.wait_ge(S["v_stored"], 16)

        @block.tensor
        def _(pe):
            def dense(key, lhs, rhs, n, k=KT):
                ps = claim(pe, key)
                for i in range(k):
                    last = nc.tensor.matmul(ps[:, 0:n], lhs(i), rhs(i), start=(i == 0), stop=(i == k - 1))
                last.then_inc(product_ready, 1)

            def w_at(u, first=True):
                if first:
                    pe.wait_ge(w_landed[W_SLOT[u]], 16 * w_count(u))
                return wdense(u).rearrange("p (k n) -> p k n", k=KT)

            def tok(t):
                return slice(t * P, (t + 1) * P)

            def qkT(i):
                ps = claim(pe, ("qkT", i)).rearrange("p (a b) -> p a b", a=4)
                pe.wait_ge(S["qk_normed"], i + 1)
                for a in range(NPAIR):
                    last = nc.tensor.transpose(ps[:, a, :], nrm[i % 2][:, a * P:(a + 1) * P], ident)
                last.then_inc(product_ready, 1)

            w = w_at(0, False)
            for t in range(NT):
                if t < 2:
                    pe.wait_ge(S["hT_ready"], t + 1)
                ps = claim(pe, ("u", t))
                for k in range(KT):
                    if t == 0 and k == 0:
                        pe.wait_ge(S["w0_half_landed"], 16)
                    if t == 0 and k == 4:
                        pe.wait_ge(w_landed[0], 16)
                    last = nc.tensor.matmul(ps, hT[:, k, tok(t)], w[:, k, :], start=(k == 0), stop=(k == KT - 1))
                last.then_inc(product_ready, 1)
            pe.wait_ge(S["consts_built"], 1)
            for i in range(10):
                w = w_at(1 + i // 5, i % 5 == 0)
                dense(("qk", i), lambda k: hT[:, k, tok(i % 5)], lambda k: w[:, k, :], 512)
                if i >= 2:
                    qkT(i - 2)
            def v_product(t):
                w = w_at(3, t == 0)
                dense(("v", t), lambda k: hT[:, k, tok(t)], lambda k: w[:, k, :], 512)

            def mem_product(kind, i):
                w = w_at((5 if kind == "mk" else 7) + i // 2, i % 2 == 0)
                if kind == "mk" and i == 0:
                    pe.wait_ge(S["memT_ready"], 1)
                dense((kind, i), lambda k: memT[:, k, tok(i % 2)], lambda k: w[:, k, :], 512)

            def fill(products):
                for kind, i in products:
                    if kind == "v":
                        v_product(i)
                    else:
                        mem_product(kind, i)

            for t in range(3):
                v_product(t)
                if t < 2:
                    qkT(8 + t)

            pe.wait_ge(S["U_turned"], 1)
            for i in range(8):
                ps = claim(pe, ("UT", i)).rearrange("p (a b) -> p a b", a=4)
                for a in range(4):
                    g = 4 * i + a
                    last = nc.tensor.transpose(ps[:, a, 0:NCH], U[:, g, :], ident[0:NCH, 0:NCH])
                last.then_inc(product_ready, 1)

            for hf in range(HALVES):
                pe.wait_ge(S["b_ready"], hf + 1)
                for i in range(4):
                    ps = claim(pe, ("G", 4 * hf + i)).rearrange("p (a r b) -> p a r b", a=2, r=2)
                    for a in range(2):
                        for r in range(2):
                            last = nc.tensor.transpose(ps[:, a, r, :], BL[r][:, 2 * i + a, :, :].rearrange("p j c -> p (j c)"), ident)
                    last.then_inc(product_ready, 1)
                fill(FILL[hf][0])
                pe.wait_ge(S["w_ready"], hf + 1)
                for i in range(4):
                    ps = claim(pe, ("K", 4 * hf + i)).rearrange("p (a b) -> p a b", a=4)
                    lo = GS * (i % 2)
                    for a in range(4):
                        pr = 4 * (i // 2) + a
                        for r in range(2):
                            last = nc.tensor.matmul(ps[0:GC, a, :], Bb[r][lo:lo + GS, HP * hf + pr, :],
                                                    Wm[r][lo:lo + GS, pr, 0:L, :].rearrange("p j c -> p (j c)"),
                                                    start=(r == 0), stop=(r == 1))
                    last.then_inc(product_ready, 1)
                pe.wait_ge(drained["UT"], 8)
                pe.wait_ge(drained["G"], 4 * hf + 4)
                for i in range(4):
                    ps = claim(pe, ("V", 4 * hf + i))
                    r = i % 2
                    for a in range(4):
                        pr = 4 * (i // 2) + a
                        for g2 in range(2):
                            last = nc.tensor.matmul(ps[GS * g2:GS * g2 + GS, a * NCH:(a + 1) * NCH],
                                                    Gm[:, pr, r, GS * g2:GS * g2 + GS],
                                                    UT[:, 2 * (HP * hf + pr) + g2, :], start=True, stop=True)
                    last.then_inc(product_ready, 1)
                fill(FILL[hf][1])
                pe.wait_ge(S["state_ready"], hf + 1)
                for i in range(4):
                    ps = claim(pe, ("Y", 4 * hf + i)).rearrange("p (a b) -> p a b", a=4)
                    g2 = i % 2
                    lo = GS * g2
                    pe.wait_ge(S[f"kt_landed{g2}"], 16 * 8 * (2 * hf + i // 2 + 1))
                    for a in range(4):
                        pr = 4 * (i // 2) + a
                        nc.tensor.matmul(ps[0:NCH, a, :], UT[:, 2 * (HP * hf + pr) + g2, :], Kt[:, pr, g2, :],
                                         start=True, stop=False)
                        for r, st in ((0, Sr), (1, Si)):
                            last = nc.tensor.matmul(ps[0:NCH, a, :], st[lo:lo + GS, pr, :],
                                                    Wm[r][lo:lo + GS, pr, 1:L + 1, :].rearrange("p j c -> p (j c)"),
                                                    start=False, stop=(r == 1))
                    last.then_inc(product_ready, 1)
                pe.wait_ge(drained["Y"], 4 * hf + 4)
                for i in range(4):
                    ps = claim(pe, ("YT", 4 * hf + i)).rearrange("p (a b) -> p a b", a=4)
                    for a in range(4):
                        last = nc.tensor.transpose(ps[:, a, 0:NCH], Yh[:, 4 * (i % 2) + a, P * (i // 2):P * (i // 2) + P],
                                                   ident[0:NCH, 0:NCH])
                    last.then_inc(product_ready, 1)

                fill(FILL[hf][2])

            wg = w_at(4).rearrange("p k n -> p (k n)").rearrange("p (k n) -> p k n", k=4)
            pe.wait_ge(S["gelu_ready"], 1)
            for c in range(4):
                for kind, o in (("gg", 512), ("gv", 0)):
                    dense((kind, c), lambda k: wg[:, k, o + c * P:o + (c + 1) * P], lambda k: yT[:, k, 0:TP], TP, 4)
            for c in range(4):
                ps = claim(pe, ("gs", c))
                for j, o in enumerate((512, 0)):
                    for k in range(4):
                        last = nc.tensor.matmul(ps[:, j * P:(j + 1) * P], wg[:, k, o + c * P:o + (c + 1) * P],
                                                yT[:, k, TP:T], start=(k == 0), stop=(k == 3))
                last.then_inc(product_ready, 1)

            pe.wait_ge(drained["qkT"], 10)
            pe.wait_ge(drained["v"], NT)

            def scores(i):
                t, h = PROMPT_UNITS[i]
                ps = claim(pe, ("S", i))
                lo = HD * (h % 2)
                nc.tensor.matmul(ps[:, 0:P * (t + 1)], qT[lo:lo + HD, h // 2, tok(t)], kT[lo:lo + HD, h // 2, 0:P * (t + 1)],
                                 start=True, stop=True).then_inc(product_ready, 1)

            def turn(kind, i, unit, tiles, first=0):
                ps = claim(pe, (kind, i)).rearrange("p (a b) -> p a b", a=4)
                pe.wait_ge(S["p_scaled"], unit + 1)
                for a in range(tiles):
                    last = nc.tensor.transpose(ps[:, a, :], Pb[unit % 3][:, (first + a) * P:(first + a + 1) * P], ident)
                last.then_inc(product_ready, 1)

            n = len(PROMPT_UNITS)
            for i in range(n + 4):
                if i < n:
                    scores(i)
                if 0 <= i - 2 < n:
                    turn("PT", i - 2, i - 2, PROMPT_UNITS[i - 2][0] + 1)
                if i >= 4 and (i - 4) % 2 == 1 and i - 4 < n:
                    m = (i - 4) // 2
                    ps = claim(pe, ("PV", m))
                    pe.wait_ge(drained["PT"], i - 3)
                    for unit in (i - 5, i - 4):
                        t, h = PROMPT_UNITS[unit]
                        lo = HD * (h % 2)
                        for k in range(t + 1):
                            last = nc.tensor.matmul(ps[lo:lo + HD, 0:P], v_rows[:, k, h * HD:(h + 1) * HD],
                                                    PT[unit % 4][:, k, :], start=(k == 0), stop=(k == t))
                    last.then_inc(product_ready, 1)
            pe.wait_ge(S["qblk_ready"], 1)
            for b in range(NB + 3):
                if b < NB:
                    ps = claim(pe, ("sA", b))
                    pe.wait_ge(S[f"kc{b % 2}"], 16 * (b // 2 + 1))
                    for a in range(NPAIR):
                        last = nc.tensor.matmul(ps, qblk[:, b, a, :], kc[b % 2][:, a, :], start=(a == 0), stop=(a == 3))
                    last.then_inc(product_ready, 1)
                    ps = claim(pe, ("sB", b))
                    for a in range(NPAIR):
                        last = nc.tensor.matmul(ps[:, 0:P], qblk[:, b, a, :], kT[:, a, TP:T], start=(a == 0), stop=(a == 3))
                    last.then_inc(product_ready, 1)
                if 0 <= b - 1 < NB:
                    turn("sPa", b - 1, n + b - 1, 4)
                    turn("sPb", b - 1, n + b - 1, 1, first=4)
                if 0 <= b - 2 < NB:
                    c = b - 2
                    ps = claim(pe, ("sPV", c))
                    pe.wait_ge(drained["sPb"], c + 1)
                    pe.wait_ge(S[f"vc{c % 2}"], 16 * (c // 2 + 1))
                    for a in range(NPAIR):
                        for k in range(5):
                            v = vc[c % 2][:, k, a * P:(a + 1) * P] if k < 4 else v_rows[:, 4, a * P:(a + 1) * P]
                            last = nc.tensor.matmul(ps[a * 32:(a + 1) * 32, 0:P], PT[(n + c) % 4][:, k, a * 32:(a + 1) * 32], v,
                                                    start=(k == 0), stop=(k == 4))
                    last.then_inc(product_ready, 1)
                if 0 <= b - 3 < NB:
                    ps = claim(pe, ("sO", b - 3))
                    pe.wait_ge(drained["sPV"], b - 2)
                    nc.tensor.transpose(ps[:, 0:P], s_rows[(b - 3) % 2], ident).then_inc(product_ready, 1)

            for i in range(4):
                ps = claim(pe, ("mkT", i)).rearrange("p (a b) -> p a b", a=4)
                pe.wait_ge(S["mk_normed"], i + 1)
                for a in range(4):
                    last = nc.tensor.transpose(ps[:, a, :], mk_rows[:, i // 2, (i % 2) * 512 + a * P:(i % 2) * 512 + (a + 1) * P], ident)
                last.then_inc(product_ready, 1)

            ps = claim(pe, ("ss", 0))
            for br in range(2):
                for k in range(4):
                    pe.wait_ge(S["sq_ready"], 4 * br + k + 1)
                    for t in range(NT):
                        last = nc.tensor.matmul(ps[:, (br * 4 + k) * NT + t:(br * 4 + k) * NT + t + 1],
                                                sq_t[:, (4 * br + k) % 2, tok(t)], ones[:, 0:1], start=True, stop=True)
                    if k < 3 or br == 0:
                        last.then_inc(S["sq_used"], 1)
            last.then_inc(product_ready, 1)

            def turn_rows(kind, i):
                t, hh = i // 2, i % 2
                ps = claim(pe, (kind, i)).rearrange("p (a b) -> p a b", a=4)
                for a in range(4):
                    last = nc.tensor.transpose(ps[:, a, :], xr[:, t, (4 * hh + a) * P:(4 * hh + a + 1) * P], ident)
                last.then_inc(product_ready, 1)

            pe.wait_ge(S["branch_scaled"], 2)
            wo = [w_at(9), w_at(10)]
            for t in range(NT + 1):
                if t < NT:
                    for c in range(2):
                        for kind, k0, src in (("oS", 0, ysT), ("oA", 4, yaT)):
                            dense((kind, 2 * t + c), lambda k: src[:, k, tok(t)],
                                  lambda k: wo_rows(wo, k0 + k, c), 512, 4)
                if t >= 1:
                    for hh in range(2):
                        pe.wait_ge(drained["oA"], 2 * t - 1 + hh)
                        turn_rows("x1T", 2 * t - 2 + hh)
            pe.wait_ge(drained["x1T"], 10)
            wq = [w_at(11), w_at(12)]
            for i in range(12):
                if i < 10:
                    dense(("mq", i), lambda k: hT[:, k, tok(i // 2)], lambda k: wq[i % 2][:, k, :], 512)
                if i >= 2:
                    j = i - 2
                    ps = claim(pe, ("mqT", j)).rearrange("p (a b) -> p a b", a=4)
                    pe.wait_ge(S["mq_normed"], j + 1)
                    for a in range(4):
                        last = nc.tensor.transpose(ps[:, a, :], mnrm[j % 2][:, a * P:(a + 1) * P], ident)
                    last.then_inc(product_ready, 1)
            pe.wait_ge(drained["mqT"], 10)
            pe.wait_ge(drained["mkT"], 4)
            n = len(MEM_UNITS)

            def mem_turn(i):
                ps = claim(pe, ("mPT", i)).rearrange("p (a b) -> p a b", a=4)
                pe.wait_ge(S["mp_scaled"], i + 1)
                for a in range(2):
                    last = nc.tensor.transpose(ps[:, a, :], mP[i % 4][:, a * P:(a + 1) * P], ident)
                last.then_inc(product_ready, 1)

            for i in range(n + 3):
                if i < n:
                    t, h = MEM_UNITS[i]
                    dense(("mS", i), lambda k: qm[:, 2 * h + k, tok(t)], lambda k: mkT[:, 2 * h + k, :], NM, 2)
                if 0 <= i - 2 < n:
                    mem_turn(i - 2)
                if 0 <= i - 3 < n:
                    j = i - 3
                    t, h = MEM_UNITS[j]
                    ps = claim(pe, ("mPV", j)).rearrange("p (a b) -> p a b", a=4)
                    pe.wait_ge(drained["mPT"], j + 1)
                    for dt in range(2):
                        for k in range(2):
                            last = nc.tensor.matmul(ps[:, dt, :], mv_rows[:, k, h * MD + dt * P:h * MD + (dt + 1) * P],
                                                    mPT[j % 4][:, k, :], start=(k == 0), stop=(k == 1))
                    last.then_inc(product_ready, 1)
            pe.wait_ge(S["qblk2_ready"], 1)
            for i in range(7):
                if i < 4:
                    ps = claim(pe, ("mS", n + i))
                    for b2 in range(2):
                        pe.wait_ge(S[f"kc{b2}"], 16 * (NB // 2 + i + 1))
                        for k in range(8):
                            last = nc.tensor.matmul(ps[64 * b2:64 * b2 + 64, 0:NM], qblk2[:, 2 * i + b2, k, :], mkc[b2][:, k, :],
                                                    start=(k == 0), stop=(k == 7))
                    last.then_inc(product_ready, 1)
                if 0 <= i - 1 < 4:
                    mem_turn(n + i - 1)
                if 0 <= i - 2 < 4:
                    pe.wait_ge(drained["mPT"], n + i - 1)
                    for c in range(2):
                        ps = claim(pe, ("smPV", 2 * (i - 2) + c))
                        for b2 in range(2):
                            pe.wait_ge(S[f"vc{b2}"], 16 * (NB // 2 + i - 1))
                            for k in range(2):
                                last = nc.tensor.matmul(ps[64 * b2:64 * b2 + 64, :], mPT[(n + i - 2) % 4][:, k, 64 * b2:64 * b2 + 64],
                                                        mvc[b2][:, k, 512 * c:512 * c + 512], start=(k == 0), stop=(k == 1))
                        last.then_inc(product_ready, 1)
                if 0 <= i - 3 < 4:
                    for c in range(2):
                        j = 2 * (i - 3) + c
                        ps = claim(pe, ("smT", j)).rearrange("p (a b) -> p a b", a=4)
                        pe.wait_ge(drained["smPV"], j + 1)
                        for a in range(4):
                            last = nc.tensor.transpose(ps[:, a, :], sm_rows[(i - 3) % 2][:, (4 * c + a) * P:(4 * c + a + 1) * P], ident)
                        last.then_inc(product_ready, 1)
            wo2 = [w_at(13), w_at(14)]
            pe.wait_ge(drained["mPV"], n)
            pe.wait_ge(drained["smT"], NB)
            for t in range(NT + 1):
                if t < NT:
                    for c in range(2):
                        dense(("mo", 2 * t + c), lambda k: oT[:, k, tok(t)], lambda k: wo2[c][:, k, :], 512)
                if t >= 1:
                    for hh in range(2):
                        pe.wait_ge(drained["mo"], 2 * t - 1 + hh)
                        turn_rows("x2T", 2 * t - 2 + hh)
            pe.wait_ge(drained["x2T"], 10)
            for t in range(NT):
                dense(("rt", t), lambda k: hT[:, k, tok(t)], lambda k: rw[:, k, :], NG + NE)
            pe.wait_ge(S["choice_ready"], 1)
            ps = claim(pe, ("rank", 0))
            for t in range(NT + 1):
                for k in range(min(t + 1, NT)):
                    last = nc.tensor.matmul(ps[:, t * NE:(t + 1) * NE], tri if k == t else ones, chosen[:, k, :],
                                            start=(k == 0), stop=(k == min(t, NT - 1)))
            last.then_inc(product_ready, 1)
            ps = claim(pe, ("tab", 0))
            pe.wait_ge(S["table_parts_ready"], 1)
            for j in range(2):
                for t in range(NT):
                    last = nc.tensor.matmul(ps[0:CAP, 0:NU], slot_hot[:, j, t, :], unit_tok[:, j, t, :],
                                            start=(j == t == 0), stop=(j == 1 and t == NT - 1))
            last.then_inc(product_ready, 1)
            moe_tensor(pe)

        @block.scalar
        def _(act):
            n_chain = [0]

            def link(ins):
                n_chain[0] += 1
                ins.then_inc(act_chain, 1)
                act.wait_ge(act_chain, n_chain[0])

            A = nc.scalar.activation
            act.wait_ge(S["x_landed"], 16)
            for t in range(NT):
                if t:
                    act.wait_ge(S["x_squared"], t)
                A(squares, x_early[:, t, :], ACT.Square, accum_out=ssx[:, t:t + 1]).then_inc(S["x_squared"], 1)
            ssm_scalar(act, link)
            act.wait_ge(S["rstd_x_ready"], 1)
            for t in range(NT):
                done(act, ("u", t))
                if t >= 2:
                    act.wait_ge(S[f"u_stored{t % 2}"], 16 * (t // 2))
                A(raw[t % 2], bank(("u", t)), ACT.Copy, scale=rstd_x[:, t:t + 1]).then_inc(drained["u"], 1)
            act.wait_ge(S["mem_landed"], 16)
            for t in range(2):
                act.wait_ge(*((S["mem_squared"], t) if t else (S["x_squared"], NT)))
                A(squares, mem_r[:, t, :], ACT.Square, accum_out=ssm_[:, t:t + 1]).then_inc(S["mem_squared"], 1)
            act.wait_ge(S["u_stored0"], 48)
            act.wait_ge(S["u_stored1"], 32)

            def qkT(i):
                done(act, ("qkT", i))
                src = bank(("qkT", i)).rearrange("p (a b) -> p a b", a=4)
                dst = (qT if i < 5 else kT)[:, :, (i % 5) * P:(i % 5 + 1) * P]
                if i < 5:
                    A(dst, src, ACT.Copy, scale=tmp48[:, 0:1]).then_inc(drained["qkT"], 1)
                else:
                    A(dst, src, ACT.Copy).then_inc(drained["qkT"], 1)

            act.wait_ge(S["hT_ready"], 3)
            for i in range(10):
                done(act, ("qk", i))
                if i >= 2:
                    act.wait_ge(S["qk_normed"], i - 1)
                A(raw[i % 2], bank(("qk", i)), ACT.Copy, scale=rstd_x[:, i % 5:i % 5 + 1]).then_inc(drained["qk"], 1)
                if i >= 2:
                    qkT(i - 2)
            def v_out_rows(t):
                done(act, ("v", t))
                A(v_rows[:, t, :], bank(("v", t)), ACT.Copy, scale=rstd_x[:, t:t + 1]).then_inc(drained["v"], 1)

            def mem_rows_out(kind, i):
                n = i if kind == "mk" else 4 + i
                done(act, (kind, i))
                if n == 0:
                    act.wait_ge(S["rstd_m_ready"], 1)
                if n >= 2:
                    act.wait_ge(S[f"m_stored{n % 2}"], 16 * (n // 2))
                A(m_stage[n % 2], bank((kind, i)), ACT.Copy, scale=rstd_m[:, i % 2:i % 2 + 1]).then_inc(drained[kind], 1)

            def fill(products):
                for kind, i in products:
                    if kind == "v":
                        v_out_rows(i)
                    else:
                        mem_rows_out(kind, i)

            for t in range(3):
                v_out_rows(t)
                if t < 2:
                    qkT(8 + t)
            act.wait_ge(S["U_landed"], 16)
            A(U.rearrange("p g (j c) -> p j g c", j=L), Uc.rearrange("p j (g c) -> p j g c", g=G), ACT.Copy).then_inc(S["U_turned"], 1)
            for i in range(8):
                done(act, ("UT", i))
                A(UT[:, 4 * i:4 * i + 4, :], bank(("UT", i)).rearrange("p (a b) -> p a b", a=4)[:, :, 0:NCH], ACT.Copy).then_inc(drained["UT"], 1)
            done(act, ("UT", 7))
            for hf in range(HALVES):
                for i in range(4):
                    done(act, ("G", 4 * hf + i))
                    if hf:
                        done(act, ("V", 3))
                    A(Gm[:, 2 * i:2 * i + 2, :, :].rearrange("p a r b -> p (a r b)"), bank(("G", 4 * hf + i)), ACT.Copy).then_inc(drained["G"], 1)
                fill(FILL[hf][0])
                for i in range(4):
                    done(act, ("V", 4 * hf + i))
                    dst = (Vr, Vi)[i % 2][:, 4 * (i // 2):4 * (i // 2) + 4, :].rearrange("p a b -> p (a b)")
                    act.wait_ge(S["w_ready"], hf + 1)
                    A(dst, bank(("V", 4 * hf + i))[:, 0:4 * NCH], ACT.Copy).then_inc(drained["V"], 1)
                fill(FILL[hf][1])
                for i in range(4):
                    done(act, ("Y", 4 * hf + i))
                    if hf:
                        done(act, ("YT", 3))
                    g2, q = i % 2, i // 2
                    dst = Yh.rearrange("p j (a g c) -> p a g j c", g=2, c=GC)[:, 4 * q:4 * q + 4, g2, :, :]
                    src = bank(("Y", 4 * hf + i)).rearrange("p (a j c) -> p a j c", a=4, c=GC)[0:NCH]
                    A(dst, src, ACT.Copy).then_inc(drained["Y"], 1)
                for i in range(4):
                    done(act, ("YT", 4 * hf + i))
                    src = bank(("YT", 4 * hf + i)).rearrange("p (a b) -> p a b", a=4)[:, :, 0:NCH]
                    dst = yT[:, 2 * hf + i // 2, :].rearrange("p (c j) -> p j c", j=L)[:, 4 * (i % 2):4 * (i % 2) + 4, :]
                    A(dst, src, ACT.Copy).then_inc(drained["YT"], 1)
            act.wait_ge(drained["YT"], 8)
            yf = at(R, 4 * T)
            gsq = at(R + 16384, 4 * T)
            A(gsq, yf, ACT.Square).then_inc(S["gelu_sq"], 1)
            act.wait_ge(S["gelu_arg"], 1)
            A(gsq, gsq, ACT.Tanh, scale=GELU_C).then_inc(S["gelu_th"], 1)
            fill(FILL[1][2])
            act.wait_ge(S["gelu_ready"], 1)
            for c in range(8):
                if c < 4:
                    src, key = bank(("gg", c)), ("gg", c)
                    done(act, key)
                    if c >= 2:
                        act.wait_ge(drained["gv"], c - 1)
                    A(glu_t[c % 2], src, ACT.Tanh, scale=0.25).then_inc(drained["gg"], 1)
                else:
                    key = ("gs", c - 4)
                    done(act, key)
                    act.wait_ge(*((drained["gv"], c - 1) if c < 6 else (drained["gs"], c - 5)))
                    A(glu_t[c % 2][:, 0:P], bank(key)[:, 0:P], ACT.Tanh, scale=0.25).then_inc(S["glu_th"], 1)

            def exp_unit(i, parts):
                act.wait_ge(S["row_max"], i + 1)
                if i >= 3:
                    turned(act, i - 3)
                for j, (key, n, c0) in enumerate(parts):
                    ins = A(Pb[i % 3][:, c0:c0 + n], bank(key)[:, 0:n], ACT.Exp, bias=smax[:, i % 4, 2:3],
                            accum_out=ssum[:, i % 4, j:j + 1])
                    if j < len(parts) - 1:
                        ins.then_inc(drained[key[0]], 1)
                ins.then_inc(drained[parts[-1][0][0]], 1)

            def turned(eng, i):
                n = len(PROMPT_UNITS)
                done(eng, ("PT", i) if i < n else ("sPb", i - n))

            def pt_out(kind, i, unit, tiles, first=0):
                done(act, (kind, i))
                if unit >= 4:
                    n = len(PROMPT_UNITS)
                    u = unit - 4
                    done(act, ("PV", u // 2) if u < n else ("sPV", u - n))
                src = bank((kind, i)).rearrange("p (a b) -> p a b", a=4)[:, 0:tiles, :]
                A(PT[unit % 4][:, first:first + tiles, :], src, ACT.Copy).then_inc(drained[kind], 1)

            n = len(PROMPT_UNITS)
            for i in range(n + 2):
                if i < n:
                    exp_unit(i, [(("S", i), P * (PROMPT_UNITS[i][0] + 1), 0)])
                if i >= 2:
                    pt_out("PT", i - 2, i - 2, PROMPT_UNITS[i - 2][0] + 1)
            for b in range(NB + 2):
                if b < NB:
                    exp_unit(n + b, [(("sA", b), 512, 0), (("sB", b), P, 512)])
                if 0 <= b - 1 < NB:
                    pt_out("sPa", b - 1, n + b - 1, 4)
                    pt_out("sPb", b - 1, n + b - 1, 1, first=4)
                if b >= 2:
                    done(act, ("sPV", b - 2))
                    if b >= 4:
                        done(act, ("sO", b - 4))
                    A(s_rows[b % 2], bank(("sPV", b - 2))[:, 0:P], ACT.Copy).then_inc(drained["sPV"], 1)
            for i in range(4):
                done(act, ("mkT", i))
                src = bank(("mkT", i)).rearrange("p (a b) -> p a b", a=4)
                A(mkT[:, 4 * (i % 2):4 * (i % 2) + 4, (i // 2) * P:(i // 2 + 1) * P], src, ACT.Copy).then_inc(drained["mkT"], 1)
            for t in range(NT):
                act.wait_ge(drained["oA"], 2 * t + 2)
                if t:
                    act.wait_ge(S["x1_squared"], t)
                A(at(R + 22528, D), xr[:, t, :], ACT.Square, accum_out=ss1[:, t:t + 1]).then_inc(S["x1_squared"], 1)
            act.wait_ge(S["rstd_1_ready"], 1)
            for i in range(10):
                done(act, ("mq", i))
                if i >= 2:
                    act.wait_ge(S["mq_normed"], i - 1)
                A(mraw[i % 2], bank(("mq", i)), ACT.Copy, scale=rstd_1[:, i // 2:i // 2 + 1]).then_inc(drained["mq"], 1)

            def mem_pt(i):
                done(act, ("mPT", i))
                n = len(MEM_UNITS)
                if i >= 4:
                    j = i - 4
                    done(act, ("mPV", j) if j < n else ("smPV", 2 * (j - n) + 1))
                A(mPT[i % 4], bank(("mPT", i)).rearrange("p (a b) -> p a b", a=4)[:, 0:2, :], ACT.Copy).then_inc(drained["mPT"], 1)

            n = len(MEM_UNITS)
            act.wait_ge(S["x1_squared"], NT)
            def mem_exp(i):
                act.wait_ge(S["mrow_max"], i + 1)
                if i >= 4:
                    done(act, ("mPT", i - 4))
                A(mP[i % 4], bank(("mS", i))[:, 0:NM], ACT.Exp, bias=smax[:, i % 4, 2:3],
                  accum_out=ssum[:, i % 4, 0:1]).then_inc(drained["mS"], 1)

            for i in range(n + 2):
                if i < n:
                    mem_exp(i)
                if i >= 2:
                    mem_pt(i - 2)
            act.wait_ge(S["v_stored"], 16)
            for i in range(6):
                if i < 4:
                    mem_exp(n + i)
                if 0 <= i - 1 < 4:
                    mem_pt(n + i - 1)
                if i >= 2:
                    if i >= 4:
                        done(act, ("smT", 2 * (i - 4) + 1))
                    for c in range(2):
                        done(act, ("smPV", 2 * (i - 2) + c))
                        A(sm_rows[i % 2][:, 512 * c:512 * c + 512], bank(("smPV", 2 * (i - 2) + c)), ACT.Copy).then_inc(drained["smPV"], 1)
            for t in range(NT):
                act.wait_ge(drained["mo"], 2 * t + 2)
                if t:
                    act.wait_ge(S["x2_squared"], t)
                A(at(R + 14336, D), xr[:, t, :], ACT.Square, accum_out=ss2[:, t:t + 1]).then_inc(S["x2_squared"], 1)
            act.wait_ge(S["rstd_2_ready"], 1)
            for t in range(NT):
                if t >= 2:
                    act.wait_ge(S[f"xn_stored{t % 2}"], 16 * (t // 2))
                A(xn[t % 2], xr[:, t, :], ACT.Copy, scale=rstd_2[:, t:t + 1]).then_inc(S["xn_ready"], 1)
            act.wait_ge(S["logits_ready"], 1)
            A(gsm[1], gsm[1], ACT.Exp).then_inc(S["choice_exp"], 1)
            act.wait_ge(S["logits_ready"], 2)
            A(rs_[4], rs_[4], ACT.Exp).then_inc(S["choice_exp"], 1)

            def TH(i, c):
                e = 4 * i + c
                act.wait_ge(moe["gu_done"], e + 1)
                if late(i, c, 2):
                    act.wait_ge(moe["h_ready"], e - 1)
                A(th_b[c % 2][:, :, 0:CAP], banks[:, 4 + c % 2, :].rearrange("p (a b) -> p a b", a=4)[:, 0:2, 0:CAP], ACT.Tanh,
                  scale=0.5).then_inc(moe["th_ready"], 1)

            def YE(i, c):
                e = 4 * i + c
                if late(i, c, 2):
                    act.wait_ge(moe[f"y_st{c % 2}"], 32 * i + 16 * (c // 2))
                for ch in range(2):
                    act.wait_ge(moe["dn_done"], 2 * e + ch + 1)
                    A(ye[c % 2][0:CAP, ch * 512:(ch + 1) * 512], banks[0:CAP, 6 + ch, :], ACT.Copy).then_inc(moe["ye_ready"], 1)

            TH(0, 0)
            for c in range(1, 5):
                TH(0, c)
                YE(0, c - 1)
            with act.Fori(1, 7) as i:
                for c in range(1, 5):
                    TH(i, c)
                    YE(i, c - 1)
            for c in range(29, 32):
                TH(0, c)
                YE(0, c - 1)
            YE(0, 31)
            nov = act.value_load(ov_regs[0:1, NOV:NOV + 1], min_val=0, max_val=NOV)
            act.wait_ge(moe["y_st0"], 16 * 16)
            with act.Fori(0, NOV) as v:
                with act.If(v < nov):
                    act.wait_ge(moe["gu_done"], NE + v + 1)
                    A(th_b[0][:, :, 0:CAP], banks[:, 4, :].rearrange("p (a b) -> p a b", a=4)[:, 0:2, 0:CAP], ACT.Tanh,
                      scale=0.5).then_inc(moe["th_ready"], 1)
                    act.wait_ge(moe["dn_done"], 2 * NE + v + 1)
                    act.wait_ge(moe["y_st0"], 16 * (NE // 2) + 16 * v)
                    A(ye[0][0:CAP, 0:512], banks[0:CAP, 6, :], ACT.Copy)
                    A(ye[0][0:CAP, 512:1024], banks[0:CAP, 7, :], ACT.Copy).then_inc(moe["ye_ready"], 1)

        @block.gpsimd
        def _(pool):
            n_chain = [0]
            g = nc.gpsimd

            def link(ins):
                n_chain[0] += 1
                ins.then_inc(pool_chain, 1)
                pool.wait_ge(pool_chain, n_chain[0])

            def rsqrt_mean(dst, src, n, count, signal, col=8):
                mean = tmp48[:, col:col + n]
                link(g.tensor_scalar(mean, src, 1.0 / count, EPS, ALU.mult, ALU.add))
                g.tensor_tensor(dst, mean, minus_half[:, 0:n], ALU.pow).then_inc(signal, 1)

            link(g.memset(minus_half, -0.5))
            link(g.memset(ident, 0.0))
            link(g.affine_select(out=ident, in_=ident, compare_op=ALU.not_equal, fill=1.0, base=0,
                                 pattern=[[-1, P]], channel_multiplier=1))
            link(g.memset(ones, 1.0))
            link(g.affine_select(out=tri, in_=ones, compare_op=ALU.is_gt, fill=0.0, base=0,
                                 pattern=[[1, P]], channel_multiplier=-1))
            link(g.iota(iota_slot, [[1, max(CAP, NU)]], base=0, channel_multiplier=0, allow_small_or_imprecise_dtypes=True))
            g.iota(tokid, [[P, NT]], base=0, channel_multiplier=1, allow_small_or_imprecise_dtypes=True).then_inc(S["consts_built"], 1)
            pool.wait_ge(S["x_squared"], NT)
            rsqrt_mean(rstd_x, ssx, NT, D, S["rstd_x_ready"])
            pool.wait_ge(S["rel_built"], 1)
            g.dma_start(e_dram.ap(), spread(rel_ext[0:NH, :].unsqueeze(1), [NH, P, 385])).then_inc(S["e_stored"], 16)
            for t in range(NT):
                pool.wait_ge(drained["u"], t + 1)
                g.dma_start(u_dram.ap()[t * P:(t + 1) * P, :], raw[t % 2]).then_inc(S[f"u_stored{t % 2}"], 16)

            pool.wait_ge(S["mem_squared"], 2)
            rsqrt_mean(rstd_m, ssm_, 2, D, S["rstd_m_ready"], col=40)

            def k_store(i):
                pool.wait_ge(S["qk_normed"], i + 1)
                g.dma_start(k_out[(i - 5) * P:(i - 4) * P, :], nrm[i % 2]).then_inc(S[f"k_stored{i % 2}"], 16)

            for i in range(10):
                pool.wait_ge(S["qk_stats"], i + 1)
                rsqrt_mean(qf[:, i % 4, :], qss[:, i % 4, :], NH, HD, S["qk_factor"])
                if i >= 6:
                    k_store(i - 1)
            k_store(9)
            pool.wait_ge(drained["v"], NT)
            g.dma_start(v_out.rearrange("(t p) d -> p t d", p=P), v_rows).then_inc(S["v_stored"], 16)
            for kind, dst in (("mk", mk_dram.ap()), ("mv", mv_out)):
                for i in range(4):
                    pool.wait_ge(drained[kind], i + 1)
                    c, t = i // 2, i % 2
                    g.dma_start(dst[t * P:(t + 1) * P, c * 512:(c + 1) * 512], m_stage[i % 2]).then_inc(S[f"m_stored{i % 2}"], 16)
            pool.wait_ge(S["state_ready"], 2)
            g.dma_start(s_out, fin).then_inc(S["s_stored"], 16)
            n = len(PROMPT_UNITS)
            for i in range(n + NB):
                w = P * (PROMPT_UNITS[i][0] + 1) if i < n else 640
                pool.wait_ge(S["p_normed"], i + 1)
                g.tensor_scalar(Pb[i % 3][:, 0:w], Pb[i % 3][:, 0:w], ssum[:, i % 4, 3:4], None, ALU.mult).then_inc(S["p_scaled"], 1)
            pool.wait_ge(S["mk_stats"], 1)
            rsqrt_mean(qf8, qss8, 8, MD, S["mk_factor"])
            pool.wait_ge(S["mk_normed"], 4)
            g.dma_start(mk_out.rearrange("(t p) d -> p t d", p=P), mk_rows).then_inc(S["mk_stored"], 16)
            done(pool, ("ss", 0))
            pool.wait_ge(drained["ss"], 1)
            rsqrt_mean(rstd_g, ssg, 2 * NT, AW, S["rstd_g_ready"])
            pool.wait_ge(S["x1_squared"], NT)
            rsqrt_mean(rstd_1, ss1, NT, D, S["rstd_1_ready"])
            for i in range(10):
                pool.wait_ge(S["mq_stats"], i + 1)
                rsqrt_mean(qf[:, i % 4, 0:2], qss[:, i % 4, 0:2], 2, MD, S["mq_factor"])
            link(g.memset(zeros, 0.0))
            for vv in range(NOV):
                rows = moe_dram.ap()[(NE + vv) * CAP:(NE + vv + 1) * CAP, :].rearrange("p (a d) -> p a d", d=512)
                g.dma_start(rows, spread(zeros[0:CAP].unsqueeze(1), [CAP, 2, 512])).then_inc(S["rows_zeroed"], 16)
            for i in range(n_mem_units):
                pool.wait_ge(S["mp_exp"], i + 1)
                g.tensor_scalar(mP[i % 4], mP[i % 4], ssum[:, i % 4, 3:4], None, ALU.mult).then_inc(S["mp_scaled"], 1)
            pool.wait_ge(S["x2_squared"], NT)
            rsqrt_mean(rstd_2, ss2, NT, D, S["rstd_2_ready"])
            for t in range(NT):
                pool.wait_ge(S["xn_ready"], t + 1)
                g.dma_start(xn_dram.ap()[t * P:(t + 1) * P, :], xn[t % 2]).then_inc(S[f"xn_stored{t % 2}"], 16)
            pool.wait_ge(S["xn_stored0"], 48)
            pool.wait_ge(S["xn_stored1"], 32)
            pool.wait_ge(drained["tab"], 1)

            def GA(i, c):
                e = 4 * i + c
                if c >= 2:
                    pool.wait_ge(moe["tx_done"], 2 * e - 2)
                col = tok_idx[0:CAP, bass.ds(e, 1)] if not isinstance(e, int) else tok_idx[0:CAP, e:e + 1]
                g.indirect_dma_start(xg[c % 2][0:CAP, :], None, xn_dram.ap(), bass.IndirectOffsetOnAxis(col, 0)).then_inc(moe[f"xg{c % 2}"], 16)

            GA(0, 0)
            GA(0, 1)
            for c in range(2, NE):
                GA(0, c)
            pool.wait_ge(S["rows_zeroed"], 16 * NOV)
            pool.wait_ge(S["slots_ready"], 1)
            nov = pool.value_load(ov_regs[0:1, NOV:NOV + 1], min_val=0, max_val=NOV)
            pool.wait_ge(moe["tx_done"], 2 * NE)
            for v in range(NOV):
                with pool.If(v < nov):
                    pool.wait_ge(moe["tx_done"], 2 * NE + 2 * v)
                    g.indirect_dma_start(xg[0][0:CAP, :], None, xn_dram.ap(),
                                         bass.IndirectOffsetOnAxis(tok_idx[0:CAP, NE + v:NE + v + 1], 0)).then_inc(moe["xg0"], 16)
                    pool.wait_ge(moe["y_st0"], 16 * (NE // 2) + 16 * v + 16)
            pool.wait_ge(moe["y_st0"], 16 * (NE // 2))
            pool.wait_ge(moe["y_st1"], 16 * (NE // 2))
            for t in range(NT):
                if t >= 2:
                    pool.wait_ge(moe["y_ready"], t - 1)
                for j in range(2):
                    g.indirect_dma_start(yg[2 * (t % 2) + j], None, moe_dram.ap(),
                                         bass.IndirectOffsetOnAxis(slot_idx[:, j * NT + t:j * NT + t + 1], 0)).then_inc(moe[f"yg_landed{t % 2}"], 16)

        @block.vector
        def _(dve):
            n_chain = [0]
            v = nc.vector

            def link(ins):
                n_chain[0] += 1
                ins.then_inc(dve_chain, 1)
                dve.wait_ge(dve_chain, n_chain[0])

            def tt(o, a, b, op):
                link(v.tensor_tensor(o, a, b, op))

            def cmul(or_, oi, ar, ai, br, bi, x, y, conj_b=False):
                tt(x, ar, br, ALU.mult)
                tt(y, ai, bi, ALU.mult)
                tt(or_, x, y, ALU.add if conj_b else ALU.subtract)
                tt(x, ai, br, ALU.mult)
                tt(y, ar, bi, ALU.mult)
                tt(oi, x, y, ALU.subtract if conj_b else ALU.add)

            dve.wait_ge(S["xT_landed"], 32)
            v.tensor_tensor(hT[:, :, 0:P], hT[:, :, 0:P], spread(norm_mix.unsqueeze(2), [P, KT, P]), ALU.mult).then_inc(S["hT_ready"], 1)
            dve.wait_ge(S["xT_rest_landed"], 16)
            for k in range(KT):
                ins = v.tensor_scalar(hT[:, k, P:T], hT[:, k, P:T], norm_mix[:, k:k + 1], None, ALU.mult)
            ins.then_inc(S["hT_ready"], 1)
            v.tensor_scalar(tmp48[:, 0:1], q_gain, float(HD) ** -0.5, None, ALU.mult).then_inc(S["hT_ready"], 1)

            lr, li = par[:, 0, :], par[:, 1, :]
            dve.wait_ge(S["ssm_landed"], 64)
            dve.wait_ge(act_ssm, 1)
            tt(sm[1], lr, sm[0], ALU.mult)
            tt(sm[2], li, sm[0], ALU.mult)
            link(v.tensor_scalar(sm[7], sm[2], float(1.0 / (2 * np.pi)), ROUND, ALU.mult, ALU.add))
            link(v.tensor_scalar(sm[7], sm[7], ROUND, None, ALU.subtract))
            link(v.scalar_tensor_tensor(sm[2], sm[7], -TWO_PI_HI, sm[2], ALU.mult, ALU.add))
            link(v.scalar_tensor_tensor(sm[2], sm[7], -TWO_PI_LO, sm[2], ALU.mult, ALU.add))
            v.tensor_scalar(sm[2], sm[2], 3.1415925, -3.1415925, ALU.min, ALU.max).then_inc(dve_ssm, 1)
            dve.wait_ge(act_ssm, 5)
            tt(sm[7], sm[5], sm[5], ALU.mult)
            link(v.tensor_scalar(sm[5], sm[7], -2.0, 1.0, ALU.mult, ALU.add))
            cosp, sinp, rad = sm[5], sm[4], sm[3]
            link(v.memset(Pw[0][:, :, 0], 1.0))
            link(v.memset(Pw[1][:, :, 0], 0.0))
            tt(Pw[0][:, :, 1], rad, cosp, ALU.mult)
            tt(Pw[1][:, :, 1], rad, sinp, ALU.mult)
            tt(sm[7], lr, lr, ALU.mult)
            tt(sm[8], li, li, ALU.mult)
            tt(sm[7], sm[7], sm[8], ALU.add)
            link(v.reciprocal(sm[7], sm[7]))
            link(v.tensor_scalar(sm[8], Pw[0][:, :, 1], -1.0, None, ALU.add))
            cmul(sm[9], sm[10], sm[8], Pw[1][:, :, 1], lr, li, sm[11], sm[12], conj_b=True)
            tt(sm[9], sm[9], sm[7], ALU.mult)
            tt(sm[10], sm[10], sm[7], ALU.mult)
            full = [P, GP, GC]
            Fr, Fi = (spread(sm[i].unsqueeze(2), full) for i in (9, 10))
            dve.wait_ge(S["x_squared"], NT)
            cmul(Bb[0], Bb[1], Fr, Fi, bc[:, 0], bc[:, 1], t1(GP, GC), t2(GP, GC))
            for lo, n in ((1, 1), (1, 2), (1, 4)):
                m = {1: 1, 2: 2, 4: 4}[n]
                pr_, pi_ = (spread(Pw[r][:, :, m:m + 1], [P, GP, n]) for r in range(2))
                cmul(Pw[0][:, :, m + 1:m + 1 + n], Pw[1][:, :, m + 1:m + 1 + n], Pw[0][:, :, 1:1 + n], Pw[1][:, :, 1:1 + n],
                     pr_, pi_, t1(GP, n), t2(GP, n))
            for r in range(2):
                for j in range(L):
                    ins = v.tensor_copy(Pv[r][:, :, j], Pw[r][:, :, L - 1 - j])
                link(ins)
            cur = (cosp, sinp)
            for a, b in ((7, 8), (9, 10), (7, 8)):
                cmul(sm[a], sm[b], cur[0], cur[1], cur[0], cur[1], sm[11], sm[12])
                cur = (sm[a], sm[b])
            e8 = cur

            dve.wait_ge(S["rel_landed"], 16)
            link(v.tensor_copy(rel_ext[0:NH, 0:P], spread(rel_ext[0:NH, P:P + 1], [NH, P])))
            link(v.tensor_copy(bias_far[0:NH, :], rel_ext[0:NH, 0:1]))
            v.tensor_scalar(rel_ext[0:NH, :], rel_ext[0:NH, :], bias_far[0:NH, :], None, ALU.subtract).then_inc(S["rel_built"], 1)

            def half_matrices(hf):
                s = slice(HP * hf, HP * hf + HP)
                sh = [P, HP, L, GC]
                br_, bi_ = (spread(Bb[r][:, s, :].unsqueeze(2), sh) for r in range(2))
                pr_, pi_ = (spread(Pv[r][:, s, :].unsqueeze(3), sh) for r in range(2))
                if hf:
                    done(dve, ("Y", 3))
                x, y = t1(HP, L, GC), t2(HP, L, GC)
                tt(x, br_, pr_, ALU.mult)
                tt(y, bi_, pi_, ALU.mult)
                tt(BL[0], x, y, ALU.subtract)
                tt(x, br_, pi_, ALU.mult)
                tt(y, bi_, pr_, ALU.mult)
                v.tensor_tensor(BL[1], x, y, ALU.add).then_inc(S["b_ready"], 1)
                dve.wait_ge(S["b_ready"], hf + 1)

            def half_outputs(hf):
                s = slice(HP * hf, HP * hf + HP)
                sh = [P, HP, L + 1, GC]
                cr_, ci_ = (spread(bc[:, 2 + r, s, :].unsqueeze(2), sh) for r in range(2))
                pr_, pi_ = (spread(Pw[r][:, s, :].unsqueeze(3), sh) for r in range(2))
                x, y = t1(HP, L + 1, GC), t2(HP, L + 1, GC)
                tt(x, cr_, pr_, ALU.mult)
                tt(y, ci_, pi_, ALU.mult)
                tt(Wm[0], x, y, ALU.subtract)
                tt(x, cr_, pi_, ALU.mult)
                tt(y, ci_, pr_, ALU.mult)
                xf, yf, wf = (a.rearrange("p a b c -> p (a b c)") for a in (x, y, Wm[1]))
                link(v.scalar_tensor_tensor(wf, xf, -1.0, yf, ALU.mult, ALU.subtract))
                x, y = t1(HP, 32), t2(HP, 32)
                link(v.tensor_copy(Tr[:, :, 0], e8[0][:, s]))
                link(v.tensor_copy(Ti[:, :, 0], e8[1][:, s]))
                n = 1
                while n < PCH:
                    a_, b_ = (spread(q[:, :, n - 1:n], [P, HP, n]) for q in (Tr, Ti))
                    cmul(Tr[:, :, n:2 * n], Ti[:, :, n:2 * n], Tr[:, :, 0:n], Ti[:, :, 0:n], a_, b_, x[:, :, 0:n], y[:, :, 0:n])
                    n *= 2
                link(v.tensor_copy(rho_t, spread(sm[6][:, s].unsqueeze(2), [P, HP, PCH])))
                v.memset(rho_t[:, :, 0], 0.0).then_inc(S["w_ready"], 1)
                dve.wait_ge(S["w_ready"], hf + 1)

            def kernels(hf):
                for i in range(4):
                    key = ("K", 4 * hf + i)
                    done(dve, key)
                    kp = Kpad[i % 2]
                    if 4 * hf + i >= 2:
                        dve.wait_ge(S[f"kt_landed{i % 2}"], 16 * 8 * (2 * hf + i // 2))
                    ps = bank(key).rearrange("p (a b) -> p a b", a=4)
                    v.tensor_copy(kp[:, :, P:2 * P], ps[0:GC]).then_inc(drained["K"], 1)
                    dve.wait_ge(drained["K"], 4 * hf + i + 1)
                    gs = HP * hf + 4 * (i // 2)
                    dd = d_tmp[0:GC].rearrange("p (a c) -> p a c", c=GC)
                    dg = dskip.rearrange("p (a g) -> p a g", g=2)[:, gs:gs + 4, i % 2]
                    tt(dd, spread(ident[0:GC, 0:GC].unsqueeze(1), [GC, 4, GC]), spread(dg.unsqueeze(2), [GC, 4, GC]), ALU.mult)
                    v.tensor_tensor(kp[:, :, P:P + GC], kp[:, :, P:P + GC], dd, ALU.add).then_inc(S["kpad_ready"], 1)

            def states(hf):
                s = slice(HP * hf, HP * hf + HP)
                dve.wait_ge(drained["V"], 4 * hf + 4)
                vp = [q[:, :, 0:PCH] for q in (Vr, Vi)]
                x, y = wr, wi
                z = at(R + 13568, HP, PCH)
                zz = at(R + 14080, HP, PCH)
                dve.wait_ge(S["kt_landed0"], 16 * 8 * 2 * (hf + 1))
                dve.wait_ge(S["kt_landed1"], 16 * 8 * 2 * (hf + 1))
                cmul(z, zz, vp[0], vp[1], Tr, Ti, x, y, conj_b=True)
                flat = lambda q: q.rearrange("p a b -> p (a b)")
                link(v.tensor_tensor_scan(flat(wr), flat(rho_t), flat(z), 0.0, ALU.mult, ALU.add))
                link(v.tensor_tensor_scan(flat(wi), flat(rho_t), flat(zz), 0.0, ALU.mult, ALU.add))
                tt(z, wr, Tr, ALU.mult)
                tt(zz, wi, Ti, ALU.mult)
                if hf:
                    done(dve, ("Y", 3))
                tt(Sr[:, :, 1:PCH], z[:, :, 0:PCH - 1], zz[:, :, 0:PCH - 1], ALU.subtract)
                tt(fin[:, 0, s, 0:1], z[:, :, PCH - 1:PCH], zz[:, :, PCH - 1:PCH], ALU.subtract)
                tt(z, wr, Ti, ALU.mult)
                tt(zz, wi, Tr, ALU.mult)
                tt(Si[:, :, 1:PCH], z[:, :, 0:PCH - 1], zz[:, :, 0:PCH - 1], ALU.add)
                tt(fin[:, 1, s, 0:1], z[:, :, PCH - 1:PCH], zz[:, :, PCH - 1:PCH], ALU.add)
                link(v.memset(Sr[:, :, 0:1], 0.0))
                link(v.memset(Si[:, :, 0:1], 0.0))
                SS = [q[:, :, PCH:NCH].rearrange("p a (b c) -> p a b c", c=2) for q in (Sr, Si)]
                VV = [q[:, :, PCH:NCH].rearrange("p a (b c) -> p a b c", c=2) for q in (Vr, Vi)]
                sh = [P, HP, NB]
                ar_, ai_ = (spread(Pw[r][:, s, L:L + 1], sh) for r in range(2))
                x, y = wr[:, :, 0:NB], wi[:, :, 0:NB]
                zr, zi = z[:, :, 0:NB], zz[:, :, 0:NB]
                link(v.tensor_copy(SS[0][:, :, :, 0], s0[:, 0, s, :]))
                link(v.tensor_copy(SS[1][:, :, :, 0], s0[:, 1, s, :]))
                cmul(zr, zi, s0[:, 0, s, :], s0[:, 1, s, :], ar_, ai_, x, y)
                tt(SS[0][:, :, :, 1], zr, VV[0][:, :, :, 0], ALU.add)
                tt(SS[1][:, :, :, 1], zi, VV[1][:, :, :, 0], ALU.add)
                cmul(zr, zi, SS[0][:, :, :, 1], SS[1][:, :, :, 1], ar_, ai_, x, y)
                tt(fin[:, 0, s, 1:NB + 1], zr, VV[0][:, :, :, 1], ALU.add)
                link(v.tensor_tensor(fin[:, 1, s, 1:NB + 1], zi, VV[1][:, :, :, 1], ALU.add))
                link(v.memset(Kpad[0][:, :, 0:P], 0.0))
                v.memset(Kpad[1][:, :, 0:P], 0.0).then_inc(S["state_ready"], 1)
                dve.wait_ge(S["state_ready"], hf + 1)

            def norm_rows(src, dst, ss_ap, f_ap, heads, hd, stats, factor, count, gain, signal, n):
                sh = [P, heads, hd]
                s3 = src.rearrange("p (h d) -> p h d", h=heads)
                d3 = dst.rearrange("p (h d) -> p h d", h=heads)
                tt(dst, src, src, ALU.mult)
                v.tensor_reduce(ss_ap, d3, AXX, ALU.add).then_inc(stats, 1)
                dve.wait_ge(factor, count)
                fb = spread(f_ap.unsqueeze(2), sh)
                if gain is None:
                    v.tensor_tensor(d3, s3, fb, ALU.mult).then_inc(signal, 1)
                else:
                    tt(d3, s3, fb, ALU.mult)
                    v.tensor_tensor(d3, d3, spread(gain.unsqueeze(1), sh), ALU.mult).then_inc(signal, 1)

            dve.wait_ge(S["consts_built"], 1)
            dve.wait_ge(S["mem_squared"], 2)
            link(v.memset(Kpad[0][:, :, 0:P], 0.0))
            link(v.memset(Kpad[1][:, :, 0:P], 0.0))
            half_matrices(0)
            dve.wait_ge(S["consts_landed"], 16 * 4)
            for i in range(10):
                dve.wait_ge(drained["qk"], i + 1)
                if i >= 2:
                    done(dve, ("qkT", i - 2))
                if i >= 7:
                    dve.wait_ge(S[f"k_stored{i % 2}"], 16 * ((i - 5) // 2))
                norm_rows(raw[i % 2], nrm[i % 2], qss[:, i % 4, :], qf[:, i % 4, :], NH, HD, S["qk_stats"], S["qk_factor"],
                          i + 1, kg if i >= 5 else None, S["qk_normed"], i)
            half_outputs(0)
            dve.wait_ge(S["memT_landed"], 16)
            for k in range(KT):
                ins = v.tensor_scalar(memT[:, k, :], memT[:, k, :], mem_in_norm[:, k:k + 1], None, ALU.mult)
            ins.then_inc(S["memT_ready"], 1)
            dve.wait_ge(S["bias_landed"], 16 * NH)
            link(v.memset(bias_new, NEG))
            v.tensor_copy(bias_new[:, 112:128], bias_s[:, 128:144]).then_inc(S["bias_built"], 1)
            kernels(0)
            states(0)
            half_matrices(1)
            half_outputs(1)
            kernels(1)
            states(1)
            dve.wait_ge(S["state_ready"], 2)
            done(dve, ("Y", 7))
            yf = at(R, 4 * T)
            gsq = at(R + 16384, 4 * T)
            dve.wait_ge(S["gelu_sq"], 1)
            link(v.tensor_scalar(gsq, gsq, 0.044715, 1.0, ALU.mult, ALU.add))
            v.tensor_tensor(gsq, gsq, yf, ALU.mult).then_inc(S["gelu_arg"], 1)
            dve.wait_ge(S["gelu_th"], 1)
            v.scalar_tensor_tensor(yf, gsq, 1.0, yf, ALU.add, ALU.mult).then_inc(S["gelu_ready"], 1)
            for c in range(4):
                dve.wait_ge(drained["gg"], c + 1)
                done(dve, ("gv", c))
                v.scalar_tensor_tensor(ysT[:, c, 0:TP], glu_t[c % 2], 1.0, bank(("gv", c)), ALU.add, ALU.mult).then_inc(drained["gv"], 1)
            for c in range(4):
                dve.wait_ge(S["glu_th"], c + 1)
                v.scalar_tensor_tensor(ysT[:, c, TP:T], glu_t[c % 2][:, 0:P], 1.0, bank(("gs", c))[:, P:2 * P],
                                       ALU.add, ALU.mult).then_inc(drained["gs"], 1)
            link(v.memset(qblk, 0.0))
            for a in range(NPAIR):
                for h2 in range(2):
                    lo = HD * h2
                    c0 = (2 * a + h2) * SQ
                    ins = v.tensor_copy(qblk[lo:lo + HD, :, a, c0:c0 + SQ],
                                        qT[lo:lo + HD, a, TP:T].rearrange("p (b s) -> p b s", s=SQ))
            ins.then_inc(S["qblk_ready"], 1)
            dve.wait_ge(S["bias_p_landed"], 16)
            link(v.memset(bias_p[0:CH, :, P + CH:2 * P], NEG))

            def soft_in(i, parts, signal):
                for j, (key, n, b, c0) in enumerate(parts):
                    done(dve, key)
                    ps = bank(key)
                    if b is not None:
                        w = b.shape[-1]
                        link(v.tensor_tensor(ps[:, c0:c0 + w], ps[:, c0:c0 + w], b, ALU.add))
                    if i >= 4 and j == 0 and not mem[0]:
                        dve.wait_ge(S["p_scaled"], i - 3)
                    link(v.tensor_reduce(smax[:, i % 4, j:j + 1], ps[:, 0:n], AXX, ALU.max))
                src = smax[:, i % 4, 0:1]
                if len(parts) == 2:
                    tt(smax[:, i % 4, 0:1], smax[:, i % 4, 0:1], smax[:, i % 4, 1:2], ALU.max)
                v.tensor_scalar(smax[:, i % 4, 2:3], src, -1.0, None, ALU.mult).then_inc(signal, 1)

            def soft_out(i, kinds, two, signal):
                for kind, c in kinds:
                    dve.wait_ge(drained[kind], c)
                src = ssum[:, i % 4, 0:1]
                if two:
                    tt(src, src, ssum[:, i % 4, 1:2], ALU.add)
                v.reciprocal(ssum[:, i % 4, 3:4], src).then_inc(signal, 1)

            mem = [False]
            n = len(PROMPT_UNITS)

            def attn_in(i):
                if i < n:
                    t, h = PROMPT_UNITS[i]
                    b = bias_p[:, h, :] if t else bias_p[:, h, P:2 * P]
                    soft_in(i, [(("S", i), P * (t + 1), b, P * max(t - 1, 0))], S["row_max"])
                else:
                    b = i - n
                    soft_in(i, [(("sA", b), 512, bias_s[:, 0:P], 384),
                                (("sB", b), P, bias_new[:, 112 - SQ * b:240 - SQ * b], 0)], S["row_max"])

            def attn_out(i):
                if i < n:
                    soft_out(i, [("S", i + 1)], False, S["p_normed"])
                else:
                    soft_out(i, [("sA", i - n + 1), ("sB", i - n + 1)], True, S["p_normed"])

            def pv_out(m):
                t, h = PROMPT_UNITS[2 * m]
                done(dve, ("PV", m))
                v.tensor_copy(yaT[:, h // 2, t * P:(t + 1) * P], bank(("PV", m))[:, 0:P]).then_inc(drained["PV"], 1)

            def spv_out(b):
                done(dve, ("sO", b))
                ps = bank(("sO", b))[:, 0:P].rearrange("p (a s) -> p a s", s=SQ)
                for h2 in range(2):
                    lo = HD * h2
                    ins = v.tensor_copy(yaT[lo:lo + HD, :, TP + SQ * b:TP + SQ * b + SQ], ps[lo:lo + HD, h2:8:2, :])
                ins.then_inc(drained["sO"], 1)

            for i in range(n):
                attn_in(i)
                if i >= 1:
                    attn_out(i - 1)
                if i >= 5 and i % 2:
                    pv_out((i - 5) // 2)
            attn_out(n - 1)
            pv_out(n // 2 - 2)
            pv_out(n // 2 - 1)
            for b in range(NB):
                if b >= 1:
                    attn_out(n + b - 1)
                attn_in(n + b)
                if b >= 3:
                    spv_out(b - 3)
            attn_out(n + NB - 1)
            for b in range(NB - 3, NB):
                spv_out(b)

            dve.wait_ge(S["mem_landed"], 48)
            for t in range(2):
                tt(at(R + 22528, D), mk_rows[:, t, :], mk_rows[:, t, :], ALU.mult)
                ins = v.tensor_reduce(qss8[:, 4 * t:4 * t + 4], at(R + 22528, MH, MD), AXX, ALU.add)
                if t == 0:
                    link(ins)
            ins.then_inc(S["mk_stats"], 1)
            dve.wait_ge(S["mk_factor"], 1)
            for i in range(4):
                seg = mk_rows[:, i // 2, (i % 2) * 512:(i % 2 + 1) * 512].rearrange("p (h d) -> p h d", h=2)
                f = qf8[:, 4 * (i // 2) + 2 * (i % 2):4 * (i // 2) + 2 * (i % 2) + 2]
                tt(seg, seg, spread(f.unsqueeze(2), [P, 2, MD]), ALU.mult)
                v.tensor_tensor(seg, seg, spread(mkg.unsqueeze(1), [P, 2, MD]), ALU.mult).then_inc(S["mk_normed"], 1)
            for br, y in enumerate((ysT, yaT)):
                for k in range(4):
                    i = 4 * br + k
                    if i >= 2:
                        dve.wait_ge(S["sq_used"], i - 1)
                    v.tensor_tensor(sq_t[:, i % 2, :], y[:, k, :], y[:, k, :], ALU.mult).then_inc(S["sq_ready"], 1)
            done(dve, ("ss", 0))
            for br in range(2):
                ps = bank(("ss", 0))[:, 0:8 * NT].rearrange("p (r k t) -> p r t k", r=2, k=4)[:, br]
                ins = v.tensor_reduce(ssg[:, br * NT:(br + 1) * NT], ps, AXX, ALU.add)
            link(ins)
            v.tensor_scalar(ssg[:, 0:NT], ssg[:, 0:NT], 1.0 / 16, None, ALU.mult).then_inc(drained["ss"], 1)
            link(v.tensor_scalar(out_ssm, out_ssm, 0.25, None, ALU.mult))
            for y, gain in ((ysT, out_ssm), (yaT, out_att)):
                for k in range(4):
                    ins = v.tensor_scalar(y[:, k, :], y[:, k, :], gain[:, k:k + 1], None, ALU.mult)
                ins.then_inc(S["branch_scaled"], 1)
            dve.wait_ge(S["rstd_g_ready"], 1)
            dve.wait_ge(S["xr_landed"], 16)

            def turn_out(kind, i, gain):
                t, hh = i // 2, i % 2
                done(dve, (kind, i))
                v.tensor_tensor(hT[:, 4 * hh:4 * hh + 4, t * P:(t + 1) * P], bank((kind, i)).rearrange("p (a b) -> p a b", a=4),
                                spread(gain[:, 4 * hh:4 * hh + 4].unsqueeze(2), [P, 4, P]), ALU.mult).then_inc(drained[kind], 1)

            for t in range(NT):
                for c in range(2):
                    i = 2 * t + c
                    x = xr[:, t, c * 512:(c + 1) * 512]
                    done(dve, ("oS", i))
                    v.scalar_tensor_tensor(x, bank(("oS", i)), rstd_g[:, t:t + 1], x, ALU.mult, ALU.add).then_inc(drained["oS"], 1)
                    dve.wait_ge(drained["oS"], i + 1)
                    done(dve, ("oA", i))
                    v.scalar_tensor_tensor(x, bank(("oA", i)), rstd_g[:, NT + t:NT + t + 1], x, ALU.mult, ALU.add).then_inc(drained["oA"], 1)
                if t >= 1:
                    turn_out("x1T", 2 * t - 2, norm_mem)
                    turn_out("x1T", 2 * t - 1, norm_mem)
            turn_out("x1T", 8, norm_mem)
            turn_out("x1T", 9, norm_mem)
            link(v.tensor_scalar(mq_gain4[:, 0:2], mq_gain, float(MD) ** -0.5, None, ALU.mult))
            link(v.tensor_scalar(mq_gain4[:, 2:4], mq_gain, float(MD) ** -0.5, None, ALU.mult))

            def mqT_out(j):
                done(dve, ("mqT", j))
                v.tensor_tensor(qm[:, 4 * (j % 2):4 * (j % 2) + 4, (j // 2) * P:(j // 2 + 1) * P],
                                bank(("mqT", j)).rearrange("p (a b) -> p a b", a=4),
                                spread(mq_gain4.unsqueeze(2), [P, 4, P]), ALU.mult).then_inc(drained["mqT"], 1)

            for i in range(10):
                dve.wait_ge(drained["mq"], i + 1)
                if i >= 2:
                    done(dve, ("mqT", i - 2))
                norm_rows(mraw[i % 2], mnrm[i % 2], qss[:, i % 4, 0:2], qf[:, i % 4, 0:2], 2, MD, S["mq_stats"], S["mq_factor"],
                          i + 1, None, S["mq_normed"], i)
                if i >= 2:
                    mqT_out(i - 2)
            mqT_out(8)
            mqT_out(9)
            done(dve, ("oA", 9))
            link(v.memset(qblk2, 0.0))
            for h in range(MH):
                for k in range(2):
                    ins = v.tensor_copy(qblk2[:, :, 2 * h + k, h * SQ:(h + 1) * SQ],
                                        qm[:, 2 * h + k, TP:T].rearrange("p (b s) -> p b s", s=SQ))
            ins.then_inc(S["qblk2_ready"], 1)
            mem[0] = True
            n = len(MEM_UNITS)

            def mem_out(i):
                soft_out(i, [("mS", i + 1)], False, S["mp_exp"])

            def mpv_out(j):
                t, h = MEM_UNITS[j]
                done(dve, ("mPV", j))
                v.tensor_copy(oT[:, 2 * h:2 * h + 2, t * P:(t + 1) * P],
                              bank(("mPV", j)).rearrange("p (a b) -> p a b", a=4)[:, 0:2, :]).then_inc(drained["mPV"], 1)

            def smt_out(i):
                for c in range(2):
                    done(dve, ("smT", 2 * i + c))
                    ps = bank(("smT", 2 * i + c)).rearrange("p (a b h s) -> p a b h s", a=4, b=2, s=SQ)
                    for q in range(2):
                        dst = oT[:, 4 * c + 2 * q:4 * c + 2 * q + 2, TP + 2 * SQ * i:TP + 2 * SQ * (i + 1)]
                        ins = v.tensor_copy(dst.rearrange("p a (b s) -> p a b s", s=SQ), ps[:, 2 * q:2 * q + 2, :, 2 * c + q, :])
                    ins.then_inc(drained["smT"], 1)

            def mem_in(i):
                if i >= 4:
                    dve.wait_ge(S["mp_scaled"], i - 3)
                soft_in(i, [(("mS", i), NM, None, 0)], S["mrow_max"])

            for i in range(n):
                mem_in(i)
                if i >= 1:
                    mem_out(i - 1)
                if i >= 3:
                    mpv_out(i - 3)
            mem_out(n - 1)
            for j in range(n - 3, n):
                mpv_out(j)
            for i in range(7):
                if 1 <= i < 5:
                    mem_out(n + i - 1)
                if i < 4:
                    mem_in(n + i)
                if i >= 3:
                    smt_out(i - 3)
            for t in range(NT):
                for c in range(2):
                    i = 2 * t + c
                    x = xr[:, t, c * 512:(c + 1) * 512]
                    done(dve, ("mo", i))
                    v.tensor_tensor(x, bank(("mo", i)), x, ALU.add).then_inc(drained["mo"], 1)
                if t >= 1:
                    turn_out("x2T", 2 * t - 2, norm_ffn)
                    turn_out("x2T", 2 * t - 1, norm_ffn)
            turn_out("x2T", 8, norm_ffn)
            turn_out("x2T", 9, norm_ffn)

            dve.wait_ge(S["rstd_2_ready"], 1)
            for t in range(NT):
                done(dve, ("rt", t))
                v.scalar_tensor_tensor(logit[:, t, :], bank(("rt", t))[:, 0:NG + NE], rstd_2[:, t:t + 1], rb, ALU.mult, ALU.add).then_inc(drained["rt"], 1)
            dve.wait_ge(drained["rt"], NT)
            lg, le = logit[:, :, 0:NG], logit[:, :, NG:NG + NE]
            gmax, gidx, p1, v1, dv = rs_
            idx, ta, tb, blk, unit = rs2_
            i1, i2, v2 = idx[:, 0], idx[:, 1], ta[:, 0]
            sg, se = [P, NT, NG], [P, NT, NE]
            link(v.tensor_reduce(gmax, lg, AXX, ALU.max))
            v.tensor_tensor(gsm[1], lg, spread(gmax.unsqueeze(2), sg), ALU.subtract).then_inc(S["logits_ready"], 1)

            def first(mask, idx, iota, n, shape, onehot, scratch):
                link(v.scalar_tensor_tensor(scratch, mask, -64.0, spread(iota.unsqueeze(1), shape), ALU.mult, ALU.add))
                link(v.tensor_reduce(idx, scratch, AXX, ALU.min))
                link(v.tensor_scalar(idx, idx, 64.0, None, ALU.add))
                tt(onehot, spread(iota.unsqueeze(1), shape), spread(idx.unsqueeze(2), shape), ALU.is_equal)

            tt(gsm[0], lg, spread(gmax.unsqueeze(2), sg), ALU.is_equal)
            first(gsm[0], gidx, iota4, NG, sg, gsm[0], gsm[2])
            link(v.tensor_scalar(gsm[2], gsm[0], -NEG, NEG, ALU.mult, ALU.add))
            s4 = [P, NT, NG, EPG]
            l4, le4 = lsel.rearrange("p t (g e) -> p t g e", g=NG), logit[:, :, NG:NG + NE].rearrange("p t (g e) -> p t g e", g=NG)
            tt(l4, le4, spread(gsm[0].unsqueeze(3), s4), ALU.mult)
            tt(l4, l4, spread(gsm[2].unsqueeze(3), s4), ALU.add)
            link(v.tensor_reduce(v1, lsel, AXX, ALU.max))
            tt(oh1, lsel, spread(v1.unsqueeze(2), se), ALU.is_equal)
            first(oh1, i1, iota32, NE, se, oh1, rtmp[:, 0])
            link(v.scalar_tensor_tensor(lsel, oh1, 3 * NEG, lsel, ALU.mult, ALU.add))
            link(v.tensor_reduce(v2, lsel, AXX, ALU.max))
            tt(oh2, lsel, spread(v2.unsqueeze(2), se), ALU.is_equal)
            first(oh2, i2, iota32, NE, se, oh2, rtmp[:, 0])
            v.tensor_tensor(chosen, oh1, oh2, ALU.add).then_inc(S["choice_ready"], 1)
            v.tensor_tensor(dv, v2, v1, ALU.subtract).then_inc(S["logits_ready"], 1)
            dve.wait_ge(S["choice_exp"], 2)
            link(v.tensor_reduce(p1, gsm[1], AXX, ALU.add))
            link(v.scalar_tensor_tensor(p1, dv, 1.0, p1, ALU.add, ALU.mult))
            link(v.reciprocal(w12[:, 0, :], p1))
            tt(w12[:, 1, :], w12[:, 0, :], dv, ALU.mult)
            done(dve, ("rank", 0))
            v.tensor_copy(rank_sb.rearrange("p a b -> p (a b)"), bank(("rank", 0))[:, 0:(NT + 1) * NE]).then_inc(drained["rank"], 1)
            dve.wait_ge(drained["rank"], 1)
            total = rank_sb[:, NT, :]
            link(v.memset(extra, 0.0))
            for k in range(1, NBLK):
                link(v.scalar_tensor_tensor(extra, total, float(CAP * k), extra, ALU.is_gt, ALU.add))
            link(v.tensor_tensor_scan(incl, ones[:, 0:NE], extra, 0.0, ALU.mult, ALU.add))
            tt(ovb, incl, extra, ALU.subtract)
            sr = [P, 2, NT, NE]
            tt(rtmp, oh, spread(rank_sb[:, 0:NT, :].unsqueeze(1), sr), ALU.mult)
            link(v.tensor_reduce(ta, rtmp, AXX, ALU.add))
            tt(rtmp.rearrange("p a b c -> p (a b) c"), oh.rearrange("p a b c -> p (a b) c"),
               spread(ovb.unsqueeze(1), [P, 2 * NT, NE]), ALU.mult)
            link(v.tensor_reduce(tb, rtmp, AXX, ALU.add))
            link(v.tensor_scalar(blk, ta, float(CAP), None, ALU.is_ge))
            for k in range(2, NBLK):
                link(v.scalar_tensor_tensor(blk, ta, float(CAP * k), blk, ALU.is_ge, ALU.add))
            link(v.scalar_tensor_tensor(ta, blk, -float(CAP), ta, ALU.mult, ALU.add))
            link(v.scalar_tensor_tensor(tb, blk, float(NE - 1), tb, ALU.add, ALU.add))
            tt(unit, idx, tb, ALU.subtract)
            link(v.scalar_tensor_tensor(unit, blk, 0.0, unit, ALU.is_equal, ALU.mult))
            tt(unit, unit, tb, ALU.add)
            done(dve, ("mo", 9))
            n2 = 2 * NT
            flat2 = lambda a: a.rearrange("p a b -> p (a b)")
            unit3, slot3 = (spread(flat2(a).unsqueeze(2), [P, n2, n]) for a, n in ((unit, NU), (ta, CAP)))
            ut3, sh3 = (a.rearrange("p a b c -> p (a b) c") for a in (unit_tok, slot_hot))
            tt(ut3, spread(iota_slot[:, 0:NU].unsqueeze(1), [P, n2, NU]), unit3, ALU.is_equal)
            link(v.tensor_tensor(sh3, spread(iota_slot[:, 0:CAP].unsqueeze(1), [P, n2, CAP]), slot3, ALU.is_equal))
            for j in range(2):
                ins = v.tensor_tensor(unit_tok[:, j], unit_tok[:, j], spread(tokid.unsqueeze(2), [P, NT, NU]), ALU.mult)
            ins.then_inc(S["table_parts_ready"], 1)
            link(v.scalar_tensor_tensor(slot_f, unit, float(CAP), ta, ALU.mult, ALU.add))
            done(dve, ("tab", 0))
            v.tensor_copy(tok_idx[0:CAP, :], bank(("tab", 0))[0:CAP, 0:NU]).then_inc(drained["tab"], 1)
            link(v.tensor_copy(ovt[:, :, :], spread(incl.unsqueeze(1), [P, NOV, NE])))
            tt(ovt, ovt, spread(iota_slot[:, 0:NOV].unsqueeze(2), [P, NOV, NE]), ALU.is_le)
            link(v.tensor_reduce(ovf[:, 0:NOV], ovt, AXX, ALU.add))
            link(v.tensor_scalar(ovf[:, 0:NOV], ovf[:, 0:NOV], float(NE - 1), None, ALU.min))
            link(v.tensor_copy(ovf[:, NOV:NOV + 1], incl[:, NE - 1:NE]))
            link(v.tensor_copy(ov_regs[:, :], ovf))
            v.tensor_copy(slot_idx[:, :], slot_f.rearrange("p a b -> p (a b)")).then_inc(S["slots_ready"], 1)

            def xg_out(src, dst, xi):
                return v.tensor_tensor(dst[:, 4 * xi:4 * xi + 4, 0:CAP], src.rearrange("p (a b) -> p a b", a=4)[:, :, 0:CAP],
                                       spread(norm_ffn[:, 4 * xi:4 * xi + 4].unsqueeze(2), [P, 4, CAP]), ALU.mult)

            def gated(ps, th, hb, a_done):
                b4 = ps.rearrange("p (a b) -> p a b", a=4)
                v.scalar_tensor_tensor(a_b[:, :, 0:CAP], th[:, :, 0:CAP], 1.0, b4[:, 0:2, 0:CAP], ALU.add, ALU.mult).then_inc(moe_a, 1)
                dve.wait_ge(moe_a, a_done)
                return v.scalar_tensor_tensor(hb[:, :, 0:CAP], a_b[:, :, 0:CAP], 0.5, b4[:, 2:4, 0:CAP], ALU.mult, ALU.mult)

            def XT(i, c):
                e = 4 * i + c
                if late(i, c, 2):
                    dve.wait_ge(moe["gu_done"], e - 1)
                for xi in range(2):
                    dve.wait_ge(moe["tx_done"], 2 * e + xi + 1)
                    xg_out(banks[:, 2 * (c % 2) + xi, :], xgT[c % 2], xi).then_inc(moe["xgT_ready"], 1)

            def H(i, c):
                e = 4 * i + c
                dve.wait_ge(moe["th_ready"], e + 1)
                if late(i, c, 2):
                    dve.wait_ge(moe["dn_done"], 2 * e - 2)
                if late(i, c, 1):
                    dve.wait_ge(moe["h_ready"], e)
                gated(banks[:, 4 + c % 2, :], th_b[c % 2], h_b[c % 2], e + 1).then_inc(moe["h_ready"], 1)

            XT(0, 0)
            XT(0, 1)
            H(0, 0)
            for c in range(1, 5):
                XT(0, c + 1)
                H(0, c)
            with dve.Fori(1, 7) as i:
                for c in range(1, 5):
                    XT(i, c + 1)
                    H(i, c)
            for c in range(29, 32):
                if c < 31:
                    XT(0, c + 1)
                H(0, c)
            nov = dve.value_load(ov_regs[0:1, NOV:NOV + 1], min_val=0, max_val=NOV)
            dve.wait_ge(moe["dn_done"], 2 * NE)
            with dve.Fori(0, NOV) as vv:
                with dve.If(vv < nov):
                    dve.wait_ge(moe["tx_done"], 2 * NE + 2 * vv + 2)
                    xg_out(banks[:, 0, :], xgT[0], 0).then_inc(moe["xgT_ready"], 1)
                    xg_out(banks[:, 1, :], xgT[0], 1).then_inc(moe["xgT_ready"], 1)
                    dve.wait_ge(moe["th_ready"], NE + vv + 1)
                    dve.wait_ge(moe["h_ready"], NE + vv)
                    gated(banks[:, 4, :], th_b[0], h_b[0], vv + NE + 1).then_inc(moe["h_ready"], 1)
            for t in range(NT):
                dve.wait_ge(moe[f"yg_landed{t % 2}"], 32 * (t // 2 + 1))
                a, b = yg[2 * (t % 2)], yg[2 * (t % 2) + 1]
                link(v.scalar_tensor_tensor(xr[:, t, :], a, w12[:, 0, t:t + 1], xr[:, t, :], ALU.mult, ALU.add))
                v.scalar_tensor_tensor(xr[:, t, :], b, w12[:, 1, t:t + 1], xr[:, t, :], ALU.mult, ALU.add).then_inc(moe["y_ready"], 1)


_INS = ["x_t", "x_rows", "mem_t", "mem_rows", "dense_w", "exp_gu", "exp_dn", "ck_t", "cv", "cmk_t", "cmv", "cols", "k_gain",
        "mk_gain", "router_w", "router_b", "ssm_small", "ssm_bc", "ssm_d", "ssm_s0", "rel_rev"]
_OUTS = [("y", (T, D)), ("k", (T, AW)), ("v", (T, AW)), ("mk", (NM, D)), ("mv", (NM, D)), ("s", (P, 2, GP, NB + 1))]


def kernel(**inputs):
    import concourse.bacc as bacc
    from concourse.bass_utils import run_bass_kernel_spmd

    w = {k: np.asarray(a) for k, a in inputs.items()}

    def tiles(a, n):
        return a.reshape(-1, P, n).transpose(1, 0, 2)

    def col(a):
        return a.reshape(-1, P).T

    x = np.concatenate([w["x_prompt"].reshape(TP, D), w["x_sample"].reshape(TS, D)])
    mem = w["mem_prompt"].reshape(NM, D)
    w_in = w["w_in"][0]
    halves = lambda a: [tiles(a[:, i * 512:(i + 1) * 512], 512) for i in range(a.shape[1] // 512)]
    units = (halves(w_in) + halves(w["w_mem_k"][0]) + halves(w["w_mem_v"][0]) + halves(w["w_out"][0])
             + halves(w["w_mem_q"][0]) + halves(w["w_mem_o"][0]))
    units.insert(4, tiles(w["w_glu"][0], 1024))
    q_gain = w["att_q_gain"].reshape(HD, 1)
    state = lambda a: a.reshape(GP, 2, GS, -1).transpose(1, 2, 0, 3).reshape(P, GP, -1)
    pair = lambda a: state(a.reshape(G, GS, -1))
    c_t = lambda a: a[0].transpose(0, 2, 1)
    gu = np.concatenate([w["exp_w_gate"][0], w["exp_w_up"][0]], axis=2)
    router = np.concatenate([w["router_g_w"][0], w["router_e_w"][0].transpose(1, 0, 2).reshape(D, NE)], axis=1)
    step = np.broadcast_to(w["ssm_log_step"].reshape(G, 1), (G, GS))
    arrays = {
        "x_t": tiles(x.T, T),
        "x_rows": x,
        "mem_t": tiles(mem.T, NM),
        "mem_rows": mem,
        "dense_w": np.stack([u.reshape(P, 4096) for u in units]),
        "exp_gu": gu.reshape(NE, KT, P, 2 * FF).transpose(0, 2, 1, 3),
        "exp_dn": w["exp_w_down"][0].reshape(NE, 2, P, D).transpose(0, 2, 1, 3),
        "ck_t": w["cache_attn_k"][0].reshape(NB, 512, NPAIR, P).transpose(0, 3, 2, 1),
        "cv": w["cache_attn_v"][0].reshape(NB, 512, AW),
        "cmk_t": w["cache_mem_k"][0].reshape(NB, NM, 8, P).transpose(0, 3, 2, 1),
        "cmv": w["cache_mem_v"][0].reshape(NB, NM, D),
        "cols": np.concatenate([col(w[k]) for k in ("norm_mix", "norm_mem", "mem_in_norm", "norm_ffn", "out_norm_ssm",
                                                    "out_norm_att")]
                               + [np.concatenate([q_gain, q_gain]), col(w["mem_q_gain"])], axis=1),
        "k_gain": w["att_k_gain"].reshape(HD),
        "mk_gain": w["mem_k_gain"].reshape(MD),
        "router_w": tiles(router, NG + NE),
        "router_b": np.concatenate([w["router_g_b"].reshape(-1), w["router_e_b"].reshape(-1)]),
        "ssm_small": np.stack([pair(a)[:, :, 0] for a in (w["ssm_lambda_re"], w["ssm_lambda_im"], step)], axis=1),
        "ssm_bc": np.stack([pair(w["ssm_b_re"][0]), pair(w["ssm_b_im"][0]), pair(c_t(w["ssm_c_re"])), pair(c_t(w["ssm_c_im"]))], axis=1),
        "ssm_d": w["ssm_d"].reshape(G, GC).T,
        "ssm_s0": np.stack([pair(a[0].transpose(1, 2, 0)) for a in (w["state_ssm_re"], w["state_ssm_im"])], axis=1),
        "rel_rev": w["att_rel_bias"][0][:, ::-1],
    }
    nc = bacc.Bacc("TRN2", target_bir_lowering=False, num_devices=1)
    sent, ins, outs = {}, {}, {}
    for name in _INS:
        a = np.ascontiguousarray(arrays[name])
        sent[f"in_{name}"] = a
        ins[name] = nc.dram_tensor(f"in_{name}", a.shape, mybir.dt.from_np(a.dtype), kind="ExternalInput").ap()
    for name, shape in _OUTS:
        outs[f"{name}_out"] = nc.dram_tensor(f"out_{name}", shape, F32, kind="ExternalOutput").ap()
    program(nc, **ins, **outs)
    got = run_bass_kernel_spmd(nc, [sent], core_ids=[0]).results[0]
    y, k, v, mk, mv, s = (np.asarray(got[f"out_{name}"]) for name, _ in _OUTS)
    s = s.reshape(2, GS, 2, GP, NB + 1).transpose(2, 4, 3, 0, 1).reshape(2, NB + 1, G, GS)
    heads = lambda a, *lead: a.reshape(*lead, NH, HD)
    return (y[:TP].reshape(1, TP, D), y[TP:].reshape(NB, SQ, D),
            heads(k[:TP], 1, 1, TP), heads(v[:TP], 1, 1, TP), s[0, 0:1][None], s[1, 0:1][None],
            mk.reshape(1, 1, NM, MH, MD), mv.reshape(1, 1, NM, MH, MD),
            heads(k[TP:], 1, NB, SQ), heads(v[TP:], 1, NB, SQ), s[0, 1:][None], s[1, 1:][None])
```

```python
from contextlib import ExitStack

import numpy as np

import concourse.bass as bass
from concourse import mybir

F32 = mybir.dt.float32
U32 = mybir.dt.uint32
I32 = mybir.dt.int32
ALU = mybir.AluOpType
ACT = mybir.ActivationFunctionType
AXX = mybir.AxisListType.X

P = 128
D = 1024
KT = D // P
TP, TS = 512, 128
NT = (TP + TS) // P
T = NT * P
NB, SQ = 8, 16
HD, NH = 64, 8
AW = NH * HD
NPAIR = NH // 2
CH = 64
REL = 128
EXT = P + 2 * REL + 1
G, GC, GS = 32, 16, 64
GP = G // 2
L = 8
NCH = T // L
PCH = TP // L
HALVES = 2
HP = GP // HALVES
NM, MH, MD = 256, 4, 256
NG, EPG = 4, 8
NE = NG * EPG
FF = 256
EPS = 1e-6
NEG = -1e30
CAP = 104
NBLK = -(-T // CAP)
NOV = (2 * T) // CAP - 1
NU = NE + NOV
TWO_PI_HI = 6.28125
TWO_PI_LO = 0.0019353071795864769
GELU_C = 0.7978845608028654
ROUND = 12582912.0

PROMPT_UNITS = [(t, h) for t in range(NT - 1) for h in range(NH)]
MEM_UNITS = [(t, h) for t in range(NT - 1) for h in range(MH)]
BAND_UNITS = len(PROMPT_UNITS) + NB


FILL = [[[], [("v", 3), ("v", 4), ("mk", 0)], [("mk", 1)]],
        [[("mk", 2), ("mk", 3)], [("mv", 0), ("mv", 1), ("mv", 2)], [("mv", 3)]]]



def pe_order():
    o = [("u", t) for t in range(NT)]
    for i in range(10):
        o.append(("qk", i))
        if i >= 2:
            o.append(("qkT", i - 2))
    o += [("v", 0), ("qkT", 8), ("v", 1), ("qkT", 9), ("v", 2)]
    o += [("UT", i) for i in range(8)]
    for hf in range(HALVES):
        o += [("G", 4 * hf + i) for i in range(4)]
        o += FILL[hf][0]
        o += [("K", 4 * hf + i) for i in range(4)]
        o += [("V", 4 * hf + i) for i in range(4)]
        o += FILL[hf][1]
        o += [("Y", 4 * hf + i) for i in range(4)]
        o += [("YT", 4 * hf + i) for i in range(4)]
        o += FILL[hf][2]
    for c in range(4):
        o += [("gg", c), ("gv", c)]
    o += [("S", 0), ("S", 1)]
    o += [("gs", c) for c in range(4)]
    n = len(PROMPT_UNITS)
    for i in range(n + 4):
        if 2 <= i < n:
            o.append(("S", i))
        if 0 <= i - 2 < n:
            o.append(("PT", i - 2))
        if i >= 4 and (i - 4) % 2 == 1 and i - 4 < n:
            o.append(("PV", (i - 4) // 2))
    for b in range(NB + 3):
        if b < NB:
            o += [("sA", b), ("sB", b)]
        if 0 <= b - 1 < NB:
            o += [("sPa", b - 1), ("sPb", b - 1)]
        if 0 <= b - 2 < NB:
            o.append(("sPV", b - 2))
        if 0 <= b - 3 < NB:
            o.append(("sO", b - 3))
    for t in range(NT + 1):
        if t < NT:
            for c in range(2):
                o += [("oS", 2 * t + c), ("oA", 2 * t + c)]
        if t == 0:
            o.append(("ss", 0))
        if t >= 1:
            o += [("x1T", 2 * t - 2), ("x1T", 2 * t - 1)]
    o += [("mkT", i) for i in range(4)]
    for i in range(12):
        if i < 10:
            o.append(("mq", i))
        if i == 10:
            o += [("mS", 0), ("mS", 1)]
        if i >= 2:
            o.append(("mqT", i - 2))
    n = len(MEM_UNITS)
    for i in range(n + 3):
        if 2 <= i < n:
            o.append(("mS", i))
        if 0 <= i - 2 < n:
            o.append(("mPT", i - 2))
        if 0 <= i - 3 < n:
            o.append(("mPV", i - 3))
    for i in range(7):
        if i < 4:
            o.append(("mS", n + i))
        if 0 <= i - 1 < 4:
            o.append(("mPT", n + i - 1))
        if 0 <= i - 2 < 4:
            o += [("smPV", 2 * (i - 2)), ("smPV", 2 * (i - 2) + 1)]
        if 0 <= i - 3 < 4:
            o += [("smT", 2 * (i - 3)), ("smT", 2 * (i - 3) + 1)]
    for t in range(NT + 3):
        if t < NT:
            o += [("mo", 2 * t), ("mo", 2 * t + 1)]
        if 0 <= t - 1 < NT:
            o += [("x2T", 2 * t - 2), ("x2T", 2 * t - 1)]
        if 0 <= t - 2 < NT:
            o.append(("rt", t - 2))
        if t >= 3:
            o.append(("rtT", t - 3))
    o += [("rank", 0), ("tab", 0)]
    return o


ORDER = pe_order()
NUMBER = {key: n for n, key in enumerate(ORDER)}
KINDS = sorted({k for k, _ in ORDER})

W_SLOT = {0: 0, 1: 1, 2: 2, 3: 0, 5: 2, 6: 0, 7: 2, 8: 0, 4: 2, 9: 1, 10: 0, 11: 2, 12: 1, 13: 0, 14: 2}
W_LOADS = list(W_SLOT)
W_AFTER = {3: ("u", 4), 5: None, 6: ("v", 4), 7: ("mk", 1), 8: ("mk", 3), 4: ("mv", 1), 9: ("mv", 3), 10: ("mv", 3),
           11: ("ss", 0), 12: ("oA", 8), 13: ("oA", 9), 14: ("mq", 8)}


def w_count(u):
    before = W_LOADS[:W_LOADS.index(u) + 1]
    return sum(W_SLOT[i] == W_SLOT[u] for i in before)


HT = 12288
QT = HT + KT * T
KTO = QT + NPAIR * T
VR = KTO + NPAIR * T
CONST = VR + NT * AW
R = CONST + 2560
WORDS = R + 25472


def program(nc, x_t, x_rows, mem_t, mem_rows, dense_w, exp_gu, exp_dn, ck_t, cv, cmk_t, cmv, cols, k_gain, mk_gain,
            router_w, router_b, ssm_small, ssm_bc, ssm_d, ssm_s0, rel_rev,
            y_out, k_out, v_out, mk_out, mv_out, s_out):
    ctx = ExitStack()
    with ctx:
        arena = ctx.enter_context(nc.sbuf_tensor("arena", [P, WORDS], F32))
        banks = ctx.enter_context(nc.psum_tensor("banks", [P, 8, 512], F32))
        slot_idx = ctx.enter_context(nc.sbuf_tensor("slot_idx", [P, 2 * NT], U32))
        tok_idx = ctx.enter_context(nc.sbuf_tensor("tok_idx", [P, NU], U32))
        ov_regs = ctx.enter_context(nc.sbuf_tensor("ov_regs", [P, NOV + 1], I32))
        u_dram = nc.dram_tensor("u_scratch", [T, 512], F32)
        e_dram = nc.dram_tensor("bias_scratch", [NH, P, EXT], F32)
        mk_dram = nc.dram_tensor("memory_key_scratch", [NM, D], F32)
        xn_dram = nc.dram_tensor("xn_scratch", [T, D], F32)
        moe_dram = nc.dram_tensor("moe_scratch", [NU * CAP, D], F32)

        def at(off, *dims, p0=0, p1=P):
            n = int(np.prod(dims))
            v = arena[p0:p1, off:off + n]
            if len(dims) == 1:
                return v
            names = "abcd"[:len(dims)]
            s = " ".join(names)
            return v.rearrange(f"p ({s}) -> p {s}", **{k: d for k, d in zip(names, dims)})

        def sem(name):
            return ctx.enter_context(nc.semaphore(name))

        def spread(ap, shape):
            return ap.to_broadcast(shape)

        W = [at(4096 * s, 4096) for s in range(3)]

        def wdense(u):
            return W[W_SLOT[u]]

        hT = at(HT, KT, T)
        qT = at(QT, NPAIR, T)
        kT = at(KTO, NPAIR, T)
        v_rows = at(VR, NT, AW)
        pos = [CONST]

        def const(*dims):
            off = pos[0]
            pos[0] += int(np.prod(dims))
            assert pos[0] <= R
            return at(off, *dims)

        ident = const(P)
        tri = const(P)
        ones = const(P)
        colc = const(56)
        norm_mix, norm_mem, mem_in_norm, norm_ffn = (colc[:, 8 * i:8 * i + 8] for i in range(4))
        out_ssm, out_att = colc[:, 32:36], colc[:, 36:40]
        q_gain, mq_gain = colc[:, 40:41], colc[:, 41:43]
        bias_far = colc[:, 43:44]
        mq_gain4 = colc[:, 44:48]
        minus_half = const(48)
        kg = const(HD)
        mkg = const(MD)
        rw = const(KT, NG + NE)
        rb = const(NG + NE)
        bias_s = const(144)
        bias_new = const(240)
        ssx, rstd_x = const(NT), const(NT)
        ssm_, rstd_m = const(2), const(2)
        ss1, rstd_1 = const(NT), const(NT)
        ss2, rstd_2 = const(NT), const(NT)
        ssg, rstd_g = const(2 * NT), const(2 * NT)
        iota_slot = const(max(CAP, NU))
        iota32, iota4 = iota_slot[:, 0:NE], iota_slot[:, 0:NG]
        qss, qf = const(4, NH), const(4, NH)
        smax, ssum = const(4, 4), const(4, 4)
        rel_ext = const(EXT)
        tokid = const(NT)
        tmp48 = const(48)
        qss8, qf8 = const(8), const(8)
        d_tmp = const(64)

        yT = at(R, 4, T)
        y_half = [at(R + 2 * T * i, 2 * T) for i in range(2)]
        gelu_sq = [at(R + 18176 + 2 * T * i, 2 * T) for i in range(2)]
        Uc = at(8192, L, 512, p1=NCH)
        U = at(R + 2560, G, L * GC, p1=NCH)
        Yh = at(R + 2560, L, 256, p1=NCH)
        Gm = at(R + 4608, HP, 2, P)
        UT = at(R + 6656, G, NCH)
        BL = [at(R + 9216 + 1024 * i, HP, L, GC) for i in range(2)]
        Kt = at(R + 9216, HP, 2, P)
        Wm = [at(R + 11264 + 1152 * i, HP, L + 1, GC) for i in range(2)]
        Kpad = [at(R + 13568 + 1024 * i, 4, 256, p1=GC) for i in range(2)]
        tA = R + 15616
        t1, t2 = (lambda *d: at(tA, *d)), (lambda *d: at(tA + 1152, *d))
        Vr, Vi = at(tA, HP, NCH), at(tA + 640, HP, NCH)
        Sr, Si = at(tA + 1280, HP, NCH), at(tA + 1920, HP, NCH)
        Tr, Ti = at(R + 18176, HP, PCH), at(R + 18688, HP, PCH)
        rho_t = at(R + 19200, HP, PCH)
        wr, wi = at(R + 19712, HP, PCH), at(R + 20224, HP, PCH)
        spos = [R + 20736]

        def small(*dims, **k):
            off = spos[0]
            spos[0] += int(np.prod(dims))
            assert spos[0] <= R + 23424
            return at(off, *dims, **k)

        par = small(3, GP)
        bc = small(4, GP, GC)
        Bb = [small(GP, GC) for _ in range(2)]
        Pw = [small(GP, L + 1) for _ in range(2)]
        Pv = [bc[:, r].rearrange("p a c -> p (a c)")[:, 0:GP * L].rearrange("p (a c) -> p a c", c=L) for r in range(2)]
        s0 = small(2, GP, NB)
        dskip = small(G, p1=GC)
        sm = [small(GP) for _ in range(14)]
        step, radius, sinp, radius8 = sm[0], sm[3], sm[4], sm[6]
        fin = small(2, GP, NB + 1)
        stage_off = R + 23424
        raw = [at(stage_off + 512 * i, 512) for i in range(2)]
        nrm = [at(stage_off + 1024 + 512 * i, 512) for i in range(2)]
        x_early = at(R + 9216, NT, D)
        mem_r = at(R + 2560, 2, D)
        squares = at(R + 14336, D)
        memT = at(4096, KT, NM)
        m_stage = [at(4096 + KT * NM + 512 * i, 512) for i in range(2)]

        ysT = at(R + 2560, 4, T)
        xr = at(R + 5120, NT, D)
        yaT = at(R, 4, T)
        qblk = at(R + 10240, NB, NPAIR, P)
        bias_p = at(R + 14336, NH, 256)
        kc = [at(R + 16384 + 2048 * i, NPAIR, 512) for i in range(2)]
        vc = [at(R + 20480 + 2048 * i, 4, 512) for i in range(2)]
        Pb = [at(HT + 640 * i, 640) for i in range(3)]
        PT = [at(HT + 1920 + 640 * i, 5, P) for i in range(4)]
        s_rows = [at(HT + 4480 + P * i, P) for i in range(2)]
        glu_t = [at(R + 16384 + 512 * i, 512) for i in range(2)]
        branch_sq = at(8192, 4, T)
        branch_sum = [at(8192 + 4 * T + T * i, T) for i in range(2)]

        qm = at(QT, 8, T)
        mk_rows = at(R + 14336, 2, D)
        mv_rows = at(R + 16384, 2, D)
        mkT = at(R + 18432, 8, NM)
        mraw = [at(R + 20480 + 512 * i, 512) for i in range(2)]
        mnrm = [at(R + 21504 + 512 * i, 512) for i in range(2)]
        mP = [at(R + 22528 + 256 * i, 256) for i in range(4)]
        mPT = [at(R + 23552 + 256 * i, 2, P) for i in range(4)]
        qblk2 = at(R, NB, 8, 64)
        mkc = [at(o, 8, NM) for o in (R + 10240, R + 14336, 4096, 6144)]
        mvc = [at(o, 2, D) for o in (R + 12288, R + 20480, R + 16384, R + 18432)]

        def mem_loads(b):
            return (NB // 2 if b % 4 < 2 else 0) + b // 4 + 1
        sm_rows = [at(VR + D * i, D) for i in range(2)]
        oT = hT

        xn = [at(R + 10240 + 1024 * i, D) for i in range(2)]
        rpos = [R + 12288]

        def rt(*dims):
            off = rpos[0]
            rpos[0] += int(np.prod(dims))
            assert rpos[0] <= R + 15616
            return at(off, *dims)

        gu_buf = [at(o, KT, 512) for o in (QT, 4096, 0, 8192)]
        dn_buf = [at(R + 15616 + 2048 * i, 2, D) for i in range(4)]
        xg = [at(HT + 1024 * i, D) for i in range(2)]
        xgT = [at(HT + 2048 + 1024 * i, KT, P) for i in range(2)]
        th_b = [at(HT + 4096 + 256 * i, 2, P) for i in range(2)]
        h_b = [at(HT + 4608 + 256 * i, 2, P) for i in range(2)]
        ye = [at(QT + 4096 + 1024 * i, D) for i in range(2)]
        a_b = at(QT + 6144, 2, P)
        yg = [at(D * i, D) for i in range(2 * NT)]

        product_ready = sem("product_ready")
        drained = {k: sem(f"drained_{k}") for k in KINDS}
        dve_chain, act_chain, pool_chain = sem("dve_chain"), sem("act_chain"), sem("pool_chain")
        w_landed = [sem(f"w_landed{i}") for i in range(3)]
        names = ("xT_landed xT_rest_landed w0_half_landed x_landed consts_landed ssm_landed rel_landed consts_built x_squared rstd_x_ready hT_ready "
                 "qk_stats qk_factor qk_normed k_stored0 k_stored1 v_stored u_stored0 u_stored1 U_landed U_turned b_ready w_ready "
                 "kpad_ready kt_landed0 kt_landed1 state_ready gelu_sq gelu_arg gelu_th gelu_ready "
                 "rel_built e_stored bias_landed bias_p_landed bias_built glu_th "
                 "row_max p_normed p_scaled qblk_ready kc0 kc1 vc0 vc1 "
                 "mem_landed mem_squared rstd_m_ready memT_ready mk_stats mk_factor mk_normed mk_stored memT_landed m_stored0 m_stored1 "
                 "sq_ready rstd_g_ready branch_scaled  rstd_1_ready  mq_normed "
                 "kc2 kc3 vc2 vc3 qblk2_ready "
                 "rstd_2_ready xn_ready xn_stored0 xn_stored1 logits_ready "
                 "choice_exp choice_ready slots_ready rows_zeroed table_parts_ready s_stored").split()
        S = {n: sem(n) for n in names}

        def bank(key):
            return banks[:, NUMBER[key] % 8, :]

        def claim(pe, key):
            n = NUMBER[key]
            if n >= 8:
                kind, i = ORDER[n - 8]
                pe.wait_ge(drained[kind], i + 1)
            return banks[:, n % 8, :]

        def done(eng, key):
            eng.wait_ge(product_ready, NUMBER[key] + 1)

        logit = rt(NT, NG + NE)
        chosen, before = rt(NT + 1, NE), rt(NT + 1, NE)
        block_starts = rt(NBLK - 1)
        past = rt(NE, NBLK - 1)
        oh = rt(2, NT, NE)
        oh1, oh2 = oh[:, 0], oh[:, 1]
        logit_t = [at(R + 4096 + P * i, P) for i in range(2)]
        lsel, rtmp = rt(NT, NE), rt(2, NT, NE)
        gsm = [rt(NT, NG) for _ in range(3)]
        gmax, gidx, p1, v1, dv = (rt(NT) for _ in range(5))
        idx, ta, tb, blk, unit_of = (rt(2, NT) for _ in range(5))
        slot_f, w12 = rt(2, NT), rt(2, NT)
        rank_sb = rt(NT + 1, NE)
        extra, incl, ovb = rt(NE), rt(NE), rt(NE)
        ovt, ovf = rt(NOV, NE), rt(NOV + 1)
        zeros = at(R + 24576, 512)
        slot_hot = at(R, 2, NT, CAP)
        unit_tok = at(R + 2 * NT * CAP, 2, NT, NU)

        moe_names = ("tx_done xgT_ready gu_done th_ready h_ready dn_done ye_ready xg0 xg1 y_st0 y_st1 "
                     "gu_l0 gu_l1 gu_l2 gu_l3 dn_l0 dn_l1 dn_l2 dn_l3 yg_landed0 yg_landed1 yg_landed2 yg_landed3 yg_landed4 y_ready y_out "
                     "o_w").split()
        moe = {n: sem("moe_" + n) for n in moe_names}

        moe_a = sem("moe_silu_ready")

        def late(i, c, n):
            return not isinstance(i, int) or 4 * i + c >= n

        act_ssm, dve_ssm = sem("ssm_functions"), sem("ssm_arguments")

        def moe_load_first(sp, e):
            if e == 0:
                done(sp, ("smT", NB - 1))
                sp.wait_ge(S["mk_stored"], 16)
            if e == 2:
                done(sp, ("mo", 9))
                sp.wait_ge(S["xn_stored0"], 48)
                sp.wait_ge(S["xn_stored1"], 32)
            sp.dma_start(gu_buf[e], exp_gu[e]).then_inc(moe[f"gu_l{e}"], 16)
            sp.dma_start(dn_buf[e], exp_dn[e]).then_inc(moe[f"dn_l{e}"], 16)

        def moe_sync(sp):
            def step(i, c):
                s = 4 * i + c
                if c >= 1:
                    e = (c + 3) % 4
                    sp.wait_ge(moe["gu_done"], s)
                    sp.dma_start(gu_buf[e], exp_gu[bass.ds(s + 3, 1)].rearrange("e p k n -> (e p) k n")).then_inc(moe[f"gu_l{e}"], 16)
                    sp.wait_ge(moe["dn_done"], 2 * s)
                    sp.dma_start(dn_buf[e], exp_dn[bass.ds(s + 3, 1)].rearrange("e p k n -> (e p) k n")).then_inc(moe[f"dn_l{e}"], 16)
                    store(i, c)

            def store(i, c):
                s = 4 * i + c
                sp.wait_ge(moe["ye_ready"], 2 * s)
                sp.dma_start(moe_dram.ap()[bass.ds((s - 1) * CAP, CAP), :], ye[(c - 1) % 2][0:CAP, :]).then_inc(moe[f"y_st{(c - 1) % 2}"], 16)

            with sp.Fori(0, 7) as i:
                for c in range(1, 5):
                    step(i, c)
            for c in range(29, 33):
                store(0, c)
            sp.wait_ge(S["rows_zeroed"], 16 * NOV)
            nov = sp.value_load(ov_regs[0:1, NOV:NOV + 1], min_val=0, max_val=NOV)
            with sp.Fori(0, NOV) as v:
                with sp.If(v < nov):
                    ex = sp.value_load(ov_regs[0:1, bass.ds(v, 1)], min_val=0, max_val=NE - 1)
                    sp.wait_ge(moe["dn_done"], 2 * NE + v)
                    sp.dma_start(gu_buf[0], exp_gu[bass.ds(ex, 1)].rearrange("e p k n -> (e p) k n")).then_inc(moe["o_w"], 16)
                    sp.dma_start(dn_buf[0], exp_dn[bass.ds(ex, 1)].rearrange("e p k n -> (e p) k n")).then_inc(moe["o_w"], 16)
                    sp.wait_ge(moe["ye_ready"], 2 * NE + v + 1)
                    sp.dma_start(moe_dram.ap()[bass.ds((v + NE) * CAP, CAP), :], ye[0][0:CAP, :]).then_inc(moe["y_st0"], 16)

        def unit_turn(ps, src, xi):
            for a in range(4):
                last = nc.tensor.transpose(ps[:, a * P:a * P + CAP], src[0:CAP, (4 * xi + a) * P:(4 * xi + a + 1) * P], ident[0:CAP, 0:CAP])
            return last

        def unit_gate_up(ps, x, w):
            for f in range(4):
                for k in range(KT):
                    last = nc.tensor.matmul(ps[:, f * P:f * P + CAP], w[:, k, f * P:(f + 1) * P], x[:, k, 0:CAP],
                                            start=(k == 0), stop=(k == KT - 1))
            return last

        def unit_down(ps, hb, w, c):
            for k in range(2):
                last = nc.tensor.matmul(ps[0:CAP, :], hb[:, k, 0:CAP], w[:, k, c * 512:(c + 1) * 512], start=(k == 0), stop=(k == 1))
            return last

        def moe_tensor(pe):
            def TX(i, c):
                e = 4 * i + c
                pe.wait_ge(moe[f"xg{c % 2}"], 32 * i + 16 * (c // 2 + 1))
                for xi in range(2):
                    if late(i, c, 2):
                        pe.wait_ge(moe["xgT_ready"], 2 * e - 3 + xi)
                    unit_turn(banks[:, 2 * (c % 2) + xi, :], xg[c % 2], xi).then_inc(moe["tx_done"], 1)

            def GU(i, c):
                e = 4 * i + c
                pe.wait_ge(moe["xgT_ready"], 2 * e + 2)
                pe.wait_ge(moe[f"gu_l{c % 4}"], 16 * i + 16 * (c // 4 + 1))
                if late(i, c, 2):
                    pe.wait_ge(moe["h_ready"], e - 1)
                unit_gate_up(banks[:, 4 + c % 2, :], xgT[c % 2], gu_buf[c % 4]).then_inc(moe["gu_done"], 1)

            def DN(i, c):
                e = 4 * i + c
                pe.wait_ge(moe["h_ready"], e + 1)
                pe.wait_ge(moe[f"dn_l{c % 4}"], 16 * i + 16 * (c // 4 + 1))
                for ch in range(2):
                    if late(i, c, 1):
                        pe.wait_ge(moe["ye_ready"], 2 * e - 1 + ch)
                    unit_down(banks[:, 6 + ch, :], h_b[c % 2], dn_buf[c % 4], ch).then_inc(moe["dn_done"], 1)

            for kind, j in ORDER[-8:]:
                pe.wait_ge(drained[kind], j + 1)
            TX(0, 0)
            TX(0, 1)
            GU(0, 0)
            peeled = [1, 2, 3, 4]
            for c in peeled:
                TX(0, c + 1)
                GU(0, c)
                DN(0, c - 1)
            with pe.Fori(1, 7) as i:
                for c in range(1, 5):
                    TX(i, c + 1)
                    GU(i, c)
                    DN(i, c - 1)
            for c in range(29, 32):
                if c < 31:
                    TX(0, c + 1)
                GU(0, c)
                DN(0, c - 1)
            DN(0, 31)
            nov = pe.value_load(ov_regs[0:1, NOV:NOV + 1], min_val=0, max_val=NOV)
            with pe.Fori(0, NOV) as v:
                with pe.If(v < nov):
                    pe.wait_ge(moe["xg0"], 16 * (NE // 2) + 16 * v + 16)
                    for xi in range(2):
                        unit_turn(banks[:, xi, :], xg[0], xi).then_inc(moe["tx_done"], 1)
                    pe.wait_ge(moe["xgT_ready"], 2 * NE + 2 * v + 2)
                    pe.wait_ge(moe["o_w"], 32 * v + 32)
                    unit_gate_up(banks[:, 4, :], xgT[0], gu_buf[0]).then_inc(moe["gu_done"], 1)
                    pe.wait_ge(moe["h_ready"], NE + v + 1)
                    pe.wait_ge(moe["ye_ready"], 2 * NE + v)
                    unit_down(banks[:, 6, :], h_b[0], dn_buf[0], 0)
                    unit_down(banks[:, 7, :], h_b[0], dn_buf[0], 1).then_inc(moe["dn_done"], 1)

        block = ctx.enter_context(nc.Block())

        @block.sync
        def _(sp):
            def load_w(u):
                if W_AFTER.get(u):
                    done(sp, W_AFTER[u])
                sp.dma_start(wdense(u), dense_w[u]).then_inc(w_landed[W_SLOT[u]], 16)

            sp.dma_start(colc[:, 0:43], cols).then_inc(S["xT_landed"], 16)
            sp.dma_start(hT[:, :, 0:P], x_t[:, :, 0:P]).then_inc(S["xT_landed"], 16)
            sp.dma_start(wdense(0)[:, 0:2048], dense_w[0][:, 0:2048]).then_inc(S["w0_half_landed"], 16)
            sp.dma_start(wdense(0)[:, 2048:4096], dense_w[0][:, 2048:4096]).then_inc(w_landed[0], 16)
            sp.dma_start(hT[:, :, P:T], x_t[:, :, P:T]).then_inc(S["xT_rest_landed"], 16)
            sp.dma_start(x_early, x_rows.rearrange("(t p) d -> p t d", p=P)).then_inc(S["x_landed"], 16)
            sp.dma_start(par, ssm_small).then_inc(S["ssm_landed"], 16)
            sp.dma_start(bc, ssm_bc).then_inc(S["ssm_landed"], 16)
            sp.dma_start(s0, ssm_s0).then_inc(S["ssm_landed"], 16)
            sp.dma_start(dskip, ssm_d).then_inc(S["ssm_landed"], 16)
            load_w(1)
            sp.dma_start(kg, k_gain.partition_broadcast(P)).then_inc(S["consts_landed"], 16)
            sp.dma_start(mkg, mk_gain.partition_broadcast(P)).then_inc(S["consts_landed"], 16)
            sp.dma_start(rw, router_w).then_inc(S["consts_landed"], 16)
            sp.dma_start(rb, router_b.partition_broadcast(P)).then_inc(S["consts_landed"], 16)
            sp.dma_start(rel_ext[0:NH, P:EXT], rel_rev).then_inc(S["rel_landed"], 16)
            load_w(2)
            sp.dma_start(mem_r, mem_rows.rearrange("(t p) d -> p t d", p=P)).then_inc(S["mem_landed"], 16)
            load_w(3)
            done(sp, ("qk", 4))
            sp.dma_start(memT, mem_t).then_inc(S["memT_landed"], 16)
            sp.wait_ge(S["u_stored0"], 48)
            sp.wait_ge(S["u_stored1"], 32)
            done(sp, ("qk", 9))
            sp.dma_start(at(8192, 4096, p1=NCH), u_dram.ap().rearrange("(c j) d -> c (j d)", j=L)).then_inc(S["U_landed"], 16)
            sp.wait_ge(S["e_stored"], 16)
            for h in range(NH):
                src = bass.AP(e_dram, h * P * EXT + P, [[EXT - 1, SQ], [1, 144]])
                sp.dma_start(bias_s[SQ * h:SQ * h + SQ, :], src).then_inc(S["bias_landed"], 16)
            sp.wait_ge(S["U_turned"], 1)
            load_w(5)
            for i in range(8):
                if i == 4:
                    load_w(6)
                    load_w(7)
                    load_w(8)
                sp.wait_ge(S["kpad_ready"], i + 1)
                if i % 4 == 0:
                    done(sp, ("G", i + 3))
                if i == 4:
                    done(sp, ("Y", 3))
                q = (i % 4) // 2
                for j in range(L):
                    sp.dma_start(Kt[GC * j:GC * j + GC, 4 * q:4 * q + 4, i % 2, :],
                                 Kpad[i % 2][:, :, P - GC * j:2 * P - GC * j]).then_inc(S[f"kt_landed{i % 2}"], 16)
            load_w(4)
            done(sp, ("Y", 7))
            sp.dma_start(xr, x_rows.rearrange("(t p) d -> p t d", p=P)).then_inc(S["x_landed"], 16)
            sp.wait_ge(S["kt_landed0"], 16 * 32)
            sp.wait_ge(S["kt_landed1"], 16 * 32)
            src = bass.AP(e_dram, P, [[EXT - 1, P], [P * EXT, NH], [1, 256]])
            sp.dma_start(bias_p, src).then_inc(S["bias_p_landed"], 16)
            for i in range(2):
                sp.wait_ge(S[f"m_stored{i}"], 16 * 4)
            load_w(9)
            load_w(10)

            def load_keys(b):
                if b >= 2:
                    done(sp, ("sB", b - 2))
                elif b == 0:
                    sp.wait_ge(S["s_stored"], 16)
                    sp.wait_ge(S["k_stored0"], 32)
                    sp.wait_ge(S["k_stored1"], 48)
                    sp.wait_ge(drained["gs"], 4)
                sp.dma_start(kc[b % 2], ck_t[b]).then_inc(S[f"kc{b % 2}"], 16)

            def load_values(b):
                if b >= 2:
                    done(sp, ("sPV", b - 2))
                sp.dma_start(vc[b % 2], cv[b].rearrange("(t p) d -> p t d", p=P)).then_inc(S[f"vc{b % 2}"], 16)

            load_keys(0)
            load_keys(1)
            load_values(0)
            load_values(1)
            load_keys(2)
            for b in range(3, NB):
                load_keys(b)
                load_values(b - 1)
            load_values(NB - 1)
            done(sp, ("sB", NB - 1))
            sp.dma_start(mk_rows, mk_dram.ap().rearrange("(t p) d -> p t d", p=P)).then_inc(S["mem_landed"], 16)
            sp.dma_start(mv_rows, mv_out.rearrange("(t p) d -> p t d", p=P)).then_inc(S["mem_landed"], 16)

            def load_mem_keys(b):
                if b >= 4:
                    done(sp, ("mS", len(MEM_UNITS) + (b - 4) // 2))
                elif b >= 2:
                    done(sp, ("mq", 9))
                elif b == 1:
                    sp.wait_ge(S["mk_stored"], 16)
                    done(sp, ("mkT", 3))
                sp.dma_start(mkc[b % 4], cmk_t[b]).then_inc(S[f"kc{b % 4}"], 16)

            def load_mem_values(b):
                if b >= 4:
                    done(sp, ("smPV", 2 * (b // 2 - 2) + 1))
                elif b == 3:
                    done(sp, ("mS", len(MEM_UNITS) - 1))
                elif b == 2:
                    done(sp, ("mPV", len(MEM_UNITS) - 1))
                elif b == 1:
                    done(sp, ("mqT", 9))
                else:
                    done(sp, ("sPV", NB - 1))
                sp.dma_start(mvc[b % 4], cmv[b].rearrange("(t p) d -> p t d", p=P)).then_inc(S[f"vc{b % 4}"], 16)

            load_mem_keys(0)
            load_mem_values(0)
            load_w(11)
            load_w(12)
            load_w(13)
            load_mem_keys(1)
            load_w(14)
            for load, bs in ((load_mem_keys, (2, 3)), (load_mem_values, (1, 3, 2)), (load_mem_keys, (4, 5, 6, 7)),
                             (load_mem_values, (4, 5, 6, 7))):
                for b in bs:
                    load(b)

            for e in range(4):
                moe_load_first(sp, e)
            moe_sync(sp)
            for t in range(NT):
                sp.wait_ge(moe["y_ready"], t + 1)
                sp.dma_start(y_out[t * P:(t + 1) * P, :], xr[:, t, :]).then_inc(moe["y_out"], 16)
            sp.wait_ge(moe["y_out"], 16 * NT)
            sp.wait_ge(S["v_stored"], 16)

        @block.tensor
        def _(pe):
            def dense(key, lhs, rhs, n, k=KT):
                ps = claim(pe, key)
                for i in range(k):
                    last = nc.tensor.matmul(ps[:, 0:n], lhs(i), rhs(i), start=(i == 0), stop=(i == k - 1))
                last.then_inc(product_ready, 1)

            def w_at(u, first=True):
                if first:
                    pe.wait_ge(w_landed[W_SLOT[u]], 16 * w_count(u))
                return wdense(u).rearrange("p (k n) -> p k n", k=KT)

            def tok(t):
                return slice(t * P, (t + 1) * P)

            def qkT(i):
                ps = claim(pe, ("qkT", i)).rearrange("p (a b) -> p a b", a=4)
                pe.wait_ge(S["qk_normed"], i + 1)
                for a in range(NPAIR):
                    last = nc.tensor.transpose(ps[:, a, :], nrm[i % 2][:, a * P:(a + 1) * P], ident)
                last.then_inc(product_ready, 1)

            w = w_at(0, False)
            for t in range(NT):
                if t < 2:
                    pe.wait_ge(S["hT_ready"], t + 1)
                ps = claim(pe, ("u", t))
                for k in range(KT):
                    if t == 0 and k == 0:
                        pe.wait_ge(S["w0_half_landed"], 16)
                    if t == 0 and k == 4:
                        pe.wait_ge(w_landed[0], 16)
                    last = nc.tensor.matmul(ps, hT[:, k, tok(t)], w[:, k, :], start=(k == 0), stop=(k == KT - 1))
                last.then_inc(product_ready, 1)
            pe.wait_ge(S["consts_built"], 1)
            for i in range(10):
                w = w_at(1 + i // 5, i % 5 == 0)
                dense(("qk", i), lambda k: hT[:, k, tok(i % 5)], lambda k: w[:, k, :], 512)
                if i >= 2:
                    qkT(i - 2)
            def v_product(t):
                w = w_at(3, t == 0)
                dense(("v", t), lambda k: hT[:, k, tok(t)], lambda k: w[:, k, :], 512)

            def mem_product(kind, i):
                w = w_at((5 if kind == "mk" else 7) + i // 2, i % 2 == 0)
                if kind == "mk" and i == 0:
                    pe.wait_ge(S["memT_ready"], 1)
                dense((kind, i), lambda k: memT[:, k, tok(i % 2)], lambda k: w[:, k, :], 512)

            def fill(products):
                for kind, i in products:
                    if kind == "v":
                        v_product(i)
                    else:
                        mem_product(kind, i)

            for t in range(3):
                v_product(t)
                if t < 2:
                    qkT(8 + t)

            pe.wait_ge(S["U_turned"], 1)
            for i in range(8):
                ps = claim(pe, ("UT", i)).rearrange("p (a b) -> p a b", a=4)
                for a in range(4):
                    g = 4 * i + a
                    last = nc.tensor.transpose(ps[:, a, 0:NCH], U[:, g, :], ident[0:NCH, 0:NCH])
                last.then_inc(product_ready, 1)

            for hf in range(HALVES):
                pe.wait_ge(S["b_ready"], hf + 1)
                for i in range(4):
                    ps = claim(pe, ("G", 4 * hf + i)).rearrange("p (a r b) -> p a r b", a=2, r=2)
                    for a in range(2):
                        for r in range(2):
                            last = nc.tensor.transpose(ps[:, a, r, :], BL[r][:, 2 * i + a, :, :].rearrange("p j c -> p (j c)"), ident)
                    last.then_inc(product_ready, 1)
                fill(FILL[hf][0])
                pe.wait_ge(S["w_ready"], hf + 1)
                for i in range(4):
                    ps = claim(pe, ("K", 4 * hf + i)).rearrange("p (a b) -> p a b", a=4)
                    lo = GS * (i % 2)
                    for a in range(4):
                        pr = 4 * (i // 2) + a
                        for r in range(2):
                            last = nc.tensor.matmul(ps[0:GC, a, :], Bb[r][lo:lo + GS, HP * hf + pr, :],
                                                    Wm[r][lo:lo + GS, pr, 0:L, :].rearrange("p j c -> p (j c)"),
                                                    start=(r == 0), stop=(r == 1))
                    last.then_inc(product_ready, 1)
                pe.wait_ge(drained["UT"], 8)
                pe.wait_ge(drained["G"], 4 * hf + 4)
                for i in range(4):
                    ps = claim(pe, ("V", 4 * hf + i))
                    r = i % 2
                    for a in range(4):
                        pr = 4 * (i // 2) + a
                        for g2 in range(2):
                            last = nc.tensor.matmul(ps[GS * g2:GS * g2 + GS, a * NCH:(a + 1) * NCH],
                                                    Gm[:, pr, r, GS * g2:GS * g2 + GS],
                                                    UT[:, 2 * (HP * hf + pr) + g2, :], start=True, stop=True)
                    last.then_inc(product_ready, 1)
                fill(FILL[hf][1])
                pe.wait_ge(S["state_ready"], hf + 1)
                for i in range(4):
                    ps = claim(pe, ("Y", 4 * hf + i)).rearrange("p (a b) -> p a b", a=4)
                    g2 = i % 2
                    lo = GS * g2
                    pe.wait_ge(S[f"kt_landed{g2}"], 16 * 8 * (2 * hf + i // 2 + 1))
                    for a in range(4):
                        pr = 4 * (i // 2) + a
                        nc.tensor.matmul(ps[0:NCH, a, :], UT[:, 2 * (HP * hf + pr) + g2, :], Kt[:, pr, g2, :],
                                         start=True, stop=False)
                        for r, st in ((0, Sr), (1, Si)):
                            last = nc.tensor.matmul(ps[0:NCH, a, :], st[lo:lo + GS, pr, :],
                                                    Wm[r][lo:lo + GS, pr, 1:L + 1, :].rearrange("p j c -> p (j c)"),
                                                    start=False, stop=(r == 1))
                    last.then_inc(product_ready, 1)
                pe.wait_ge(drained["Y"], 4 * hf + 4)
                for i in range(4):
                    ps = claim(pe, ("YT", 4 * hf + i)).rearrange("p (a b) -> p a b", a=4)
                    for a in range(4):
                        last = nc.tensor.transpose(ps[:, a, 0:NCH], Yh[:, 4 * (i % 2) + a, P * (i // 2):P * (i // 2) + P],
                                                   ident[0:NCH, 0:NCH])
                    last.then_inc(product_ready, 1)

                fill(FILL[hf][2])

            wg = w_at(4).rearrange("p k n -> p (k n)").rearrange("p (k n) -> p k n", k=4)
            pe.wait_ge(S["gelu_ready"], 2)
            for c in range(4):
                for kind, o in (("gg", 512), ("gv", 0)):
                    dense((kind, c), lambda k: wg[:, k, o + c * P:o + (c + 1) * P], lambda k: yT[:, k, 0:TP], TP, 4)
            pe.wait_ge(drained["qkT"], 10)
            pe.wait_ge(drained["v"], NT)

            def scores(i):
                t, h = PROMPT_UNITS[i]
                ps = claim(pe, ("S", i))
                lo = HD * (h % 2)
                nc.tensor.matmul(ps[:, 0:P * (t + 1)], qT[lo:lo + HD, h // 2, tok(t)], kT[lo:lo + HD, h // 2, 0:P * (t + 1)],
                                 start=True, stop=True).then_inc(product_ready, 1)

            scores(0)
            scores(1)
            for c in range(4):
                ps = claim(pe, ("gs", c))
                for j, o in enumerate((512, 0)):
                    for k in range(4):
                        last = nc.tensor.matmul(ps[:, j * P:(j + 1) * P], wg[:, k, o + c * P:o + (c + 1) * P],
                                                yT[:, k, TP:T], start=(k == 0), stop=(k == 3))
                last.then_inc(product_ready, 1)

            def turn(kind, i, unit, tiles, first=0):
                ps = claim(pe, (kind, i)).rearrange("p (a b) -> p a b", a=4)
                pe.wait_ge(S["p_scaled"], unit + 1)
                for a in range(tiles):
                    last = nc.tensor.transpose(ps[:, a, :], Pb[unit % 3][:, (first + a) * P:(first + a + 1) * P], ident)
                last.then_inc(product_ready, 1)

            n = len(PROMPT_UNITS)
            for i in range(n + 4):
                if 2 <= i < n:
                    scores(i)
                if 0 <= i - 2 < n:
                    turn("PT", i - 2, i - 2, PROMPT_UNITS[i - 2][0] + 1)
                if i >= 4 and (i - 4) % 2 == 1 and i - 4 < n:
                    m = (i - 4) // 2
                    ps = claim(pe, ("PV", m))
                    pe.wait_ge(drained["PT"], i - 3)
                    for unit in (i - 5, i - 4):
                        t, h = PROMPT_UNITS[unit]
                        lo = HD * (h % 2)
                        for k in range(t + 1):
                            last = nc.tensor.matmul(ps[lo:lo + HD, 0:P], v_rows[:, k, h * HD:(h + 1) * HD],
                                                    PT[unit % 4][:, k, :], start=(k == 0), stop=(k == t))
                    last.then_inc(product_ready, 1)
            pe.wait_ge(S["qblk_ready"], 1)
            for b in range(NB + 3):
                if b < NB:
                    ps = claim(pe, ("sA", b))
                    pe.wait_ge(S[f"kc{b % 2}"], 16 * (b // 2 + 1))
                    for a in range(NPAIR):
                        last = nc.tensor.matmul(ps, qblk[:, b, a, :], kc[b % 2][:, a, :], start=(a == 0), stop=(a == 3))
                    last.then_inc(product_ready, 1)
                    ps = claim(pe, ("sB", b))
                    for a in range(NPAIR):
                        last = nc.tensor.matmul(ps[:, 0:P], qblk[:, b, a, :], kT[:, a, TP:T], start=(a == 0), stop=(a == 3))
                    last.then_inc(product_ready, 1)
                if 0 <= b - 1 < NB:
                    turn("sPa", b - 1, n + b - 1, 4)
                    turn("sPb", b - 1, n + b - 1, 1, first=4)
                if 0 <= b - 2 < NB:
                    c = b - 2
                    ps = claim(pe, ("sPV", c))
                    pe.wait_ge(drained["sPb"], c + 1)
                    pe.wait_ge(S[f"vc{c % 2}"], 16 * (c // 2 + 1))
                    for a in range(NPAIR):
                        for k in range(5):
                            v = vc[c % 2][:, k, a * P:(a + 1) * P] if k < 4 else v_rows[:, 4, a * P:(a + 1) * P]
                            last = nc.tensor.matmul(ps[a * 32:(a + 1) * 32, 0:P], PT[(n + c) % 4][:, k, a * 32:(a + 1) * 32], v,
                                                    start=(k == 0), stop=(k == 4))
                    last.then_inc(product_ready, 1)
                if 0 <= b - 3 < NB:
                    ps = claim(pe, ("sO", b - 3))
                    pe.wait_ge(drained["sPV"], b - 2)
                    nc.tensor.transpose(ps[:, 0:P], s_rows[(b - 3) % 2], ident).then_inc(product_ready, 1)

            def turn_rows(kind, i):
                t, hh = i // 2, i % 2
                ps = claim(pe, (kind, i)).rearrange("p (a b) -> p a b", a=4)
                for a in range(4):
                    last = nc.tensor.transpose(ps[:, a, :], xr[:, t, (4 * hh + a) * P:(4 * hh + a + 1) * P], ident)
                last.then_inc(product_ready, 1)

            wo = [w_at(9), w_at(10)]
            for t in range(NT + 1):
                if t < NT:
                    pe.wait_ge(S["branch_scaled"], 2 if t < NT - 1 else 3)
                    for c in range(2):
                        for kind, k0, src in (("oS", 0, ysT), ("oA", 4, yaT)):
                            dense((kind, 2 * t + c), lambda k: src[:, k, tok(t)],
                                  lambda k: wo[c][:, k0 + k, :], 512, 4)
                if t == 0:
                    ps = claim(pe, ("ss", 0))
                    pe.wait_ge(S["sq_ready"], 3)
                    for br in range(2):
                        for j in range(NT):
                            last = nc.tensor.matmul(ps[:, br * NT + j:br * NT + j + 1], branch_sum[br][:, tok(j)], ones[:, 0:1],
                                                    start=True, stop=True)
                    last.then_inc(product_ready, 1)
                if t >= 1:
                    for hh in range(2):
                        pe.wait_ge(drained["oA"], 2 * t - 1 + hh)
                        turn_rows("x1T", 2 * t - 2 + hh)
            for i in range(4):
                ps = claim(pe, ("mkT", i)).rearrange("p (a b) -> p a b", a=4)
                pe.wait_ge(S["mk_normed"], i + 1)
                for a in range(4):
                    last = nc.tensor.transpose(ps[:, a, :], mk_rows[:, i // 2, (i % 2) * 512 + a * P:(i % 2) * 512 + (a + 1) * P], ident)
                last.then_inc(product_ready, 1)

            pe.wait_ge(drained["x1T"], 10)
            wq = [w_at(11), w_at(12)]

            def mem_scores(i):
                t, h = MEM_UNITS[i]
                dense(("mS", i), lambda k: qm[:, 2 * h + k, tok(t)], lambda k: mkT[:, 2 * h + k, :], NM, 2)

            for i in range(12):
                if i < 10:
                    dense(("mq", i), lambda k: hT[:, k, tok(i // 2)], lambda k: wq[i % 2][:, k, :], 512)
                if i == 10:
                    pe.wait_ge(drained["mqT"], 2)
                    pe.wait_ge(drained["mkT"], 4)
                    mem_scores(0)
                    mem_scores(1)
                if i >= 2:
                    j = i - 2
                    ps = claim(pe, ("mqT", j)).rearrange("p (a b) -> p a b", a=4)
                    pe.wait_ge(S["mq_normed"], j + 1)
                    for a in range(4):
                        last = nc.tensor.transpose(ps[:, a, :], mnrm[j % 2][:, a * P:(a + 1) * P], ident)
                    last.then_inc(product_ready, 1)
            pe.wait_ge(drained["mqT"], 10)
            n = len(MEM_UNITS)

            def mem_turn(i):
                ps = claim(pe, ("mPT", i)).rearrange("p (a b) -> p a b", a=4)
                pe.wait_ge(S["p_scaled"], BAND_UNITS + i + 1)
                for a in range(2):
                    last = nc.tensor.transpose(ps[:, a, :], mP[i % 4][:, a * P:(a + 1) * P], ident)
                last.then_inc(product_ready, 1)

            for i in range(n + 3):
                if 2 <= i < n:
                    mem_scores(i)
                if 0 <= i - 2 < n:
                    mem_turn(i - 2)
                if 0 <= i - 3 < n:
                    j = i - 3
                    t, h = MEM_UNITS[j]
                    ps = claim(pe, ("mPV", j)).rearrange("p (a b) -> p a b", a=4)
                    pe.wait_ge(drained["mPT"], j + 1)
                    for dt in range(2):
                        for k in range(2):
                            last = nc.tensor.matmul(ps[:, dt, :], mv_rows[:, k, h * MD + dt * P:h * MD + (dt + 1) * P],
                                                    mPT[j % 4][:, k, :], start=(k == 0), stop=(k == 1))
                    last.then_inc(product_ready, 1)
            pe.wait_ge(S["qblk2_ready"], 1)
            for i in range(7):
                if i < 4:
                    ps = claim(pe, ("mS", n + i))
                    for b2 in range(2):
                        b = 2 * i + b2
                        pe.wait_ge(S[f"kc{b % 4}"], 16 * mem_loads(b))
                        for k in range(8):
                            last = nc.tensor.matmul(ps[64 * b2:64 * b2 + 64, 0:NM], qblk2[:, b, k, :], mkc[b % 4][:, k, :],
                                                    start=(k == 0), stop=(k == 7))
                    last.then_inc(product_ready, 1)
                if 0 <= i - 1 < 4:
                    mem_turn(n + i - 1)
                if 0 <= i - 2 < 4:
                    pe.wait_ge(drained["mPT"], n + i - 1)
                    for c in range(2):
                        ps = claim(pe, ("smPV", 2 * (i - 2) + c))
                        for b2 in range(2):
                            b = 2 * (i - 2) + b2
                            pe.wait_ge(S[f"vc{b % 4}"], 16 * mem_loads(b))
                            for k in range(2):
                                last = nc.tensor.matmul(ps[64 * b2:64 * b2 + 64, :], mPT[(n + i - 2) % 4][:, k, 64 * b2:64 * b2 + 64],
                                                        mvc[b % 4][:, k, 512 * c:512 * c + 512], start=(k == 0), stop=(k == 1))
                        last.then_inc(product_ready, 1)
                if 0 <= i - 3 < 4:
                    for c in range(2):
                        j = 2 * (i - 3) + c
                        ps = claim(pe, ("smT", j)).rearrange("p (a b) -> p a b", a=4)
                        pe.wait_ge(drained["smPV"], j + 1)
                        for a in range(4):
                            last = nc.tensor.transpose(ps[:, a, :], sm_rows[(i - 3) % 2][:, (4 * c + a) * P:(4 * c + a + 1) * P], ident)
                        last.then_inc(product_ready, 1)
            wo2 = [w_at(13), w_at(14)]
            pe.wait_ge(drained["mPV"], n)
            pe.wait_ge(drained["smT"], NB)
            for t in range(NT + 3):
                if t < NT:
                    for c in range(2):
                        dense(("mo", 2 * t + c), lambda k: oT[:, k, tok(t)], lambda k: wo2[c][:, k, :], 512)
                if 0 <= t - 1 < NT:
                    for hh in range(2):
                        pe.wait_ge(drained["mo"], 2 * t - 1 + hh)
                        turn_rows("x2T", 2 * t - 2 + hh)
                if 0 <= t - 2 < NT:
                    ps = claim(pe, ("rt", t - 2))
                    pe.wait_ge(drained["x2T"], 2 * (t - 1))
                    for k in range(KT):
                        last = nc.tensor.matmul(ps[0:NG + NE, 0:P], rw[:, k, :], hT[:, k, tok(t - 2)], start=(k == 0), stop=(k == KT - 1))
                    last.then_inc(product_ready, 1)
                if t >= 3:
                    ps = claim(pe, ("rtT", t - 3))
                    pe.wait_ge(drained["rt"], t - 2)
                    nc.tensor.transpose(ps[:, 0:NG + NE], logit_t[(t - 3) % 2][0:NG + NE, :], ident[0:NG + NE, 0:NG + NE]).then_inc(product_ready, 1)
            pe.wait_ge(S["choice_ready"], 1)
            ps = claim(pe, ("rank", 0))
            n = (NT + 1) * NE
            nc.tensor.matmul(ps[:, 0:n], tri, chosen.rearrange("p t e -> p (t e)"), start=True, stop=False)
            nc.tensor.matmul(ps[:, 0:n], ones, before.rearrange("p t e -> p (t e)"), start=False, stop=True).then_inc(product_ready, 1)
            ps = claim(pe, ("tab", 0))
            pe.wait_ge(S["table_parts_ready"], 1)
            for j in range(2):
                for t in range(NT):
                    last = nc.tensor.matmul(ps[0:CAP, 0:NU], slot_hot[:, j, t, :], unit_tok[:, j, t, :],
                                            start=(j == t == 0), stop=(j == 1 and t == NT - 1))
            last.then_inc(product_ready, 1)
            moe_tensor(pe)

        @block.scalar
        def _(act):
            n_chain = [0]

            def link(ins):
                n_chain[0] += 1
                ins.then_inc(act_chain, 1)
                act.wait_ge(act_chain, n_chain[0])

            A = nc.scalar.activation
            act.wait_ge(S["x_landed"], 16)
            for t in range(NT):
                if t:
                    act.wait_ge(S["x_squared"], t)
                A(squares, x_early[:, t, :], ACT.Square, accum_out=ssx[:, t:t + 1]).then_inc(S["x_squared"], 1)
            act.wait_ge(S["ssm_landed"], 64)
            A(step, par[:, 2, :], ACT.Exp).then_inc(act_ssm, 1)
            act.wait_ge(dve_ssm, 1)
            A(radius, sm[1], ACT.Exp).then_inc(act_ssm, 1)
            A(radius8, sm[1], ACT.Exp, scale=float(L)).then_inc(act_ssm, 1)
            A(sinp, sm[2], ACT.Sin).then_inc(act_ssm, 1)
            A(sm[5], sm[2], ACT.Sin, scale=0.5).then_inc(act_ssm, 1)
            act.wait_ge(S["rstd_x_ready"], 1)
            for t in range(NT):
                done(act, ("u", t))
                if t >= 2:
                    act.wait_ge(S[f"u_stored{t % 2}"], 16 * (t // 2))
                A(raw[t % 2], bank(("u", t)), ACT.Copy, scale=rstd_x[:, t:t + 1]).then_inc(drained["u"], 1)
            act.wait_ge(S["mem_landed"], 16)
            for t in range(2):
                act.wait_ge(*((S["mem_squared"], t) if t else (S["x_squared"], NT)))
                A(squares, mem_r[:, t, :], ACT.Square, accum_out=ssm_[:, t:t + 1]).then_inc(S["mem_squared"], 1)
            act.wait_ge(S["u_stored0"], 48)
            act.wait_ge(S["u_stored1"], 32)

            def qkT(i):
                done(act, ("qkT", i))
                src = bank(("qkT", i)).rearrange("p (a b) -> p a b", a=4)
                dst = (qT if i < 5 else kT)[:, :, (i % 5) * P:(i % 5 + 1) * P]
                if i < 5:
                    A(dst, src, ACT.Copy, scale=tmp48[:, 0:1]).then_inc(drained["qkT"], 1)
                else:
                    A(dst, src, ACT.Copy).then_inc(drained["qkT"], 1)

            act.wait_ge(S["hT_ready"], 3)
            for i in range(10):
                done(act, ("qk", i))
                if i >= 2:
                    act.wait_ge(S["qk_normed"], i - 1)
                A(raw[i % 2], bank(("qk", i)), ACT.Copy, scale=rstd_x[:, i % 5:i % 5 + 1]).then_inc(drained["qk"], 1)
                if i >= 2:
                    qkT(i - 2)
            def v_out_rows(t):
                done(act, ("v", t))
                A(v_rows[:, t, :], bank(("v", t)), ACT.Copy, scale=rstd_x[:, t:t + 1]).then_inc(drained["v"], 1)

            def mem_rows_out(kind, i):
                n = i if kind == "mk" else 4 + i
                done(act, (kind, i))
                if n == 0:
                    act.wait_ge(S["rstd_m_ready"], 1)
                if n >= 2:
                    act.wait_ge(S[f"m_stored{n % 2}"], 16 * (n // 2))
                A(m_stage[n % 2], bank((kind, i)), ACT.Copy, scale=rstd_m[:, i % 2:i % 2 + 1]).then_inc(drained[kind], 1)

            def fill(products):
                for kind, i in products:
                    if kind == "v":
                        v_out_rows(i)
                    else:
                        mem_rows_out(kind, i)

            for t in range(3):
                v_out_rows(t)
                if t < 2:
                    qkT(8 + t)
            act.wait_ge(S["U_landed"], 16)
            A(U.rearrange("p g (j c) -> p j g c", j=L), Uc.rearrange("p j (g c) -> p j g c", g=G), ACT.Copy).then_inc(S["U_turned"], 1)
            for i in range(8):
                done(act, ("UT", i))
                A(UT[:, 4 * i:4 * i + 4, :], bank(("UT", i)).rearrange("p (a b) -> p a b", a=4)[:, :, 0:NCH], ACT.Copy).then_inc(drained["UT"], 1)
            done(act, ("UT", 7))

            def gelu_square(hf):
                act.wait_ge(drained["YT"], 4 * hf + 4)
                A(gelu_sq[hf], y_half[hf], ACT.Square).then_inc(S["gelu_sq"], 1)

            def gelu_tanh(hf):
                act.wait_ge(S["gelu_arg"], hf + 1)
                A(gelu_sq[hf], gelu_sq[hf], ACT.Tanh, scale=GELU_C).then_inc(S["gelu_th"], 1)

            for hf in range(HALVES):
                for i in range(4):
                    done(act, ("G", 4 * hf + i))
                    if hf:
                        done(act, ("V", 3))
                    A(Gm[:, 2 * i:2 * i + 2, :, :].rearrange("p a r b -> p (a r b)"), bank(("G", 4 * hf + i)), ACT.Copy).then_inc(drained["G"], 1)
                fill(FILL[hf][0])
                for i in range(4):
                    done(act, ("V", 4 * hf + i))
                    dst = (Vr, Vi)[i % 2][:, 4 * (i // 2):4 * (i // 2) + 4, :].rearrange("p a b -> p (a b)")
                    act.wait_ge(S["w_ready"], hf + 1)
                    A(dst, bank(("V", 4 * hf + i))[:, 0:4 * NCH], ACT.Copy).then_inc(drained["V"], 1)
                fill(FILL[hf][1])
                if hf:
                    act.wait_ge(S["state_ready"], 2)
                    gelu_square(0)
                for i in range(4):
                    if hf and i == 2:
                        gelu_tanh(0)
                    done(act, ("Y", 4 * hf + i))
                    if hf:
                        done(act, ("YT", 3))
                    g2, q = i % 2, i // 2
                    dst = Yh.rearrange("p j (a g c) -> p a g j c", g=2, c=GC)[:, 4 * q:4 * q + 4, g2, :, :]
                    src = bank(("Y", 4 * hf + i)).rearrange("p (a j c) -> p a j c", a=4, c=GC)[0:NCH]
                    A(dst, src, ACT.Copy).then_inc(drained["Y"], 1)
                for i in range(4):
                    done(act, ("YT", 4 * hf + i))
                    src = bank(("YT", 4 * hf + i)).rearrange("p (a b) -> p a b", a=4)[:, :, 0:NCH]
                    dst = yT[:, 2 * hf + i // 2, :].rearrange("p (c j) -> p j c", j=L)[:, 4 * (i % 2):4 * (i % 2) + 4, :]
                    A(dst, src, ACT.Copy).then_inc(drained["YT"], 1)
                if hf == 0:
                    fill(FILL[hf][2])
            act.wait_ge(drained["YT"], 8)
            gelu_square(1)
            gelu_tanh(1)
            fill(FILL[1][2])
            act.wait_ge(S["gelu_ready"], 2)
            for c in range(4):
                done(act, ("gg", c))
                if c >= 2:
                    act.wait_ge(drained["gv"], c - 1)
                A(glu_t[c % 2], bank(("gg", c)), ACT.Tanh, scale=0.25).then_inc(drained["gg"], 1)

            def exp_unit(i, parts):
                act.wait_ge(S["row_max"], i + 1)
                if i >= 3:
                    turned(act, i - 3)
                for j, (key, n, c0) in enumerate(parts):
                    ins = A(Pb[i % 3][:, c0:c0 + n], bank(key)[:, 0:n], ACT.Exp, bias=smax[:, i % 4, 2:3],
                            accum_out=ssum[:, i % 4, j:j + 1])
                    if j < len(parts) - 1:
                        ins.then_inc(drained[key[0]], 1)
                ins.then_inc(drained[parts[-1][0][0]], 1)

            def turned(eng, i):
                n = len(PROMPT_UNITS)
                done(eng, ("PT", i) if i < n else ("sPb", i - n))

            def pt_out(kind, i, unit, tiles, first=0):
                done(act, (kind, i))
                if unit >= 4:
                    n = len(PROMPT_UNITS)
                    u = unit - 4
                    done(act, ("PV", u // 2) if u < n else ("sPV", u - n))
                src = bank((kind, i)).rearrange("p (a b) -> p a b", a=4)[:, 0:tiles, :]
                A(PT[unit % 4][:, first:first + tiles, :], src, ACT.Copy).then_inc(drained[kind], 1)

            def exp_prompt(i):
                exp_unit(i, [(("S", i), P * (PROMPT_UNITS[i][0] + 1), 0)])

            exp_prompt(0)
            exp_prompt(1)
            for c in range(4):
                done(act, ("gs", c))
                act.wait_ge(*((drained["gv"], c + 3) if c < 2 else (drained["gs"], c - 1)))
                A(glu_t[c % 2][:, 0:P], bank(("gs", c))[:, 0:P], ACT.Tanh, scale=0.25).then_inc(S["glu_th"], 1)
            n = len(PROMPT_UNITS)
            for i in range(n + 2):
                if 2 <= i < n:
                    exp_prompt(i)
                if i >= 2:
                    pt_out("PT", i - 2, i - 2, PROMPT_UNITS[i - 2][0] + 1)
            for b in range(NB + 2):
                if b < NB:
                    exp_unit(n + b, [(("sA", b), 512, 0), (("sB", b), P, 512)])
                if 0 <= b - 1 < NB:
                    pt_out("sPa", b - 1, n + b - 1, 4)
                    pt_out("sPb", b - 1, n + b - 1, 1, first=4)
                if b >= 2:
                    done(act, ("sPV", b - 2))
                    if b >= 4:
                        done(act, ("sO", b - 4))
                    A(s_rows[b % 2], bank(("sPV", b - 2))[:, 0:P], ACT.Copy).then_inc(drained["sPV"], 1)
            for t in range(NT):
                act.wait_ge(drained["oA"], 2 * t + 2)
                if t:
                    act.wait_ge(S["x_squared"], NT + t)
                A(at(R + 22528, D), xr[:, t, :], ACT.Square, accum_out=ss1[:, t:t + 1]).then_inc(S["x_squared"], 1)
            for i in range(4):
                done(act, ("mkT", i))
                src = bank(("mkT", i)).rearrange("p (a b) -> p a b", a=4)
                A(mkT[:, 4 * (i % 2):4 * (i % 2) + 4, (i // 2) * P:(i // 2 + 1) * P], src, ACT.Copy).then_inc(drained["mkT"], 1)
            act.wait_ge(S["rstd_1_ready"], 1)
            for i in range(10):
                done(act, ("mq", i))
                if i >= 2:
                    act.wait_ge(S["mq_normed"], i - 1)
                A(mraw[i % 2], bank(("mq", i)), ACT.Copy, scale=rstd_1[:, i // 2:i // 2 + 1]).then_inc(drained["mq"], 1)

            def mem_pt(i):
                done(act, ("mPT", i))
                n = len(MEM_UNITS)
                if i >= 4:
                    j = i - 4
                    done(act, ("mPV", j) if j < n else ("smPV", 2 * (j - n) + 1))
                A(mPT[i % 4], bank(("mPT", i)).rearrange("p (a b) -> p a b", a=4)[:, 0:2, :], ACT.Copy).then_inc(drained["mPT"], 1)

            n = len(MEM_UNITS)
            act.wait_ge(S["x_squared"], NT + NT)
            def mem_exp(i):
                act.wait_ge(S["row_max"], BAND_UNITS + i + 1)
                if i >= 4:
                    done(act, ("mPT", i - 4))
                A(mP[i % 4], bank(("mS", i))[:, 0:NM], ACT.Exp, bias=smax[:, i % 4, 2:3],
                  accum_out=ssum[:, i % 4, 0:1]).then_inc(drained["mS"], 1)

            mem_exp(0)
            mem_exp(1)
            for i in range(n + 2):
                if 2 <= i < n:
                    mem_exp(i)
                if i >= 2:
                    mem_pt(i - 2)
            act.wait_ge(S["v_stored"], 16)
            for i in range(6):
                if i < 4:
                    mem_exp(n + i)
                if 0 <= i - 1 < 4:
                    mem_pt(n + i - 1)
                if i >= 2:
                    if i >= 4:
                        done(act, ("smT", 2 * (i - 4) + 1))
                    for c in range(2):
                        done(act, ("smPV", 2 * (i - 2) + c))
                        A(sm_rows[i % 2][:, 512 * c:512 * c + 512], bank(("smPV", 2 * (i - 2) + c)), ACT.Copy).then_inc(drained["smPV"], 1)

            def normed_rows(t):
                act.wait_ge(S["rstd_2_ready"], t + 1)
                if t >= 2:
                    act.wait_ge(S[f"xn_stored{t % 2}"], 16 * (t // 2))
                A(xn[t % 2], xr[:, t, :], ACT.Copy, scale=rstd_2[:, t:t + 1]).then_inc(S["xn_ready"], 1)

            for t in range(NT):
                act.wait_ge(drained["mo"], 2 * t + 2)
                if t:
                    act.wait_ge(S["x_squared"], 2 * NT + t)
                A(at(R + 14592, D), xr[:, t, :], ACT.Square, accum_out=ss2[:, t:t + 1]).then_inc(S["x_squared"], 1)
                if t >= 1:
                    normed_rows(t - 1)
            normed_rows(NT - 1)
            act.wait_ge(S["logits_ready"], 1)
            A(gsm[1], gsm[1], ACT.Exp).then_inc(S["choice_exp"], 1)
            act.wait_ge(S["logits_ready"], 2)
            A(dv, dv, ACT.Exp).then_inc(S["choice_exp"], 1)

            def TH(i, c):
                e = 4 * i + c
                act.wait_ge(moe["gu_done"], e + 1)
                if late(i, c, 2):
                    act.wait_ge(moe["h_ready"], e - 1)
                A(th_b[c % 2][:, :, 0:CAP], banks[:, 4 + c % 2, :].rearrange("p (a b) -> p a b", a=4)[:, 0:2, 0:CAP], ACT.Tanh,
                  scale=0.5).then_inc(moe["th_ready"], 1)

            def YE(i, c):
                e = 4 * i + c
                if late(i, c, 2):
                    act.wait_ge(moe[f"y_st{c % 2}"], 32 * i + 16 * (c // 2))
                for ch in range(2):
                    act.wait_ge(moe["dn_done"], 2 * e + ch + 1)
                    A(ye[c % 2][0:CAP, ch * 512:(ch + 1) * 512], banks[0:CAP, 6 + ch, :], ACT.Copy).then_inc(moe["ye_ready"], 1)

            TH(0, 0)
            for c in range(1, 5):
                TH(0, c)
                YE(0, c - 1)
            with act.Fori(1, 7) as i:
                for c in range(1, 5):
                    TH(i, c)
                    YE(i, c - 1)
            for c in range(29, 32):
                TH(0, c)
                YE(0, c - 1)
            YE(0, 31)
            nov = act.value_load(ov_regs[0:1, NOV:NOV + 1], min_val=0, max_val=NOV)
            act.wait_ge(moe["y_st0"], 16 * 16)
            with act.Fori(0, NOV) as v:
                with act.If(v < nov):
                    act.wait_ge(moe["gu_done"], NE + v + 1)
                    A(th_b[0][:, :, 0:CAP], banks[:, 4, :].rearrange("p (a b) -> p a b", a=4)[:, 0:2, 0:CAP], ACT.Tanh,
                      scale=0.5).then_inc(moe["th_ready"], 1)
                    act.wait_ge(moe["dn_done"], 2 * NE + v + 1)
                    act.wait_ge(moe["y_st0"], 16 * (NE // 2) + 16 * v)
                    A(ye[0][0:CAP, 0:512], banks[0:CAP, 6, :], ACT.Copy)
                    A(ye[0][0:CAP, 512:1024], banks[0:CAP, 7, :], ACT.Copy).then_inc(moe["ye_ready"], 1)

        @block.gpsimd
        def _(pool):
            n_chain = [0]
            g = nc.gpsimd

            def link(ins):
                n_chain[0] += 1
                ins.then_inc(pool_chain, 1)
                pool.wait_ge(pool_chain, n_chain[0])

            def rsqrt_mean(dst, src, n, count, signal, col=8):
                mean = tmp48[:, col:col + n]
                link(g.tensor_scalar(mean, src, 1.0 / count, EPS, ALU.mult, ALU.add))
                g.tensor_tensor(dst, mean, minus_half[:, 0:n], ALU.pow).then_inc(signal, 1)

            link(g.memset(minus_half, -0.5))
            link(g.memset(ident, 0.0))
            link(g.affine_select(out=ident, in_=ident, compare_op=ALU.not_equal, fill=1.0, base=0,
                                 pattern=[[-1, P]], channel_multiplier=1))
            link(g.memset(ones, 1.0))
            link(g.affine_select(out=tri, in_=ones, compare_op=ALU.is_gt, fill=0.0, base=0,
                                 pattern=[[1, P]], channel_multiplier=-1))
            link(g.iota(iota_slot, [[1, max(CAP, NU)]], base=0, channel_multiplier=0, allow_small_or_imprecise_dtypes=True))
            g.iota(tokid, [[P, NT]], base=0, channel_multiplier=1, allow_small_or_imprecise_dtypes=True).then_inc(S["consts_built"], 1)
            pool.wait_ge(S["x_squared"], NT)
            rsqrt_mean(rstd_x, ssx, NT, D, S["rstd_x_ready"])
            for t in range(NT):
                pool.wait_ge(drained["u"], t + 1)
                g.dma_start(u_dram.ap()[t * P:(t + 1) * P, :], raw[t % 2]).then_inc(S[f"u_stored{t % 2}"], 16)

            pool.wait_ge(S["rel_built"], 1)
            g.dma_start(e_dram.ap(), spread(rel_ext[0:NH, :].unsqueeze(1), [NH, P, EXT])).then_inc(S["e_stored"], 16)
            pool.wait_ge(S["mem_squared"], 2)
            rsqrt_mean(rstd_m, ssm_, 2, D, S["rstd_m_ready"], col=40)

            def k_store(i):
                pool.wait_ge(S["qk_normed"], i + 1)
                g.dma_start(k_out[(i - 5) * P:(i - 4) * P, :], nrm[i % 2]).then_inc(S[f"k_stored{i % 2}"], 16)

            for i in range(10):
                pool.wait_ge(S["qk_stats"], i + 1)
                rsqrt_mean(qf[:, i % 4, :], qss[:, i % 4, :], NH, HD, S["qk_factor"])
                if i >= 6:
                    k_store(i - 1)
            k_store(9)
            pool.wait_ge(drained["v"], NT)
            g.dma_start(v_out.rearrange("(t p) d -> p t d", p=P), v_rows).then_inc(S["v_stored"], 16)
            for kind, dst in (("mk", mk_dram.ap()), ("mv", mv_out)):
                for i in range(4):
                    pool.wait_ge(drained[kind], i + 1)
                    c, t = i // 2, i % 2
                    g.dma_start(dst[t * P:(t + 1) * P, c * 512:(c + 1) * 512], m_stage[i % 2]).then_inc(S[f"m_stored{i % 2}"], 16)
            pool.wait_ge(S["state_ready"], 2)
            g.dma_start(s_out, fin).then_inc(S["s_stored"], 16)
            n = len(PROMPT_UNITS)
            for i in range(n + NB):
                w = P * (PROMPT_UNITS[i][0] + 1) if i < n else 640
                pool.wait_ge(S["p_normed"], i + 1)
                g.tensor_scalar(Pb[i % 3][:, 0:w], Pb[i % 3][:, 0:w], ssum[:, i % 4, 3:4], None, ALU.mult).then_inc(S["p_scaled"], 1)
            pool.wait_ge(drained["ss"], 1)
            rsqrt_mean(rstd_g, ssg, 2 * NT, AW, S["rstd_g_ready"])
            pool.wait_ge(S["mk_stats"], 1)
            rsqrt_mean(qf8, qss8, 8, MD, S["mk_factor"])
            pool.wait_ge(S["mk_normed"], 4)
            g.dma_start(mk_out.rearrange("(t p) d -> p t d", p=P), mk_rows).then_inc(S["mk_stored"], 16)
            link(g.memset(zeros, 0.0))
            for vv in range(NOV):
                rows = moe_dram.ap()[(NE + vv) * CAP:(NE + vv + 1) * CAP, :].rearrange("p (a d) -> p a d", d=512)
                g.dma_start(rows, spread(zeros[0:CAP].unsqueeze(1), [CAP, 2, 512])).then_inc(S["rows_zeroed"], 16)
            pool.wait_ge(S["x_squared"], NT + NT)
            rsqrt_mean(rstd_1, ss1, NT, D, S["rstd_1_ready"])
            for i in range(10):
                pool.wait_ge(S["qk_stats"], 10 + i + 1)
                rsqrt_mean(qf[:, i % 4, 0:2], qss[:, i % 4, 0:2], 2, MD, S["qk_factor"])
            for i in range(len(MEM_UNITS) + NB // 2):
                pool.wait_ge(S["p_normed"], BAND_UNITS + i + 1)
                g.tensor_scalar(mP[i % 4], mP[i % 4], ssum[:, i % 4, 3:4], None, ALU.mult).then_inc(S["p_scaled"], 1)
            for t in range(NT + 1):
                if t < NT:
                    pool.wait_ge(S["x_squared"], 2 * NT + t + 1)
                    rsqrt_mean(rstd_2[:, t:t + 1], ss2[:, t:t + 1], 1, D, S["rstd_2_ready"], col=8 + t)
                if t >= 1:
                    pool.wait_ge(S["xn_ready"], t)
                    g.dma_start(xn_dram.ap()[(t - 1) * P:t * P, :], xn[(t - 1) % 2]).then_inc(S[f"xn_stored{(t - 1) % 2}"], 16)
            pool.wait_ge(S["xn_stored0"], 48)
            pool.wait_ge(S["xn_stored1"], 32)
            pool.wait_ge(drained["tab"], 1)

            def GA(i, c):
                e = 4 * i + c
                if c >= 2:
                    pool.wait_ge(moe["tx_done"], 2 * e - 2)
                col = tok_idx[0:CAP, bass.ds(e, 1)] if not isinstance(e, int) else tok_idx[0:CAP, e:e + 1]
                g.indirect_dma_start(xg[c % 2][0:CAP, :], None, xn_dram.ap(), bass.IndirectOffsetOnAxis(col, 0)).then_inc(moe[f"xg{c % 2}"], 16)

            GA(0, 0)
            GA(0, 1)
            for c in range(2, NE):
                GA(0, c)
            pool.wait_ge(S["rows_zeroed"], 16 * NOV)
            pool.wait_ge(S["slots_ready"], 1)
            nov = pool.value_load(ov_regs[0:1, NOV:NOV + 1], min_val=0, max_val=NOV)
            pool.wait_ge(moe["tx_done"], 2 * NE)
            for v in range(NOV):
                with pool.If(v < nov):
                    pool.wait_ge(moe["tx_done"], 2 * NE + 2 * v)
                    g.indirect_dma_start(xg[0][0:CAP, :], None, xn_dram.ap(),
                                         bass.IndirectOffsetOnAxis(tok_idx[0:CAP, NE + v:NE + v + 1], 0)).then_inc(moe["xg0"], 16)
                    pool.wait_ge(moe["y_st0"], 16 * (NE // 2) + 16 * v + 16)
            pool.wait_ge(moe["y_st0"], 16 * (NE // 2))
            pool.wait_ge(moe["y_st1"], 16 * (NE // 2))
            for t in range(NT):
                for j in range(2):
                    g.indirect_dma_start(yg[2 * t + j], None, moe_dram.ap(),
                                         bass.IndirectOffsetOnAxis(slot_idx[:, j * NT + t:j * NT + t + 1], 0)).then_inc(moe[f"yg_landed{t}"], 16)

        @block.vector
        def _(dve):
            n_chain = [0]
            v = nc.vector

            def link(ins):
                n_chain[0] += 1
                ins.then_inc(dve_chain, 1)
                dve.wait_ge(dve_chain, n_chain[0])

            def tt(o, a, b, op):
                link(v.tensor_tensor(o, a, b, op))

            def cmul(or_, oi, ar, ai, br, bi, x, y, conj_b=False):
                v.tensor_tensor(x, ar, br, ALU.mult)
                tt(y, ai, bi, ALU.mult)
                tt(or_, x, y, ALU.add if conj_b else ALU.subtract)
                v.tensor_tensor(x, ai, br, ALU.mult)
                tt(y, ar, bi, ALU.mult)
                tt(oi, x, y, ALU.subtract if conj_b else ALU.add)

            dve.wait_ge(S["xT_landed"], 32)
            v.tensor_tensor(hT[:, :, 0:P], hT[:, :, 0:P], spread(norm_mix.unsqueeze(2), [P, KT, P]), ALU.mult).then_inc(S["hT_ready"], 1)
            dve.wait_ge(S["xT_rest_landed"], 16)
            for k in range(KT):
                ins = v.tensor_scalar(hT[:, k, P:T], hT[:, k, P:T], norm_mix[:, k:k + 1], None, ALU.mult)
            ins.then_inc(S["hT_ready"], 1)
            v.tensor_scalar(tmp48[:, 0:1], q_gain, float(HD) ** -0.5, None, ALU.mult).then_inc(S["hT_ready"], 1)

            lr, li = par[:, 0, :], par[:, 1, :]
            dve.wait_ge(S["ssm_landed"], 64)
            dve.wait_ge(act_ssm, 1)
            tt(sm[1], lr, sm[0], ALU.mult)
            tt(sm[2], li, sm[0], ALU.mult)
            link(v.tensor_scalar(sm[7], sm[2], float(1.0 / (2 * np.pi)), ROUND, ALU.mult, ALU.add))
            link(v.tensor_scalar(sm[7], sm[7], ROUND, None, ALU.subtract))
            link(v.scalar_tensor_tensor(sm[2], sm[7], -TWO_PI_HI, sm[2], ALU.mult, ALU.add))
            link(v.scalar_tensor_tensor(sm[2], sm[7], -TWO_PI_LO, sm[2], ALU.mult, ALU.add))
            v.tensor_scalar(sm[2], sm[2], 3.1415925, -3.1415925, ALU.min, ALU.max).then_inc(dve_ssm, 1)
            dve.wait_ge(act_ssm, 5)
            tt(sm[7], sm[5], sm[5], ALU.mult)
            link(v.tensor_scalar(sm[5], sm[7], -2.0, 1.0, ALU.mult, ALU.add))
            cosp, rad = sm[5], radius
            link(v.memset(Pw[0][:, :, 0], 1.0))
            link(v.memset(Pw[1][:, :, 0], 0.0))
            tt(Pw[0][:, :, 1], rad, cosp, ALU.mult)
            tt(Pw[1][:, :, 1], rad, sinp, ALU.mult)
            tt(sm[7], lr, lr, ALU.mult)
            tt(sm[8], li, li, ALU.mult)
            tt(sm[7], sm[7], sm[8], ALU.add)
            link(v.reciprocal(sm[7], sm[7]))
            link(v.tensor_scalar(sm[8], Pw[0][:, :, 1], -1.0, None, ALU.add))
            cmul(sm[9], sm[10], sm[8], Pw[1][:, :, 1], lr, li, sm[11], sm[12], conj_b=True)
            tt(sm[9], sm[9], sm[7], ALU.mult)
            tt(sm[10], sm[10], sm[7], ALU.mult)
            full = [P, GP, GC]
            Fr, Fi = (spread(sm[i].unsqueeze(2), full) for i in (9, 10))
            dve.wait_ge(S["x_squared"], NT)
            cmul(Bb[0], Bb[1], Fr, Fi, bc[:, 0], bc[:, 1], t1(GP, GC), t2(GP, GC))
            for m in (1, 2, 4):
                n = m
                pr_, pi_ = (spread(Pw[r][:, :, m:m + 1], [P, GP, n]) for r in range(2))
                cmul(Pw[0][:, :, m + 1:m + 1 + n], Pw[1][:, :, m + 1:m + 1 + n], Pw[0][:, :, 1:1 + n], Pw[1][:, :, 1:1 + n],
                     pr_, pi_, t1(GP, n), t2(GP, n))
            for r in range(2):
                for j in range(L):
                    ins = v.tensor_copy(Pv[r][:, :, j], Pw[r][:, :, L - 1 - j])
                link(ins)
            cur = (cosp, sinp)
            for a, b in ((7, 8), (9, 10), (7, 8)):
                cmul(sm[a], sm[b], cur[0], cur[1], cur[0], cur[1], sm[11], sm[12])
                cur = (sm[a], sm[b])
            e8 = cur

            dve.wait_ge(S["rel_landed"], 16)
            link(v.tensor_copy(rel_ext[0:NH, 0:P], spread(rel_ext[0:NH, P:P + 1], [NH, P])))
            link(v.tensor_copy(bias_far[0:NH, :], rel_ext[0:NH, 0:1]))
            v.tensor_scalar(rel_ext[0:NH, :], rel_ext[0:NH, :], bias_far[0:NH, :], None, ALU.subtract).then_inc(S["rel_built"], 1)

            def half_matrices(hf):
                s = slice(HP * hf, HP * hf + HP)
                sh = [P, HP, L, GC]
                br_, bi_ = (spread(Bb[r][:, s, :].unsqueeze(2), sh) for r in range(2))
                pr_, pi_ = (spread(Pv[r][:, s, :].unsqueeze(3), sh) for r in range(2))
                if hf:
                    done(dve, ("Y", 3))
                x, y = t1(HP, L, GC), t2(HP, L, GC)
                v.tensor_tensor(x, br_, pr_, ALU.mult)
                tt(y, bi_, pi_, ALU.mult)
                tt(BL[0], x, y, ALU.subtract)
                v.tensor_tensor(x, br_, pi_, ALU.mult)
                tt(y, bi_, pr_, ALU.mult)
                v.tensor_tensor(BL[1], x, y, ALU.add).then_inc(S["b_ready"], 1)
                dve.wait_ge(S["b_ready"], hf + 1)

            def half_outputs(hf):
                s = slice(HP * hf, HP * hf + HP)
                sh = [P, HP, L + 1, GC]
                cr_, ci_ = (spread(bc[:, 2 + r, s, :].unsqueeze(2), sh) for r in range(2))
                pr_, pi_ = (spread(Pw[r][:, s, :].unsqueeze(3), sh) for r in range(2))
                x, y = t1(HP, L + 1, GC), t2(HP, L + 1, GC)
                v.tensor_tensor(x, cr_, pr_, ALU.mult)
                tt(y, ci_, pi_, ALU.mult)
                tt(Wm[0], x, y, ALU.subtract)
                v.tensor_tensor(x, cr_, pi_, ALU.mult)
                tt(y, ci_, pr_, ALU.mult)
                xf, yf, wf = (a.rearrange("p a b c -> p (a b c)") for a in (x, y, Wm[1]))
                v.scalar_tensor_tensor(wf, xf, -1.0, yf, ALU.mult, ALU.subtract).then_inc(S["w_ready"], 1)
                dve.wait_ge(S["w_ready"], hf + 1)

            def phases(hf):
                s = slice(HP * hf, HP * hf + HP)
                x, y = wr, wi
                v.tensor_copy(Tr[:, :, 0], e8[0][:, s])
                link(v.tensor_copy(Ti[:, :, 0], e8[1][:, s]))
                n = 1
                while n < PCH:
                    a_, b_ = (spread(q[:, :, n - 1:n], [P, HP, n]) for q in (Tr, Ti))
                    cmul(Tr[:, :, n:2 * n], Ti[:, :, n:2 * n], Tr[:, :, 0:n], Ti[:, :, 0:n], a_, b_, x[:, :, 0:n], y[:, :, 0:n])
                    n *= 2
                link(v.tensor_copy(rho_t, spread(sm[6][:, s].unsqueeze(2), [P, HP, PCH])))
                link(v.memset(rho_t[:, :, 0], 0.0))

            def kernels(hf):
                for i in range(4):
                    key = ("K", 4 * hf + i)
                    done(dve, key)
                    kp = Kpad[i % 2]
                    if 4 * hf + i >= 2:
                        dve.wait_ge(S[f"kt_landed{i % 2}"], 16 * 8 * (2 * hf + i // 2))
                    ps = bank(key).rearrange("p (a b) -> p a b", a=4)
                    v.tensor_copy(kp[:, :, P:2 * P], ps[0:GC]).then_inc(drained["K"], 1)
                    dve.wait_ge(drained["K"], 4 * hf + i + 1)
                    gs = HP * hf + 4 * (i // 2)
                    dd = d_tmp[0:GC].rearrange("p (a c) -> p a c", c=GC)
                    dg = dskip.rearrange("p (a g) -> p a g", g=2)[:, gs:gs + 4, i % 2]
                    tt(dd, spread(ident[0:GC, 0:GC].unsqueeze(1), [GC, 4, GC]), spread(dg.unsqueeze(2), [GC, 4, GC]), ALU.mult)
                    v.tensor_tensor(kp[:, :, P:P + GC], kp[:, :, P:P + GC], dd, ALU.add).then_inc(S["kpad_ready"], 1)

            def states(hf):
                s = slice(HP * hf, HP * hf + HP)
                dve.wait_ge(drained["V"], 4 * hf + 4)
                vp = [q[:, :, 0:PCH] for q in (Vr, Vi)]
                x, y = wr, wi
                z, zz = y_half[1][:, 0:HP * PCH], y_half[1][:, HP * PCH:2 * HP * PCH]
                z, zz = (q.rearrange("p (a b) -> p a b", a=HP) for q in (z, zz))
                cmul(z, zz, vp[0], vp[1], Tr, Ti, x, y, conj_b=True)
                flat = lambda q: q.rearrange("p a b -> p (a b)")
                v.tensor_tensor_scan(flat(wr), flat(rho_t), flat(z), 0.0, ALU.mult, ALU.add)
                link(v.tensor_tensor_scan(flat(wi), flat(rho_t), flat(zz), 0.0, ALU.mult, ALU.add))
                v.tensor_tensor(z, wr, Tr, ALU.mult)
                tt(zz, wi, Ti, ALU.mult)
                if hf:
                    done(dve, ("Y", 3))
                v.tensor_tensor(Sr[:, :, 1:PCH], z[:, :, 0:PCH - 1], zz[:, :, 0:PCH - 1], ALU.subtract)
                tt(fin[:, 0, s, 0:1], z[:, :, PCH - 1:PCH], zz[:, :, PCH - 1:PCH], ALU.subtract)
                v.tensor_tensor(z, wr, Ti, ALU.mult)
                tt(zz, wi, Tr, ALU.mult)
                v.tensor_tensor(Si[:, :, 1:PCH], z[:, :, 0:PCH - 1], zz[:, :, 0:PCH - 1], ALU.add)
                tt(fin[:, 1, s, 0:1], z[:, :, PCH - 1:PCH], zz[:, :, PCH - 1:PCH], ALU.add)
                v.memset(Sr[:, :, 0:1], 0.0)
                v.memset(Si[:, :, 0:1], 0.0)
                SS = [q[:, :, PCH:NCH].rearrange("p a (b c) -> p a b c", c=2) for q in (Sr, Si)]
                VV = [q[:, :, PCH:NCH].rearrange("p a (b c) -> p a b c", c=2) for q in (Vr, Vi)]
                sh = [P, HP, NB]
                ar_, ai_ = (spread(Pw[r][:, s, L:L + 1], sh) for r in range(2))
                x, y = wr[:, :, 0:NB], wi[:, :, 0:NB]
                zr, zi = z[:, :, 0:NB], zz[:, :, 0:NB]
                v.tensor_copy(SS[0][:, :, :, 0], s0[:, 0, s, :])
                v.tensor_copy(SS[1][:, :, :, 0], s0[:, 1, s, :])
                cmul(zr, zi, s0[:, 0, s, :], s0[:, 1, s, :], ar_, ai_, x, y)
                v.tensor_tensor(SS[0][:, :, :, 1], zr, VV[0][:, :, :, 0], ALU.add)
                tt(SS[1][:, :, :, 1], zi, VV[1][:, :, :, 0], ALU.add)
                cmul(zr, zi, SS[0][:, :, :, 1], SS[1][:, :, :, 1], ar_, ai_, x, y)
                v.tensor_tensor(fin[:, 0, s, 1:NB + 1], zr, VV[0][:, :, :, 1], ALU.add)
                v.tensor_tensor(fin[:, 1, s, 1:NB + 1], zi, VV[1][:, :, :, 1], ALU.add).then_inc(S["state_ready"], 1)
                dve.wait_ge(S["state_ready"], hf + 1)

            def norm_rows(src, dst, ss_ap, f_ap, heads, hd, stats, factor, count, gain, signal):
                sh = [P, heads, hd]
                s3 = src.rearrange("p (h d) -> p h d", h=heads)
                d3 = dst.rearrange("p (h d) -> p h d", h=heads)
                tt(dst, src, src, ALU.mult)
                v.tensor_reduce(ss_ap, d3, AXX, ALU.add).then_inc(stats, 1)
                dve.wait_ge(factor, count)
                fb = spread(f_ap.unsqueeze(2), sh)
                if gain is None:
                    v.tensor_tensor(d3, s3, fb, ALU.mult).then_inc(signal, 1)
                else:
                    tt(d3, s3, fb, ALU.mult)
                    v.tensor_tensor(d3, d3, spread(gain.unsqueeze(1), sh), ALU.mult).then_inc(signal, 1)

            dve.wait_ge(S["consts_built"], 1)
            half_matrices(0)
            dve.wait_ge(S["consts_landed"], 16 * 4)
            for i in range(10):
                dve.wait_ge(drained["qk"], i + 1)
                if i >= 2:
                    done(dve, ("qkT", i - 2))
                if i >= 7:
                    dve.wait_ge(S[f"k_stored{i % 2}"], 16 * ((i - 5) // 2))
                norm_rows(raw[i % 2], nrm[i % 2], qss[:, i % 4, :], qf[:, i % 4, :], NH, HD, S["qk_stats"], S["qk_factor"],
                          i + 1, kg if i >= 5 else None, S["qk_normed"])
            dve.wait_ge(S["mem_squared"], 2)
            link(v.memset(Kpad[0][:, :, 0:P], 0.0))
            link(v.memset(Kpad[1][:, :, 0:P], 0.0))
            half_outputs(0)
            phases(0)
            dve.wait_ge(S["memT_landed"], 16)
            for k in range(KT):
                ins = v.tensor_scalar(memT[:, k, :], memT[:, k, :], mem_in_norm[:, k:k + 1], None, ALU.mult)
            ins.then_inc(S["memT_ready"], 1)
            dve.wait_ge(S["bias_landed"], 16 * NH)
            link(v.memset(bias_new, NEG))
            v.tensor_copy(bias_new[:, 112:128], bias_s[:, 128:144]).then_inc(S["bias_built"], 1)
            kernels(0)
            states(0)
            phases(1)
            half_matrices(1)
            half_outputs(1)
            kernels(1)
            states(1)
            dve.wait_ge(S["state_ready"], 2)
            for hf in range(2):
                dve.wait_ge(S["gelu_sq"], hf + 1)
                link(v.tensor_scalar(gelu_sq[hf], gelu_sq[hf], 0.044715, 1.0, ALU.mult, ALU.add))
                v.tensor_tensor(gelu_sq[hf], gelu_sq[hf], y_half[hf], ALU.mult).then_inc(S["gelu_arg"], 1)
                dve.wait_ge(S["gelu_th"], hf + 1)
                v.scalar_tensor_tensor(y_half[hf], gelu_sq[hf], 1.0, y_half[hf], ALU.add, ALU.mult).then_inc(S["gelu_ready"], 1)
            done(dve, ("Y", 7))
            for i in range(2):
                dve.wait_ge(S[f"kt_landed{i}"], 16 * 32)
            link(v.memset(qblk, 0.0))
            for a in range(NPAIR):
                for h2 in range(2):
                    lo = HD * h2
                    c0 = (2 * a + h2) * SQ
                    ins = v.tensor_copy(qblk[lo:lo + HD, :, a, c0:c0 + SQ],
                                        qT[lo:lo + HD, a, TP:T].rearrange("p (b s) -> p b s", s=SQ))
            ins.then_inc(S["qblk_ready"], 1)
            dve.wait_ge(S["bias_p_landed"], 16)
            link(v.memset(bias_p[0:CH, :, P + CH:2 * P], NEG))
            for c in range(4):
                dve.wait_ge(drained["gg"], c + 1)
                done(dve, ("gv", c))
                v.scalar_tensor_tensor(ysT[:, c, 0:TP], glu_t[c % 2], 1.0, bank(("gv", c)), ALU.add, ALU.mult).then_inc(drained["gv"], 1)

            def soft_in(i, parts, signal, scaled=0):
                for j, (key, n, b, c0) in enumerate(parts):
                    done(dve, key)
                    ps = bank(key)
                    if b is not None:
                        w = b.shape[-1]
                        link(v.tensor_tensor(ps[:, c0:c0 + w], ps[:, c0:c0 + w], b, ALU.add))
                    if scaled and j == 0:
                        dve.wait_ge(S["p_scaled"], scaled)
                    link(v.tensor_reduce(smax[:, i % 4, j:j + 1], ps[:, 0:n], AXX, ALU.max))
                src = smax[:, i % 4, 0:1]
                if len(parts) == 2:
                    tt(smax[:, i % 4, 0:1], smax[:, i % 4, 0:1], smax[:, i % 4, 1:2], ALU.max)
                v.tensor_scalar(smax[:, i % 4, 2:3], src, -1.0, None, ALU.mult).then_inc(signal, 1)

            def soft_out(i, kinds, two, signal):
                for kind, c in kinds:
                    dve.wait_ge(drained[kind], c)
                src = ssum[:, i % 4, 0:1]
                if two:
                    tt(src, src, ssum[:, i % 4, 1:2], ALU.add)
                v.reciprocal(ssum[:, i % 4, 3:4], src).then_inc(signal, 1)

            n = len(PROMPT_UNITS)

            def attn_in(i):
                if i < n:
                    t, h = PROMPT_UNITS[i]
                    b = bias_p[:, h, :] if t else bias_p[:, h, P:2 * P]
                    soft_in(i, [(("S", i), P * (t + 1), b, P * max(t - 1, 0))], S["row_max"], max(i - 3, 0))
                else:
                    b = i - n
                    soft_in(i, [(("sA", b), 512, bias_s[:, 0:P], 384),
                                (("sB", b), P, bias_new[:, 112 - SQ * b:240 - SQ * b], 0)], S["row_max"], i - 3)

            def attn_out(i):
                if i < n:
                    soft_out(i, [("S", i + 1)], False, S["p_normed"])
                else:
                    soft_out(i, [("sA", i - n + 1), ("sB", i - n + 1)], True, S["p_normed"])

            def pv_out(m):
                t, h = PROMPT_UNITS[2 * m]
                done(dve, ("PV", m))
                v.tensor_copy(yaT[:, h // 2, t * P:(t + 1) * P], bank(("PV", m))[:, 0:P]).then_inc(drained["PV"], 1)

            def spv_out(b):
                done(dve, ("sO", b))
                ps = bank(("sO", b))[:, 0:P].rearrange("p (a s) -> p a s", s=SQ)
                for h2 in range(2):
                    lo = HD * h2
                    ins = v.tensor_copy(yaT[lo:lo + HD, :, TP + SQ * b:TP + SQ * b + SQ], ps[lo:lo + HD, h2:8:2, :])
                ins.then_inc(drained["sO"], 1)

            attn_in(0)
            attn_in(1)
            attn_out(0)
            for c in range(4):
                dve.wait_ge(S["glu_th"], c + 1)
                v.scalar_tensor_tensor(ysT[:, c, TP:T], glu_t[c % 2][:, 0:P], 1.0, bank(("gs", c))[:, P:2 * P],
                                       ALU.add, ALU.mult).then_inc(drained["gs"], 1)
            for i in range(2, n):
                if PROMPT_UNITS[i][0] >= 1:
                    attn_out(i - 1)
                    attn_in(i)
                else:
                    attn_in(i)
                    attn_out(i - 1)
                if i >= 5 and i % 2:
                    pv_out((i - 5) // 2)
            attn_out(n - 1)
            pv_out(n // 2 - 2)
            pv_out(n // 2 - 1)
            link(v.tensor_scalar(out_ssm, out_ssm, 0.25, None, ALU.mult))

            def branch_squares(y, cols, n_sums):
                if n_sums:
                    dve.wait_ge(S["sq_ready"], n_sums)
                tt(branch_sq[:, :, cols], y[:, :, cols], y[:, :, cols], ALU.mult)

            def branch_sums(br, cols):
                v.tensor_reduce(branch_sum[br][:, cols], branch_sq[:, :, cols].rearrange("p k t -> p t k"), AXX, ALU.add
                                ).then_inc(S["sq_ready"], 1)

            def branch_scale(y, gain, cols):
                w = cols.stop - cols.start
                v.tensor_tensor(y[:, :, cols], y[:, :, cols], spread(gain.unsqueeze(2), [P, 4, w]), ALU.mult
                                ).then_inc(S["branch_scaled"], 1)

            for b in range(NB):
                if b >= 1:
                    attn_out(n + b - 1)
                attn_in(n + b)
                if b >= 3:
                    spv_out(b - 3)
                if b == 0:
                    dve.wait_ge(drained["gv"], 4)
                    dve.wait_ge(drained["gs"], 4)
                    branch_squares(ysT, slice(0, T), 0)
                if b == 1:
                    branch_sums(0, slice(0, T))
                if b == 2:
                    branch_scale(ysT, out_ssm, slice(0, T))
                if b == 3:
                    dve.wait_ge(drained["PV"], len(PROMPT_UNITS) // 2)
                    branch_squares(yaT, slice(0, TP), 1)
                if b == 4:
                    branch_sums(1, slice(0, TP))
                if b == 5:
                    branch_scale(yaT, out_att, slice(0, TP))
            attn_out(n + NB - 1)
            for b in range(NB - 3, NB):
                spv_out(b)

            dve.wait_ge(drained["sO"], NB)
            branch_squares(yaT, slice(TP, T), 2)
            branch_sums(1, slice(TP, T))
            branch_scale(yaT, out_att, slice(TP, T))
            done(dve, ("ss", 0))
            ps = bank(("ss", 0))
            link(v.tensor_scalar(ssg[:, 0:NT], ps[:, 0:NT], 1.0 / 16, None, ALU.mult))
            v.tensor_copy(ssg[:, NT:2 * NT], ps[:, NT:2 * NT]).then_inc(drained["ss"], 1)
            dve.wait_ge(S["rstd_g_ready"], 1)
            dve.wait_ge(S["x_landed"], 32)

            def turn_out(kind, i, gain):
                t, hh = i // 2, i % 2
                done(dve, (kind, i))
                v.tensor_tensor(hT[:, 4 * hh:4 * hh + 4, t * P:(t + 1) * P], bank((kind, i)).rearrange("p (a b) -> p a b", a=4),
                                spread(gain[:, 4 * hh:4 * hh + 4].unsqueeze(2), [P, 4, P]), ALU.mult).then_inc(drained[kind], 1)

            def norm_mem_keys():
                dve.wait_ge(S["mem_landed"], 48)
                for t in range(2):
                    tt(at(R + 20480, D), mk_rows[:, t, :], mk_rows[:, t, :], ALU.mult)
                    ins = v.tensor_reduce(qss8[:, 4 * t:4 * t + 4], at(R + 20480, MH, MD), AXX, ALU.add)
                    if t == 0:
                        link(ins)
                ins.then_inc(S["mk_stats"], 1)
                dve.wait_ge(S["mk_factor"], 1)
                for i in range(4):
                    seg = mk_rows[:, i // 2, (i % 2) * 512:(i % 2 + 1) * 512].rearrange("p (h d) -> p h d", h=2)
                    f = qf8[:, 4 * (i // 2) + 2 * (i % 2):4 * (i // 2) + 2 * (i % 2) + 2]
                    tt(seg, seg, spread(f.unsqueeze(2), [P, 2, MD]), ALU.mult)
                    v.tensor_tensor(seg, seg, spread(mkg.unsqueeze(1), [P, 2, MD]), ALU.mult).then_inc(S["mk_normed"], 1)

            for t in range(NT):
                if t == 2:
                    norm_mem_keys()
                for c in range(2):
                    i = 2 * t + c
                    x = xr[:, t, c * 512:(c + 1) * 512]
                    done(dve, ("oS", i))
                    v.scalar_tensor_tensor(x, bank(("oS", i)), rstd_g[:, t:t + 1], x, ALU.mult, ALU.add).then_inc(drained["oS"], 1)
                    dve.wait_ge(drained["oS"], i + 1)
                    done(dve, ("oA", i))
                    v.scalar_tensor_tensor(x, bank(("oA", i)), rstd_g[:, NT + t:NT + t + 1], x, ALU.mult, ALU.add).then_inc(drained["oA"], 1)
                if t >= 1:
                    turn_out("x1T", 2 * t - 2, norm_mem)
                    turn_out("x1T", 2 * t - 1, norm_mem)
            turn_out("x1T", 8, norm_mem)
            turn_out("x1T", 9, norm_mem)
            done(dve, ("oA", 9))
            link(v.memset(qblk2, 0.0))
            link(v.tensor_scalar(mq_gain4[:, 0:2], mq_gain, float(MD) ** -0.5, None, ALU.mult))
            link(v.tensor_scalar(mq_gain4[:, 2:4], mq_gain, float(MD) ** -0.5, None, ALU.mult))

            def mqT_out(j):
                done(dve, ("mqT", j))
                v.tensor_tensor(qm[:, 4 * (j % 2):4 * (j % 2) + 4, (j // 2) * P:(j // 2 + 1) * P],
                                bank(("mqT", j)).rearrange("p (a b) -> p a b", a=4),
                                spread(mq_gain4.unsqueeze(2), [P, 4, P]), ALU.mult).then_inc(drained["mqT"], 1)

            n = len(MEM_UNITS)

            def mem_out(i):
                soft_out(i, [("mS", i + 1)], False, S["p_normed"])

            def mpv_out(j):
                t, h = MEM_UNITS[j]
                done(dve, ("mPV", j))
                v.tensor_copy(oT[:, 2 * h:2 * h + 2, t * P:(t + 1) * P],
                              bank(("mPV", j)).rearrange("p (a b) -> p a b", a=4)[:, 0:2, :]).then_inc(drained["mPV"], 1)

            def smt_out(i):
                for c in range(2):
                    done(dve, ("smT", 2 * i + c))
                    ps = bank(("smT", 2 * i + c)).rearrange("p (a b h s) -> p a b h s", a=4, b=2, s=SQ)
                    for q in range(2):
                        dst = oT[:, 4 * c + 2 * q:4 * c + 2 * q + 2, TP + 2 * SQ * i:TP + 2 * SQ * (i + 1)]
                        ins = v.tensor_copy(dst.rearrange("p a (b s) -> p a b s", s=SQ), ps[:, 2 * q:2 * q + 2, :, 2 * c + q, :])
                    ins.then_inc(drained["smT"], 1)

            def mem_in(i):
                if i >= 4:
                    dve.wait_ge(S["p_scaled"], BAND_UNITS + i - 3)
                soft_in(i, [(("mS", i), NM, None, 0)], S["row_max"])

            for i in range(10):
                dve.wait_ge(drained["mq"], i + 1)
                if i >= 2:
                    done(dve, ("mqT", i - 2))
                norm_rows(mraw[i % 2], mnrm[i % 2], qss[:, i % 4, 0:2], qf[:, i % 4, 0:2], 2, MD, S["qk_stats"], S["qk_factor"],
                          10 + i + 1, None, S["mq_normed"])
                if i >= 2:
                    mqT_out(i - 2)
            mem_in(0)
            mem_out(0)
            mem_in(1)
            mqT_out(8)
            mqT_out(9)
            dve.wait_ge(drained["mqT"], 10)
            for h in range(MH):
                for k in range(2):
                    ins = v.tensor_copy(qblk2[:, :, 2 * h + k, h * SQ:(h + 1) * SQ],
                                        qm[:, 2 * h + k, TP:T].rearrange("p (b s) -> p b s", s=SQ))
            ins.then_inc(S["qblk2_ready"], 1)
            for i in range(2, n):
                mem_out(i - 1)
                mem_in(i)
                if i >= 3:
                    mpv_out(i - 3)
            mem_out(n - 1)
            for j in range(n - 3, n):
                mpv_out(j)
            for i in range(7):
                if 1 <= i < 5:
                    mem_out(n + i - 1)
                if i < 4:
                    mem_in(n + i)
                if i >= 3:
                    smt_out(i - 3)

            def behind(t):
                if 0 <= t - 1 < NT:
                    turn_out("x2T", 2 * t - 2, norm_ffn)
                    turn_out("x2T", 2 * t - 1, norm_ffn)
                if 0 <= t - 2 < NT:
                    done(dve, ("rt", t - 2))
                    if t >= 4:
                        done(dve, ("rtT", t - 4))
                    v.tensor_copy(logit_t[t % 2][0:NG + NE, :], bank(("rt", t - 2))[0:NG + NE, 0:P]).then_inc(drained["rt"], 1)
                if t >= 3:
                    j = t - 3
                    done(dve, ("rtT", j))
                    dve.wait_ge(S["rstd_2_ready"], j + 1)
                    v.scalar_tensor_tensor(logit[:, j, :], bank(("rtT", j))[:, 0:NG + NE], rstd_2[:, j:j + 1], rb,
                                           ALU.mult, ALU.add).then_inc(drained["rtT"], 1)

            done(dve, ("smT", NB - 1))
            link(v.memset(chosen[:, NT, :], 0.0))
            link(v.memset(before[:, 0, :], 0.0))
            link(v.tensor_scalar(block_starts, iota_slot[:, 1:NBLK], float(CAP), None, ALU.mult))
            for t in range(NT):
                for c in range(2):
                    i = 2 * t + c
                    x = xr[:, t, c * 512:(c + 1) * 512]
                    done(dve, ("mo", i))
                    v.tensor_tensor(x, bank(("mo", i)), x, ALU.add).then_inc(drained["mo"], 1)
                behind(t)
            for t in range(NT, NT + 3):
                behind(t)

            dve.wait_ge(drained["rtT"], NT)
            lg, le = logit[:, :, 0:NG], logit[:, :, NG:NG + NE]
            i1, i2, v2 = idx[:, 0], idx[:, 1], ta[:, 0]
            sg, se = [P, NT, NG], [P, NT, NE]
            link(v.tensor_reduce(gmax, lg, AXX, ALU.max))
            v.tensor_tensor(gsm[1], lg, spread(gmax.unsqueeze(2), sg), ALU.subtract).then_inc(S["logits_ready"], 1)

            def first(mask, idx, iota, n, shape, onehot, scratch):
                link(v.scalar_tensor_tensor(scratch, mask, -64.0, spread(iota.unsqueeze(1), shape), ALU.mult, ALU.add))
                link(v.tensor_reduce(idx, scratch, AXX, ALU.min))
                link(v.tensor_scalar(idx, idx, 64.0, None, ALU.add))
                tt(onehot, spread(iota.unsqueeze(1), shape), spread(idx.unsqueeze(2), shape), ALU.is_equal)

            tt(gsm[0], lg, spread(gmax.unsqueeze(2), sg), ALU.is_equal)
            first(gsm[0], gidx, iota4, NG, sg, gsm[0], gsm[2])
            link(v.tensor_scalar(gsm[2], gsm[0], -NEG, NEG, ALU.mult, ALU.add))
            s4 = [P, NT, NG, EPG]
            l4, le4 = lsel.rearrange("p t (g e) -> p t g e", g=NG), logit[:, :, NG:NG + NE].rearrange("p t (g e) -> p t g e", g=NG)
            tt(l4, le4, spread(gsm[0].unsqueeze(3), s4), ALU.mult)
            tt(l4, l4, spread(gsm[2].unsqueeze(3), s4), ALU.add)
            link(v.tensor_reduce(v1, lsel, AXX, ALU.max))
            tt(oh1, lsel, spread(v1.unsqueeze(2), se), ALU.is_equal)
            first(oh1, i1, iota32, NE, se, oh1, rtmp[:, 0])
            link(v.scalar_tensor_tensor(lsel, oh1, 3 * NEG, lsel, ALU.mult, ALU.add))
            link(v.tensor_reduce(v2, lsel, AXX, ALU.max))
            tt(oh2, lsel, spread(v2.unsqueeze(2), se), ALU.is_equal)
            first(oh2, i2, iota32, NE, se, oh2, rtmp[:, 0])
            v.tensor_tensor(dv, v2, v1, ALU.subtract).then_inc(S["logits_ready"], 1)
            tt(chosen[:, 0:NT], oh1, oh2, ALU.add)
            link(v.tensor_copy(before[:, 1, :], chosen[:, 0, :]))
            for t in range(2, NT):
                tt(before[:, t, :], before[:, t - 1, :], chosen[:, t - 1, :], ALU.add)
            v.tensor_tensor(before[:, NT, :], before[:, NT - 1, :], chosen[:, NT - 1, :], ALU.add).then_inc(S["choice_ready"], 1)
            done(dve, ("rank", 0))
            v.tensor_copy(rank_sb.rearrange("p a b -> p (a b)"), bank(("rank", 0))[:, 0:(NT + 1) * NE]).then_inc(drained["rank"], 1)
            dve.wait_ge(drained["rank"], 1)
            total = rank_sb[:, NT, :]
            tt(past, spread(total.unsqueeze(2), [P, NE, NBLK - 1]), spread(block_starts.unsqueeze(1), [P, NE, NBLK - 1]), ALU.is_gt)
            link(v.tensor_reduce(extra, past, AXX, ALU.add))
            link(v.tensor_tensor_scan(incl, ones[:, 0:NE], extra, 0.0, ALU.mult, ALU.add))
            tt(ovb, incl, extra, ALU.subtract)
            sr = [P, 2, NT, NE]
            tt(rtmp, oh, spread(rank_sb[:, 0:NT, :].unsqueeze(1), sr), ALU.mult)
            link(v.tensor_reduce(ta, rtmp, AXX, ALU.add))
            tt(rtmp.rearrange("p a b c -> p (a b) c"), oh.rearrange("p a b c -> p (a b) c"),
               spread(ovb.unsqueeze(1), [P, 2 * NT, NE]), ALU.mult)
            link(v.tensor_reduce(tb, rtmp, AXX, ALU.add))
            past2 = past[:, 0:2 * NT, :]
            tt(past2, spread(ta.rearrange("p a b -> p (a b)").unsqueeze(2), [P, 2 * NT, NBLK - 1]),
               spread(block_starts.unsqueeze(1), [P, 2 * NT, NBLK - 1]), ALU.is_ge)
            link(v.tensor_reduce(blk.rearrange("p a b -> p (a b)"), past2, AXX, ALU.add))
            link(v.scalar_tensor_tensor(ta, blk, -float(CAP), ta, ALU.mult, ALU.add))
            link(v.scalar_tensor_tensor(tb, blk, float(NE - 1), tb, ALU.add, ALU.add))
            tt(unit_of, idx, tb, ALU.subtract)
            link(v.scalar_tensor_tensor(unit_of, blk, 0.0, unit_of, ALU.is_equal, ALU.mult))
            tt(unit_of, unit_of, tb, ALU.add)
            done(dve, ("mo", 9))
            n2 = 2 * NT
            flat2 = lambda a: a.rearrange("p a b -> p (a b)")
            unit3, slot3 = (spread(flat2(a).unsqueeze(2), [P, n2, n]) for a, n in ((unit_of, NU), (ta, CAP)))
            ut3, sh3 = (a.rearrange("p a b c -> p (a b) c") for a in (unit_tok, slot_hot))
            tt(ut3, spread(iota_slot[:, 0:NU].unsqueeze(1), [P, n2, NU]), unit3, ALU.is_equal)
            link(v.tensor_tensor(sh3, spread(iota_slot[:, 0:CAP].unsqueeze(1), [P, n2, CAP]), slot3, ALU.is_equal))
            for j in range(2):
                ins = v.tensor_tensor(unit_tok[:, j], unit_tok[:, j], spread(tokid.unsqueeze(2), [P, NT, NU]), ALU.mult)
            ins.then_inc(S["table_parts_ready"], 1)
            dve.wait_ge(S["choice_exp"], 2)
            link(v.tensor_reduce(p1, gsm[1], AXX, ALU.add))
            link(v.scalar_tensor_tensor(p1, dv, 1.0, p1, ALU.add, ALU.mult))
            link(v.reciprocal(w12[:, 0, :], p1))
            tt(w12[:, 1, :], w12[:, 0, :], dv, ALU.mult)
            link(v.scalar_tensor_tensor(slot_f, unit_of, float(CAP), ta, ALU.mult, ALU.add))
            done(dve, ("tab", 0))
            v.tensor_copy(tok_idx[0:CAP, :], bank(("tab", 0))[0:CAP, 0:NU]).then_inc(drained["tab"], 1)
            link(v.tensor_copy(ovt[:, :, :], spread(incl.unsqueeze(1), [P, NOV, NE])))
            tt(ovt, ovt, spread(iota_slot[:, 0:NOV].unsqueeze(2), [P, NOV, NE]), ALU.is_le)
            link(v.tensor_reduce(ovf[:, 0:NOV], ovt, AXX, ALU.add))
            link(v.tensor_scalar(ovf[:, 0:NOV], ovf[:, 0:NOV], float(NE - 1), None, ALU.min))
            link(v.tensor_copy(ovf[:, NOV:NOV + 1], incl[:, NE - 1:NE]))
            link(v.tensor_copy(ov_regs[:, :], ovf))
            v.tensor_copy(slot_idx[:, :], slot_f.rearrange("p a b -> p (a b)")).then_inc(S["slots_ready"], 1)

            def xg_out(src, dst, xi):
                return v.tensor_tensor(dst[:, 4 * xi:4 * xi + 4, 0:CAP], src.rearrange("p (a b) -> p a b", a=4)[:, :, 0:CAP],
                                       spread(norm_ffn[:, 4 * xi:4 * xi + 4].unsqueeze(2), [P, 4, CAP]), ALU.mult)

            def gated(ps, th, hb, a_done):
                b4 = ps.rearrange("p (a b) -> p a b", a=4)
                v.scalar_tensor_tensor(a_b[:, :, 0:CAP], th[:, :, 0:CAP], 1.0, b4[:, 0:2, 0:CAP], ALU.add, ALU.mult).then_inc(moe_a, 1)
                dve.wait_ge(moe_a, a_done)
                return v.scalar_tensor_tensor(hb[:, :, 0:CAP], a_b[:, :, 0:CAP], 0.5, b4[:, 2:4, 0:CAP], ALU.mult, ALU.mult)

            def XT(i, c):
                e = 4 * i + c
                if late(i, c, 2):
                    dve.wait_ge(moe["gu_done"], e - 1)
                for xi in range(2):
                    dve.wait_ge(moe["tx_done"], 2 * e + xi + 1)
                    xg_out(banks[:, 2 * (c % 2) + xi, :], xgT[c % 2], xi).then_inc(moe["xgT_ready"], 1)

            def H(i, c):
                e = 4 * i + c
                dve.wait_ge(moe["th_ready"], e + 1)
                if late(i, c, 2):
                    dve.wait_ge(moe["dn_done"], 2 * e - 2)
                if late(i, c, 1):
                    dve.wait_ge(moe["h_ready"], e)
                gated(banks[:, 4 + c % 2, :], th_b[c % 2], h_b[c % 2], e + 1).then_inc(moe["h_ready"], 1)

            XT(0, 0)
            XT(0, 1)
            H(0, 0)
            for c in range(1, 5):
                XT(0, c + 1)
                H(0, c)
            with dve.Fori(1, 7) as i:
                for c in range(1, 5):
                    XT(i, c + 1)
                    H(i, c)
            for c in range(29, 32):
                if c < 31:
                    XT(0, c + 1)
                H(0, c)
            nov = dve.value_load(ov_regs[0:1, NOV:NOV + 1], min_val=0, max_val=NOV)
            dve.wait_ge(moe["dn_done"], 2 * NE)
            with dve.Fori(0, NOV) as vv:
                with dve.If(vv < nov):
                    dve.wait_ge(moe["tx_done"], 2 * NE + 2 * vv + 2)
                    xg_out(banks[:, 0, :], xgT[0], 0).then_inc(moe["xgT_ready"], 1)
                    xg_out(banks[:, 1, :], xgT[0], 1).then_inc(moe["xgT_ready"], 1)
                    dve.wait_ge(moe["th_ready"], NE + vv + 1)
                    dve.wait_ge(moe["h_ready"], NE + vv)
                    gated(banks[:, 4, :], th_b[0], h_b[0], vv + NE + 1).then_inc(moe["h_ready"], 1)
            for t in range(NT):
                dve.wait_ge(moe[f"yg_landed{t}"], 32)
                a, b = yg[2 * t], yg[2 * t + 1]
                link(v.scalar_tensor_tensor(xr[:, t, :], a, w12[:, 0, t:t + 1], xr[:, t, :], ALU.mult, ALU.add))
                v.scalar_tensor_tensor(xr[:, t, :], b, w12[:, 1, t:t + 1], xr[:, t, :], ALU.mult, ALU.add).then_inc(moe["y_ready"], 1)


_INS = ["x_t", "x_rows", "mem_t", "mem_rows", "dense_w", "exp_gu", "exp_dn", "ck_t", "cv", "cmk_t", "cmv", "cols", "k_gain",
        "mk_gain", "router_w", "router_b", "ssm_small", "ssm_bc", "ssm_d", "ssm_s0", "rel_rev"]
_OUTS = [("y", (T, D)), ("k", (T, AW)), ("v", (T, AW)), ("mk", (NM, D)), ("mv", (NM, D)), ("s", (P, 2, GP, NB + 1))]


def kernel(**inputs):
    import concourse.bacc as bacc
    from concourse.bass_utils import run_bass_kernel_spmd

    w = {k: np.asarray(a) for k, a in inputs.items()}

    def tiles(a, n):
        return a.reshape(-1, P, n).transpose(1, 0, 2)

    def col(a):
        return a.reshape(-1, P).T

    x = np.concatenate([w["x_prompt"].reshape(TP, D), w["x_sample"].reshape(TS, D)])
    mem = w["mem_prompt"].reshape(NM, D)
    w_in = w["w_in"][0]
    halves = lambda a: [tiles(a[:, i * 512:(i + 1) * 512], 512) for i in range(a.shape[1] // 512)]
    units = (halves(w_in) + halves(w["w_mem_k"][0]) + halves(w["w_mem_v"][0]) + halves(w["w_out"][0])
             + halves(w["w_mem_q"][0]) + halves(w["w_mem_o"][0]))
    units.insert(4, tiles(w["w_glu"][0], 1024))
    q_gain = w["att_q_gain"].reshape(HD, 1)
    state = lambda a: a.reshape(GP, 2, GS, -1).transpose(1, 2, 0, 3).reshape(P, GP, -1)
    pair = lambda a: state(a.reshape(G, GS, -1))
    c_t = lambda a: a[0].transpose(0, 2, 1)
    gu = np.concatenate([w["exp_w_gate"][0], w["exp_w_up"][0]], axis=2)
    router = np.concatenate([w["router_g_w"][0], w["router_e_w"][0].transpose(1, 0, 2).reshape(D, NE)], axis=1)
    step = np.broadcast_to(w["ssm_log_step"].reshape(G, 1), (G, GS))
    arrays = {
        "x_t": tiles(x.T, T),
        "x_rows": x,
        "mem_t": tiles(mem.T, NM),
        "mem_rows": mem,
        "dense_w": np.stack([u.reshape(P, 4096) for u in units]),
        "exp_gu": gu.reshape(NE, KT, P, 2 * FF).transpose(0, 2, 1, 3),
        "exp_dn": w["exp_w_down"][0].reshape(NE, 2, P, D).transpose(0, 2, 1, 3),
        "ck_t": w["cache_attn_k"][0].reshape(NB, 512, NPAIR, P).transpose(0, 3, 2, 1),
        "cv": w["cache_attn_v"][0].reshape(NB, 512, AW),
        "cmk_t": w["cache_mem_k"][0].reshape(NB, NM, 8, P).transpose(0, 3, 2, 1),
        "cmv": w["cache_mem_v"][0].reshape(NB, NM, D),
        "cols": np.concatenate([col(w[k]) for k in ("norm_mix", "norm_mem", "mem_in_norm", "norm_ffn", "out_norm_ssm",
                                                    "out_norm_att")]
                               + [np.concatenate([q_gain, q_gain]), col(w["mem_q_gain"])], axis=1),
        "k_gain": w["att_k_gain"].reshape(HD),
        "mk_gain": w["mem_k_gain"].reshape(MD),
        "router_w": tiles(router, NG + NE),
        "router_b": np.concatenate([w["router_g_b"].reshape(-1), w["router_e_b"].reshape(-1)]),
        "ssm_small": np.stack([pair(a)[:, :, 0] for a in (w["ssm_lambda_re"], w["ssm_lambda_im"], step)], axis=1),
        "ssm_bc": np.stack([pair(w["ssm_b_re"][0]), pair(w["ssm_b_im"][0]), pair(c_t(w["ssm_c_re"])), pair(c_t(w["ssm_c_im"]))], axis=1),
        "ssm_d": w["ssm_d"].reshape(G, GC).T,
        "ssm_s0": np.stack([pair(a[0].transpose(1, 2, 0)) for a in (w["state_ssm_re"], w["state_ssm_im"])], axis=1),
        "rel_rev": w["att_rel_bias"][0][:, ::-1],
    }
    nc = bacc.Bacc("TRN2", target_bir_lowering=False, num_devices=1)
    sent, ins, outs = {}, {}, {}
    for name in _INS:
        a = np.ascontiguousarray(arrays[name])
        sent[f"in_{name}"] = a
        ins[name] = nc.dram_tensor(f"in_{name}", a.shape, mybir.dt.from_np(a.dtype), kind="ExternalInput").ap()
    for name, shape in _OUTS:
        outs[f"{name}_out"] = nc.dram_tensor(f"out_{name}", shape, F32, kind="ExternalOutput").ap()
    program(nc, **ins, **outs)
    got = run_bass_kernel_spmd(nc, [sent], core_ids=[0]).results[0]
    y, k, v, mk, mv, s = (np.asarray(got[f"out_{name}"]) for name, _ in _OUTS)
    s = s.reshape(2, GS, 2, GP, NB + 1).transpose(2, 4, 3, 0, 1).reshape(2, NB + 1, G, GS)
    heads = lambda a, *lead: a.reshape(*lead, NH, HD)
    return (y[:TP].reshape(1, TP, D), y[TP:].reshape(NB, SQ, D),
            heads(k[:TP], 1, 1, TP), heads(v[:TP], 1, 1, TP), s[0, 0:1][None], s[1, 0:1][None],
            mk.reshape(1, 1, NM, MH, MD), mv.reshape(1, 1, NM, MH, MD),
            heads(k[TP:], 1, NB, SQ), heads(v[TP:], 1, NB, SQ), s[0, 1:][None], s[1, 1:][None])
```
